# Optimizing a Trainium2 kernel written in Bass

```python
import math
import jax, jax.numpy as jnp
from jax import lax
import numpy as np

D_MODEL = 1024
BATCH = 1
SEQ = 256
DEPTH = 2

N_MIXERS = 2
N_MAMBA = (DEPTH + 1) // 2
N_MOBA = DEPTH // 2

SSM_EXPAND = 2
SSM_D_INNER = SSM_EXPAND * D_MODEL
SSM_HEAD_DIM = 64
SSM_HEADS = SSM_D_INNER // SSM_HEAD_DIM
SSM_GROUPS = 8
SSM_HEADS_PER_GROUP = SSM_HEADS // SSM_GROUPS
SSM_STATE = 128
SSM_CONV = 4
SSM_CHUNK = 256
SSM_CONV_DIM = SSM_D_INNER + 2 * SSM_GROUPS * SSM_STATE
SSM_IN_DIM = SSM_D_INNER + SSM_CONV_DIM + SSM_HEADS

ATTN_HEAD_DIM = 64
ATTN_HEADS = D_MODEL // ATTN_HEAD_DIM
MOBA_BLOCK = 256
MOBA_TOPK = 3
MOBA_Q_CHUNK = 16
ALIBI_MAX_BIAS = 8.0

D_FF = 2816
RMS_EPS = 1e-6


def rmsnorm(x, g):
    xf = x.astype(jnp.float32)
    y = xf * lax.rsqrt(jnp.mean(xf * xf, axis=-1, keepdims=True) + RMS_EPS)
    return (y * g.astype(jnp.float32)).astype(x.dtype)

def modulate(x, g, c_act, w, b):
    m = c_act @ w + b
    shift, scale, gate = jnp.split(m, 3, axis=-1)
    h = rmsnorm(x, g) * (1.0 + scale[:, None, :]) + shift[:, None, :]
    return h, gate[:, None, :]

def swiglu(h, w_gate, w_up, w_down):
    return (jax.nn.silu(h @ w_gate) * (h @ w_up)) @ w_down

def ssd_chunked_scan(x, dt, a, bm, cm):
    bsz, L = x.shape[0], x.shape[1]
    n_chunks = -(-L // SSM_CHUNK)
    pad = n_chunks * SSM_CHUNK - L

    def to_chunks(t):
        t = jnp.pad(t.astype(jnp.float32), [(0, 0), (0, pad)] + [(0, 0)] * (t.ndim - 2))
        t = t.reshape((bsz, n_chunks, SSM_CHUNK) + t.shape[2:])
        return jnp.moveaxis(t, 1, 0)

    xc, dtc, bc, cc = to_chunks(x), to_chunks(dt), to_chunks(bm), to_chunks(cm)
    causal = jnp.tril(jnp.ones((SSM_CHUNK, SSM_CHUNK), dtype=bool))[None, :, :, None, None]

    def step(state, inp):
        x_k, dt_k, b_k, c_k = inp
        acum = jnp.cumsum(dt_k * a, axis=1)
        seg = acum[:, :, None] - acum[:, None, :]
        decay = jnp.exp(jnp.where(causal, seg, -jnp.inf))
        cb = jnp.einsum('btgn,bsgn->btsg', c_k, b_k)
        w = cb[..., None] * decay * dt_k[:, None]
        y_intra = jnp.einsum('btsgr,bsgrp->btgrp', w, x_k)
        y_inter = jnp.einsum('btgn,bgrpn->btgrp', c_k, state) * jnp.exp(acum)[..., None]
        to_end = jnp.exp(acum[:, -1:] - acum) * dt_k
        new_state = (state * jnp.exp(acum[:, -1])[..., None, None]
                     + jnp.einsum('bsgn,bsgr,bsgrp->bgrpn', b_k, to_end, x_k))
        return new_state, y_intra + y_inter

    state0 = jnp.zeros((bsz, SSM_GROUPS, SSM_HEADS_PER_GROUP, SSM_HEAD_DIM, SSM_STATE), jnp.float32)
    _, y = lax.scan(step, state0, (xc, dtc, bc, cc))
    y = jnp.moveaxis(y, 0, 1).reshape((bsz, n_chunks * SSM_CHUNK) + y.shape[3:])[:, :L]
    return y.astype(x.dtype)

def mamba2_mixer(h, w_in, conv_w, conv_b, dt_bias, a_log, d_skip, norm_w, w_out):
    bsz, L, _ = h.shape
    G, R, P, N = SSM_GROUPS, SSM_HEADS_PER_GROUP, SSM_HEAD_DIM, SSM_STATE
    proj = h @ w_in
    z, xbc, dt = jnp.split(proj, [SSM_D_INNER, SSM_D_INNER + SSM_CONV_DIM], axis=-1)
    xbc = lax.conv_general_dilated(
        xbc, conv_w, window_strides=(1,), padding=[(SSM_CONV - 1, 0)],
        dimension_numbers=('NWC', 'WIO', 'NWC'), feature_group_count=SSM_CONV_DIM) + conv_b
    xbc = jax.nn.silu(xbc)
    xs, bm, cm = jnp.split(xbc, [SSM_D_INNER, SSM_D_INNER + G * N], axis=-1)
    dt = jax.nn.softplus(dt.astype(jnp.float32) + dt_bias.astype(jnp.float32))
    a = -jnp.exp(a_log.astype(jnp.float32))
    xs = xs.reshape(bsz, L, G, R, P)
    y = ssd_chunked_scan(xs, dt.reshape(bsz, L, G, R), a.reshape(G, R),
                         bm.reshape(bsz, L, G, N), cm.reshape(bsz, L, G, N))
    y = y + d_skip.reshape(G, R)[..., None] * xs
    y = y.reshape(bsz, L, SSM_D_INNER)
    y = rmsnorm(y * jax.nn.silu(z), norm_w)
    return y @ w_out

def moba_mixer(h, w_qkv, w_out):
    bsz, L, _ = h.shape
    H, dh, BLK, QC = ATTN_HEADS, ATTN_HEAD_DIM, MOBA_BLOCK, MOBA_Q_CHUNK
    qkv = (h @ w_qkv).reshape(bsz, L, 3, H, dh)
    q = jnp.transpose(qkv[:, :, 0], (0, 2, 1, 3))
    k = jnp.transpose(qkv[:, :, 1], (0, 2, 1, 3))
    v = jnp.transpose(qkv[:, :, 2], (0, 2, 1, 3))
    n_blocks = -(-L // BLK)
    K = max(1, min(MOBA_TOPK, n_blocks))
    pad = n_blocks * BLK - L
    k = jnp.pad(k, [(0, 0), (0, 0), (0, pad), (0, 0)])
    v = jnp.pad(v, [(0, 0), (0, 0), (0, pad), (0, 0)])
    kb = k.reshape(bsz, H, n_blocks, BLK, dh)
    vb = v.reshape(bsz, H, n_blocks, BLK, dh)
    kmean = jnp.mean(kb.astype(jnp.float32), axis=3)
    scale = dh ** -0.5
    slopes = jnp.exp2(-ALIBI_MAX_BIAS * (jnp.arange(H, dtype=jnp.float32) + 1.0) / H)
    bi = jnp.arange(bsz)[:, None, None, None]
    hi = jnp.arange(H)[None, :, None, None]
    blk_ids = jnp.arange(n_blocks)
    in_blk = jnp.arange(BLK)

    def chunk(ci):
        q0 = ci * QC
        own = q0 // BLK
        qc = lax.dynamic_slice_in_dim(q, q0, QC, axis=2)
        qpos = q0 + jnp.arange(QC)
        gate = jnp.einsum('bhqd,bhnd->bhqn', qc.astype(jnp.float32), kmean)
        gate = jnp.where((blk_ids < own)[None, None, None, :], gate, -jnp.inf)
        _, sel = lax.top_k(gate, K)
        sel_valid = jnp.arange(K) < own
        k_sel = kb[bi, hi, sel]
        v_sel = vb[bi, hi, sel]
        kpos_sel = sel[..., None] * BLK + in_blk
        dist_sel = (qpos[:, None, None] - kpos_sel).astype(jnp.float32)
        s_sel = (jnp.einsum('bhqd,bhqkjd->bhqkj', qc, k_sel).astype(jnp.float32) * scale
                 - slopes[:, None, None, None] * dist_sel)
        s_sel = jnp.where(sel_valid[:, None], s_sel, -jnp.inf)
        k_own = lax.dynamic_slice_in_dim(k, own * BLK, BLK, axis=2)
        v_own = lax.dynamic_slice_in_dim(v, own * BLK, BLK, axis=2)
        kpos_own = own * BLK + in_blk
        dist_own = (qpos[:, None] - kpos_own[None, :]).astype(jnp.float32)
        s_own = (jnp.einsum('bhqd,bhjd->bhqj', qc, k_own).astype(jnp.float32) * scale
                 - slopes[:, None, None] * dist_own)
        s_own = jnp.where(dist_own >= 0.0, s_own, -jnp.inf)
        s = jnp.concatenate([s_own, s_sel.reshape(bsz, H, QC, K * BLK)], axis=-1)
        p = jax.nn.softmax(s, axis=-1).astype(v.dtype)
        p_own = p[..., :BLK]
        p_sel = p[..., BLK:].reshape(bsz, H, QC, K, BLK)
        return (jnp.einsum('bhqj,bhjd->bhqd', p_own, v_own)
                + jnp.einsum('bhqkj,bhqkjd->bhqd', p_sel, v_sel))

    out = lax.map(chunk, jnp.arange(L // QC))
    out = jnp.transpose(out, (1, 0, 3, 2, 4)).reshape(bsz, L, H * dh)
    return out @ w_out

def first_inputs(seed: int = 0) -> dict:
    key = jax.random.key(seed)
    ks = jax.random.split(key, 24)
    f32 = jnp.float32

    def nrm(k, shape, s):
        return jax.random.normal(k, shape, f32) * s

    x = nrm(ks[0], (BATCH, SEQ, D_MODEL), 1.0)
    c = nrm(ks[1], (BATCH, D_MODEL), 1.0)
    norm_g = 1.0 + nrm(ks[2], (DEPTH, 3, D_MODEL), 0.05)
    mod_w = nrm(ks[3], (DEPTH, 3, D_MODEL, 3 * D_MODEL), 0.5 * D_MODEL ** -0.5)
    mod_b = nrm(ks[4], (DEPTH, 3, 3 * D_MODEL), 0.02)
    ffn_w_gate = nrm(ks[5], (DEPTH, 2, D_MODEL, D_FF), D_MODEL ** -0.5)
    ffn_w_up = nrm(ks[6], (DEPTH, 2, D_MODEL, D_FF), D_MODEL ** -0.5)
    ffn_w_down = nrm(ks[7], (DEPTH, 2, D_FF, D_MODEL), D_FF ** -0.5)
    ssm_w_in = nrm(ks[8], (N_MAMBA, D_MODEL, SSM_IN_DIM), D_MODEL ** -0.5)
    ssm_conv_w = nrm(ks[9], (N_MAMBA, SSM_CONV, 1, SSM_CONV_DIM), SSM_CONV ** -0.5)
    ssm_conv_b = nrm(ks[10], (N_MAMBA, SSM_CONV_DIM), 0.02)
    dt0 = jnp.exp(jax.random.uniform(ks[11], (N_MAMBA, SSM_HEADS), f32,
                                     math.log(1e-3), math.log(1e-1)))
    ssm_dt_bias = dt0 + jnp.log(-jnp.expm1(-dt0))
    ssm_a_log = jnp.log(jax.random.uniform(ks[12], (N_MAMBA, SSM_HEADS), f32, 1.0, 16.0))
    ssm_d = 1.0 + nrm(ks[13], (N_MAMBA, SSM_HEADS), 0.05)
    ssm_norm_w = 1.0 + nrm(ks[14], (N_MAMBA, SSM_D_INNER), 0.05)
    ssm_w_out = nrm(ks[15], (N_MAMBA, SSM_D_INNER, D_MODEL), SSM_D_INNER ** -0.5)
    attn_w_qkv = nrm(ks[16], (N_MOBA, D_MODEL, 3 * D_MODEL), D_MODEL ** -0.5)
    attn_w_out = nrm(ks[17], (N_MOBA, D_MODEL, D_MODEL), D_MODEL ** -0.5)
    final_norm_g = 1.0 + nrm(ks[18], (D_MODEL,), 0.05)
    return {"x": x, "c": c, "norm_g": norm_g, "mod_w": mod_w, "mod_b": mod_b,
            "ffn_w_gate": ffn_w_gate, "ffn_w_up": ffn_w_up, "ffn_w_down": ffn_w_down,
            "ssm_w_in": ssm_w_in, "ssm_conv_w": ssm_conv_w, "ssm_conv_b": ssm_conv_b,
            "ssm_dt_bias": ssm_dt_bias, "ssm_a_log": ssm_a_log, "ssm_d": ssm_d,
            "ssm_norm_w": ssm_norm_w, "ssm_w_out": ssm_w_out,
            "attn_w_qkv": attn_w_qkv, "attn_w_out": attn_w_out,
            "final_norm_g": final_norm_g}

def first_block(x, c, norm_g, mod_w, mod_b, ffn_w_gate, ffn_w_up, ffn_w_down,
              ssm_w_in, ssm_conv_w, ssm_conv_b, ssm_dt_bias, ssm_a_log, ssm_d,
              ssm_norm_w, ssm_w_out, attn_w_qkv, attn_w_out, final_norm_g):
    c_act = jax.nn.silu(c)
    for i in range(DEPTH):
        h, g = modulate(x, norm_g[i, 0], c_act, mod_w[i, 0], mod_b[i, 0])
        x = x + 0.5 * g * swiglu(h, ffn_w_gate[i, 0], ffn_w_up[i, 0], ffn_w_down[i, 0])
        h, g = modulate(x, norm_g[i, 1], c_act, mod_w[i, 1], mod_b[i, 1])
        j = i // N_MIXERS
        if i % N_MIXERS == 0:
            y = mamba2_mixer(h, ssm_w_in[j], ssm_conv_w[j], ssm_conv_b[j], ssm_dt_bias[j],
                             ssm_a_log[j], ssm_d[j], ssm_norm_w[j], ssm_w_out[j])
        else:
            y = moba_mixer(h, attn_w_qkv[j], attn_w_out[j])
        x = x + g * y
        h, g = modulate(x, norm_g[i, 2], c_act, mod_w[i, 2], mod_b[i, 2])
        x = x + 0.5 * g * swiglu(h, ffn_w_gate[i, 1], ffn_w_up[i, 1], ffn_w_down[i, 1])
    return rmsnorm(x, final_norm_g)


N_CONV_LAYERS = (DEPTH + N_MIXERS - 1) // N_MIXERS
N_NSA_LAYERS = DEPTH // N_MIXERS
CONV_WIDTH = 31
N_HEADS = 16
HEAD_DIM = 64
N_KV = 4
GROUP = N_HEADS // N_KV
ROT_DIM = HEAD_DIM // 4
ROPE_THETA = 500000.0
CMP_LEN = 32
CMP_STRIDE = 16
CMP_HIDDEN = 256
SEL_LEN = 64
SEL_TOPK = 16
WINDOW = 512
Q_BLOCK = 128
FFN_CONV_WIDTH = 3
EPS = 1e-6
PROJ_SIZES = (N_HEADS * HEAD_DIM,) + (N_KV * HEAD_DIM,) * 6 + (3 * N_HEADS,)
PROJ_COLS = sum(PROJ_SIZES)


def rmsnorm_2(x, g):
    xf = x.astype(jnp.float32)
    y = xf * lax.rsqrt(jnp.mean(xf * xf, axis=-1, keepdims=True) + EPS)
    return (y * g.astype(jnp.float32)).astype(x.dtype)

def layernorm(x, g, b):
    xf = x.astype(jnp.float32)
    mu = jnp.mean(xf, axis=-1, keepdims=True)
    var = jnp.mean(jnp.square(xf - mu), axis=-1, keepdims=True)
    y = (xf - mu) * lax.rsqrt(var + EPS)
    return (y * g.astype(jnp.float32) + b.astype(jnp.float32)).astype(x.dtype)

def causal_dwconv(x, w, b):
    width, ch = w.shape
    y = lax.conv_general_dilated(
        x, w[:, None, :].astype(x.dtype), window_strides=(1,),
        padding=[(width - 1, 0)], dimension_numbers=("NWC", "WIO", "NWC"),
        feature_group_count=ch)
    return y + b.astype(x.dtype)

def partial_rope(x):
    seq = x.shape[1]
    half = ROT_DIM // 2
    inv_freq = ROPE_THETA ** (-jnp.arange(half, dtype=jnp.float32) * (2.0 / ROT_DIM))
    ang = jnp.arange(seq, dtype=jnp.float32)[:, None] * inv_freq[None, :]
    cos = jnp.cos(ang)[:, None, :]
    sin = jnp.sin(ang)[:, None, :]
    xf = x.astype(jnp.float32)
    x1 = xf[..., :half]
    x2 = xf[..., half:ROT_DIM]
    out = jnp.concatenate([x1 * cos - x2 * sin, x2 * cos + x1 * sin, xf[..., ROT_DIM:]], axis=-1)
    return out.astype(x.dtype)

def masked_softmax(s, mask):
    s = jnp.where(mask, s.astype(jnp.float32), -1e30)
    m = jnp.max(s, axis=-1, keepdims=True)
    e = jnp.where(mask, jnp.exp(s - m), 0.0)
    return e / jnp.maximum(jnp.sum(e, axis=-1, keepdims=True), 1e-30)

def cmp_to_sel_matrix(n_cmp, n_sel):
    start_c = np.arange(n_cmp)[:, None] * CMP_STRIDE
    start_s = np.arange(n_sel)[None, :] * SEL_LEN
    ov = np.minimum(start_c + CMP_LEN, start_s + SEL_LEN) - np.maximum(start_c, start_s)
    return jnp.asarray(np.maximum(ov, 0).astype(np.float32) / CMP_LEN)

def conformer_conv(h, w_pw1, b_pw1, w_dw, b_dw, ln_g, ln_b, w_pw2, b_pw2):
    u = h @ w_pw1 + b_pw1
    a, gate = jnp.split(u, 2, axis=-1)
    u = a * jax.nn.sigmoid(gate)
    u = causal_dwconv(u, w_dw, b_dw)
    u = jax.nn.silu(layernorm(u, ln_g, ln_b))
    return u @ w_pw2 + b_pw2

def compress(blocks, pe, w1, w2):
    b, g, n, l, d = blocks.shape
    z = (blocks + pe).reshape(b, g, n, l * d)
    return jax.nn.silu(z @ w1) @ w2

def nsa_attention(h, w_in, q_g, kc_g, ks_g, kw_g, pe_k, pe_v, ck_w1, ck_w2, cv_w1, cv_w2, w_out):
    bsz, seq, _ = h.shape
    n_cmp = (seq - CMP_LEN) // CMP_STRIDE + 1
    n_sel = seq // SEL_LEN
    k_top = min(SEL_TOPK, n_sel)
    n_qb = seq // Q_BLOCK
    scale = HEAD_DIM ** -0.5

    splits = [int(c) for c in np.cumsum(PROJ_SIZES)[:-1]]
    q, kc, vc, ks, vs, kw, vw, gl = jnp.split(h @ w_in, splits, axis=-1)
    heads = lambda t, n: t.reshape(bsz, seq, n, HEAD_DIM)
    to_groups = lambda t: t.reshape(bsz, seq, N_KV, GROUP, HEAD_DIM).transpose(0, 2, 3, 1, 4)
    q = rmsnorm_2(heads(q, N_HEADS), q_g)
    q_nope = to_groups(q)
    q_rope = to_groups(partial_rope(q))
    gates = jax.nn.sigmoid(gl.astype(jnp.float32)).astype(h.dtype)
    gates = gates.reshape(bsz, seq, N_KV, GROUP, 3).transpose(0, 2, 3, 1, 4)

    blk_idx = np.arange(n_cmp)[:, None] * CMP_STRIDE + np.arange(CMP_LEN)[None, :]
    kc_blk = heads(kc, N_KV)[:, blk_idx].transpose(0, 3, 1, 2, 4)
    vc_blk = heads(vc, N_KV)[:, blk_idx].transpose(0, 3, 1, 2, 4)
    k_cmp = rmsnorm_2(compress(kc_blk, pe_k, ck_w1, ck_w2), kc_g)
    v_cmp = compress(vc_blk, pe_v, cv_w1, cv_w2)
    cmp_end = jnp.asarray(np.arange(n_cmp) * CMP_STRIDE + CMP_LEN - 1)
    cmp_map = cmp_to_sel_matrix(n_cmp, n_sel)

    k_sel = partial_rope(rmsnorm_2(heads(ks, N_KV), ks_g)).transpose(0, 2, 1, 3)
    k_sel = k_sel.reshape(bsz, N_KV, n_sel, SEL_LEN, HEAD_DIM)
    v_sel = heads(vs, N_KV).transpose(0, 2, 1, 3).reshape(bsz, N_KV, n_sel, SEL_LEN, HEAD_DIM)

    pad = ((0, 0), (0, 0), (WINDOW, 0), (0, 0))
    k_win = jnp.pad(partial_rope(rmsnorm_2(heads(kw, N_KV), kw_g)).transpose(0, 2, 1, 3), pad)
    v_win = jnp.pad(heads(vw, N_KV).transpose(0, 2, 1, 3), pad)

    b_ix = jnp.arange(bsz)[:, None, None, None]
    g_ix = jnp.arange(N_KV)[None, :, None, None]
    sel_off = jnp.arange(SEL_LEN)
    win_off = jnp.arange(Q_BLOCK + WINDOW)
    sel_ids = jnp.arange(n_sel)

    def query_block(qb):
        t0 = qb * Q_BLOCK
        pos = t0 + jnp.arange(Q_BLOCK)
        qn = lax.dynamic_slice_in_dim(q_nope, t0, Q_BLOCK, axis=3)
        qr = lax.dynamic_slice_in_dim(q_rope, t0, Q_BLOCK, axis=3)
        gt = lax.dynamic_slice_in_dim(gates, t0, Q_BLOCK, axis=3)

        s_c = jnp.einsum("bgrtd,bgnd->bgrtn", qn, k_cmp) * scale
        p_c = masked_softmax(s_c, cmp_end[None, :] <= pos[:, None])
        o_c = jnp.einsum("bgrtn,bgnd->bgrtd", p_c.astype(v_cmp.dtype), v_cmp)

        cur = pos // SEL_LEN
        imp = jnp.einsum("bgrtn,nj->bgtj", p_c, cmp_map)
        forced = (sel_ids[None, :] == 0) | (sel_ids[None, :] == cur[:, None]) | (sel_ids[None, :] == cur[:, None] - 1)
        imp = jnp.where(sel_ids[None, :] > cur[:, None], -1.0, jnp.where(forced, 1e4, imp))
        _, idx = lax.top_k(imp, k_top)
        k_g = k_sel[b_ix, g_ix, idx]
        v_g = v_sel[b_ix, g_ix, idx]
        s_s = jnp.einsum("bgrtd,bgtkld->bgrtkl", qr, k_g) * scale
        key_pos = idx[..., None] * SEL_LEN + sel_off
        mask_s = (key_pos <= pos[:, None, None]).reshape(bsz, N_KV, 1, Q_BLOCK, k_top * SEL_LEN)
        p_s = masked_softmax(s_s.reshape(bsz, N_KV, GROUP, Q_BLOCK, k_top * SEL_LEN), mask_s)
        o_s = jnp.einsum("bgrtm,bgtmd->bgrtd", p_s.astype(v_g.dtype),
                         v_g.reshape(bsz, N_KV, Q_BLOCK, k_top * SEL_LEN, HEAD_DIM))

        kwb = lax.dynamic_slice_in_dim(k_win, t0, Q_BLOCK + WINDOW, axis=2)
        vwb = lax.dynamic_slice_in_dim(v_win, t0, Q_BLOCK + WINDOW, axis=2)
        kp = t0 - WINDOW + win_off
        mask_w = (kp[None, :] >= 0) & (kp[None, :] <= pos[:, None]) & (kp[None, :] > pos[:, None] - WINDOW)
        s_w = jnp.einsum("bgrtd,bgsd->bgrts", qr, kwb) * scale
        p_w = masked_softmax(s_w, mask_w)
        o_w = jnp.einsum("bgrts,bgsd->bgrtd", p_w.astype(vwb.dtype), vwb)

        return gt[..., 0:1] * o_c + gt[..., 1:2] * o_s + gt[..., 2:3] * o_w

    o = lax.map(query_block, jnp.arange(n_qb))
    o = o.transpose(1, 0, 4, 2, 3, 5).reshape(bsz, seq, N_HEADS * HEAD_DIM)
    return o @ w_out

def conv_ffn(h, w_up, w_dw, b_dw, w_down):
    a, v = jnp.split(h @ w_up, 2, axis=-1)
    return (jax.nn.silu(causal_dwconv(a, w_dw, b_dw)) * v) @ w_down

def second_inputs(seed: int = 0) -> dict:
    key = jax.random.key(seed)
    ks = iter(jax.random.split(key, 40))
    f32 = jnp.float32
    D = D_MODEL
    hd = HEAD_DIM
    Lc = N_CONV_LAYERS
    Ln = N_NSA_LAYERS

    def w(shape, fan_in):
        return jax.random.normal(next(ks), shape, f32) * fan_in ** -0.5

    def gain(shape):
        return 1.0 + 0.05 * jax.random.normal(next(ks), shape, f32)

    def small(shape, s=0.02):
        return s * jax.random.normal(next(ks), shape, f32)

    return {
        "x": jax.random.normal(next(ks), (BATCH, SEQ, D), f32),
        "mix_norm_g": gain((DEPTH, D)),
        "ffn_norm_g": gain((DEPTH, D)),
        "conv_w_pw1": w((Lc, D, 2 * D), D),
        "conv_b_pw1": small((Lc, 2 * D)),
        "conv_w_dw": w((Lc, CONV_WIDTH, D), CONV_WIDTH),
        "conv_b_dw": small((Lc, D)),
        "conv_ln_g": gain((Lc, D)),
        "conv_ln_b": small((Lc, D)),
        "conv_w_pw2": w((Lc, D, D), D),
        "conv_b_pw2": small((Lc, D)),
        "nsa_w_in": w((Ln, D, PROJ_COLS), D),
        "nsa_q_norm": gain((Ln, hd)),
        "nsa_kc_norm": gain((Ln, hd)),
        "nsa_ks_norm": gain((Ln, hd)),
        "nsa_kw_norm": gain((Ln, hd)),
        "nsa_pe_k": small((Ln, CMP_LEN, hd), 0.1),
        "nsa_pe_v": small((Ln, CMP_LEN, hd), 0.1),
        "nsa_ck_w1": w((Ln, CMP_LEN * hd, CMP_HIDDEN), CMP_LEN * hd),
        "nsa_ck_w2": w((Ln, CMP_HIDDEN, hd), CMP_HIDDEN),
        "nsa_cv_w1": w((Ln, CMP_LEN * hd, CMP_HIDDEN), CMP_LEN * hd),
        "nsa_cv_w2": w((Ln, CMP_HIDDEN, hd), CMP_HIDDEN),
        "nsa_w_out": w((Ln, N_HEADS * hd, D), N_HEADS * hd),
        "ffn_w_up": w((DEPTH, D, 2 * D_FF), D),
        "ffn_w_dw": w((DEPTH, FFN_CONV_WIDTH, D_FF), FFN_CONV_WIDTH),
        "ffn_b_dw": small((DEPTH, D_FF)),
        "ffn_w_down": w((DEPTH, D_FF, D), D_FF),
    }

def second_block(x, mix_norm_g, ffn_norm_g,
              conv_w_pw1, conv_b_pw1, conv_w_dw, conv_b_dw, conv_ln_g, conv_ln_b, conv_w_pw2, conv_b_pw2,
              nsa_w_in, nsa_q_norm, nsa_kc_norm, nsa_ks_norm, nsa_kw_norm, nsa_pe_k, nsa_pe_v,
              nsa_ck_w1, nsa_ck_w2, nsa_cv_w1, nsa_cv_w2, nsa_w_out,
              ffn_w_up, ffn_w_dw, ffn_b_dw, ffn_w_down):
    for i in range(DEPTH):
        h = rmsnorm_2(x, mix_norm_g[i])
        j = i // N_MIXERS
        if i % N_MIXERS == 0:
            x = x + conformer_conv(h, conv_w_pw1[j], conv_b_pw1[j], conv_w_dw[j], conv_b_dw[j],
                                   conv_ln_g[j], conv_ln_b[j], conv_w_pw2[j], conv_b_pw2[j])
        else:
            x = x + nsa_attention(h, nsa_w_in[j], nsa_q_norm[j], nsa_kc_norm[j], nsa_ks_norm[j], nsa_kw_norm[j],
                                  nsa_pe_k[j], nsa_pe_v[j], nsa_ck_w1[j], nsa_ck_w2[j], nsa_cv_w1[j], nsa_cv_w2[j],
                                  nsa_w_out[j])
        x = x + conv_ffn(rmsnorm_2(x, ffn_norm_g[i]), ffn_w_up[i], ffn_w_dw[i], ffn_b_dw[i], ffn_w_down[i])
    return x


def setup_inputs(seed=0):
    out = dict(first_inputs(seed))
    for name, value in second_inputs(seed + 1).items():
        if name != "x":
            out[name + "_2"] = value
    return out


def reference(
    x, c, norm_g, mod_w, mod_b, ffn_w_gate, ffn_w_up, ffn_w_down, ssm_w_in, ssm_conv_w,
    ssm_conv_b, ssm_dt_bias, ssm_a_log, ssm_d, ssm_norm_w, ssm_w_out, attn_w_qkv, attn_w_out,
    final_norm_g, mix_norm_g_2, ffn_norm_g_2, conv_w_pw1_2, conv_b_pw1_2, conv_w_dw_2,
    conv_b_dw_2, conv_ln_g_2, conv_ln_b_2, conv_w_pw2_2, conv_b_pw2_2, nsa_w_in_2, nsa_q_norm_2,
    nsa_kc_norm_2, nsa_ks_norm_2, nsa_kw_norm_2, nsa_pe_k_2, nsa_pe_v_2, nsa_ck_w1_2,
    nsa_ck_w2_2, nsa_cv_w1_2, nsa_cv_w2_2, nsa_w_out_2, ffn_w_up_2, ffn_w_dw_2, ffn_b_dw_2,
    ffn_w_down_2,
):
    x = first_block(
        x, c, norm_g, mod_w, mod_b, ffn_w_gate, ffn_w_up, ffn_w_down, ssm_w_in, ssm_conv_w,
        ssm_conv_b, ssm_dt_bias, ssm_a_log, ssm_d, ssm_norm_w, ssm_w_out, attn_w_qkv,
        attn_w_out, final_norm_g,
    )
    return second_block(
        x, mix_norm_g_2, ffn_norm_g_2, conv_w_pw1_2, conv_b_pw1_2, conv_w_dw_2, conv_b_dw_2,
        conv_ln_g_2, conv_ln_b_2, conv_w_pw2_2, conv_b_pw2_2, nsa_w_in_2, nsa_q_norm_2,
        nsa_kc_norm_2, nsa_ks_norm_2, nsa_kw_norm_2, nsa_pe_k_2, nsa_pe_v_2, nsa_ck_w1_2,
        nsa_ck_w2_2, nsa_cv_w1_2, nsa_cv_w2_2, nsa_w_out_2, ffn_w_up_2, ffn_w_dw_2, ffn_b_dw_2,
        ffn_w_down_2,
    )


_drawn_inputs = setup_inputs


def setup_inputs(seed=0):
    import zlib

    import numpy as np

    out = dict(_drawn_inputs(seed))
    spreads = {}
    factors = {'ssm_conv_b': 6.036,
     'ssm_d': 4.882,
     'ssm_norm_w': 2.967,
     'conv_b_pw1_2': 3.838,
     'conv_ln_b_2': 4.021,
     'nsa_q_norm_2': 8.0,
     'nsa_kc_norm_2': 8.0,
     'nsa_ks_norm_2': 8.0,
     'nsa_kw_norm_2': 8.0,
     'nsa_pe_k_2': 8.0,
     'ffn_b_dw_2': 4.318}
    for name, (base, spread) in spreads.items():
        noise = np.random.default_rng([zlib.crc32(name.encode()), seed]).standard_normal(out[name].shape)
        drawn = base * np.exp(spread * noise) if base else spread * noise
        out[name] = __import__('jax').numpy.asarray(drawn.astype(out[name].dtype))
    for name, factor in factors.items():
        out[name] = (out[name] * factor).astype(out[name].dtype)
    return out
```

```python
from contextlib import ExitStack

import numpy as np
import concourse.bass as bass
from concourse import mybir

F32 = mybir.dt.float32
BF16 = mybir.dt.bfloat16
ALU = mybir.AluOpType
ACT = mybir.ActivationFunctionType
AX_X = mybir.AxisListType.X

P = 128
L = 256
D = 1024
KD = D // P
FF = 2816
NF = FF // P
PAIRS = NF // 2
INNER = 2048
KI = INNER // P
SH = 32
GRP = 8
HPG = SH // GRP
AH = 16
HD = 64
NB = 3
NCMP = 15
EPS = 1e-6
TRI = L + P
SLOT = 2048
RING = 6
MRING = 3
MSLOTS = 12
NMOD = 6
FSLOTS = 3 * PAIRS

LAYERS = [("ffn0", FSLOTS), ("ssm", 24 + 8), ("ffn1", FSLOTS), ("ffn2", FSLOTS), ("moba", 12 + 4),
          ("ffn3", FSLOTS), ("conf", 8 + 4), ("cffn0", FSLOTS), ("nsa", 10 + 4 + 4), ("cffn1", FSLOTS)]
AT_SLOT = {}
SLOTS = 0
for _name, _n in LAYERS:
    AT_SLOT[_name] = SLOTS
    SLOTS += _n
assert SLOTS % RING == 0

VEC = {}
NVEC = 0
for _name, _n in [("c", KD), ("norm_g", 6 * KD), ("mod_b", 6 * 24), ("conv_w", 4 * 32), ("conv_b", 32),
                  ("dt_bias", 1), ("a_log", 1), ("ssm_d", KI), ("ssm_norm", KI), ("final_g", KD),
                  ("mix_g", 2 * KD), ("ffn_g", 2 * KD), ("b_pw1", 16), ("w_dw", 31 * KD), ("b_dw", KD),
                  ("ln_g", KD), ("ln_b", KD), ("b_pw2", KD), ("q_norm", 1), ("kc_norm", 1), ("ks_norm", 1),
                  ("kw_norm", 1), ("pe_k", 16), ("pe_v", 16), ("ffn_dw", 2 * 3 * NF), ("ffn_db", 2 * NF)]:
    VEC[_name] = NVEC
    NVEC += _n

SMALL = {"w_dt": 0, "w_gl": KD * SH, "ck2": KD * SH + KD * 48, "cv2": KD * SH + KD * 48 + 2 * HD}
NSMALL = KD * SH + KD * 48 + 4 * HD

CON = {}
NCON = 0
for _name, _n in [("ident", P), ("block", P), ("tri", TRI), ("mask_sq", TRI), ("mask_qk", TRI), ("dist", TRI),
                  ("cmp_add", 2 * 32), ("cmp_one", 2 * 32), ("cos", L), ("sin", L), ("rope", P),
                  ("pick0", P), ("pick1", P)]:
    CON[_name] = NCON
    NCON += _n


def constants():
    con = np.zeros((P, NCON), np.float32)

    def put(name, a):
        con[:a.shape[0], CON[name]:CON[name] + a.shape[1]] = a

    i = np.arange(P)
    t = np.arange(L)
    put("ident", np.eye(P))
    put("block", (i[:, None] // HD == i[None, :] // HD).astype(np.float32))
    tri = [(s0 + i[:, None] <= t[None, :]).astype(np.float32) for s0 in (0, P)]
    put("tri", np.concatenate([tri[0], tri[1][:, P:]], 1))
    sq = np.concatenate([1 - tri[0], (1 - tri[1])[:, P:]], 1) * np.float32(-1e30)
    put("mask_sq", sq)
    ok = np.concatenate([i[:, None] >= i[None, :], P + i[:, None] >= t[None, :]], 1)
    put("mask_qk", np.where(ok, 0.0, -1e30))
    dist = np.concatenate([i[None, :] - i[:, None], t[None, :] - (P + i[:, None])], 1)
    put("dist", np.where(ok, dist, -1e30))
    end = np.arange(32) * 16 + 31
    seen = np.concatenate([(end[None, :] <= q0 + i[:, None]) & (np.arange(32) < NCMP)[None, :] for q0 in (0, P)], 1)
    put("cmp_add", np.where(seen, 0.0, -1e30))
    put("cmp_one", seen.astype(np.float32))
    inv = (np.float32(500000.0) ** (-np.arange(8, dtype=np.float32) * np.float32(2.0 / 16))).astype(np.float32)
    ang = (t.astype(np.float32)[None, :] * inv[:, None]).astype(np.float32).astype(np.float64)
    cos, sin, rope = np.ones((P, L)), np.zeros((P, L)), np.zeros((P, P))
    for h in (0, HD):
        for half in (0, 8):
            cos[h + half:h + half + 8] = np.cos(ang)
            sin[h + half:h + half + 8] = np.sin(ang)
        for j in range(8):
            rope[h + 8 + j, h + j] = -1.0
            rope[h + j, h + 8 + j] = 1.0
    put("cos", cos)
    put("sin", sin)
    put("rope", rope)
    for par in (0, 1):
        put(f"pick{par}", (i[:, None] == par * HD + i[None, :] % HD).astype(np.float32))
    return con


class Chain:

    def __init__(self, eng, sem):
        self.eng, self.sem, self.n, self.off = eng, sem, 0, 0

    def link(self, ins):
        ins.then_inc(self.sem, 1)
        self.n += 1
        self.eng.wait_ge(self.sem, self.n + self.off)


def build(nc, x_in, vec_in, small_in, con_in, mod_in, w_in, out):
    with ExitStack() as ctx:
        def sb(name, shape, dt=F32):
            return ctx.enter_context(nc.sbuf_tensor(name, shape, dt))

        def sem(name):
            return ctx.enter_context(nc.semaphore(name))

        ring = sb("ring", [P, RING, SLOT])
        mring = sb("mring", [P, MRING, 2, D])
        modacc = sb("modacc", [P, 2, 3 * D])
        modprod = sb("modprod", [P, D])
        vec = sb("vec", [P, NVEC])
        small = sb("small", [P, NSMALL])
        con = sb("con", [P, NCON])
        ones = sb("ones", [P, P])
        eps = sb("eps", [P, 1])
        zeros = sb("zeros", [P, 512], BF16)
        X = sb("X", [P, KD, L])
        H = sb("H", [P, KD, L])
        rstd = sb("rstd", [P, 2 * L])
        modv = sb("modv", [P, 24])
        modsc = sb("modsc", [P, KD])
        gate = sb("gate", [P, KD])
        cact = sb("cact", [P, KD])
        ARENA = 17900
        arena = sb("arena", [P, ARENA])

        def part(at, *shape):
            n = int(np.prod(shape))
            assert at + n <= ARENA
            v = arena[:, at:at + n]
            if len(shape) == 2:
                return v.rearrange("p (a b) -> p a b", a=shape[0])
            if len(shape) == 3:
                return v.rearrange("p (a b c) -> p a b c", a=shape[0], b=shape[1])
            return v

        act_buf = part(0, 2, L)
        hid_buf = part(2 * L, 4, L)
        Z = part(0, KI, L)
        XBC = part(KI * L, 2 * KI, L)
        XT = part(3 * KI * L, 2, INNER)
        at = 4 * KI * L
        Wd = part(at, 2, TRI)
        dtT = part(at + 2 * TRI, 4, SH)
        acT = part(at + 2 * TRI + 4 * SH, 2, SH)
        dts = part(at + 2 * TRI + 6 * SH, 2, L)
        negA = modv[0:SH, 0:1]
        Q = part(0, KD, L)
        K = part(2048, KD, L)
        QR = part(2048, KD, L)
        V = part(4096, 2, D)
        O = part(6144, KD, L)
        Pb = part(8192, 3, TRI)
        PT = part(9344, 2, TRI)
        nmax = part(10112, 3, 2)
        psum_ = part(10118, 3, 2)
        KS = part(10130, 2, L)
        KW = part(10642, 2, L)
        KC = part(11154, 2, L)
        VC = part(11666, 2, L)
        gates = part(12178, 2, 48)
        zk = part(12274, 16, 60)
        hidc = part(13234, 2, 60)
        hidr = part(13354, 2, 512)
        kcmp = part(14378, 30)
        vcmp = part(14408, 4, HD)
        pc = part(14664, 2, 512)
        PC = part(15688, 4, L)
        st32 = part(16712, 2, 32)
        sqb = part(16776, 512)
        UP = part(0, KD, 30 + L)
        CV = part(2304, KD, L)
        sgb = part(4352, 2, L)

        acc = ctx.enter_context(nc.psum_tensor("acc", [P, 4, 512], F32))
        up = ctx.enter_context(nc.psum_tensor("up", [P, 2, 512], F32))
        stat = ctx.enter_context(nc.psum_tensor("stat", [P, 512], F32))
        misc = ctx.enter_context(nc.psum_tensor("misc", [P, 512], F32))

        def acc_t(m):
            return acc[:, m // 2, (m % 2) * L:(m % 2 + 1) * L]

        def v1(name, col=0, n=1):
            return vec[:, VEC[name] + col:VEC[name] + col + n]

        def cs(name, a, b):
            return con[:, CON[name] + a:CON[name] + b]

        ident = cs("ident", 0, P)

        vec_landed, con_landed, small_landed, x_landed = (sem(s) for s in (
            "vec_landed", "con_landed", "small_landed", "x_landed"))
        slot_landed = [sem(f"slot_landed{i}") for i in range(RING)]
        mod_landed = [sem(f"mod_landed{i}") for i in range(MRING)]
        slot_done = sem("slot_done")
        mod_used = sem("mod_used")
        mod_reduced = sem("mod_reduced")
        modvec_ready = sem("modvec_ready")
        setup_done = sem("setup_done")
        cact_ready = sem("cact_ready")
        x_ready = sem("x_ready")
        down_ready = sem("down_ready")
        sq_ready = sem("sq_ready")
        stat_ready = sem("stat_ready")
        root_ready = sem("root_ready")
        xn_ready = sem("xn_ready")
        h_ready = sem("h_ready")
        pair_free = sem("pair_free")
        silu_ready = sem("silu_ready")
        dwc_ready = sem("dwc_ready")
        misc_ready = sem("misc_ready")
        xt_ready = sem("xt_ready")
        misc_used = sem("misc_used")
        aux_v = sem("aux_v")
        aux_s = sem("aux_s")
        bc_ready = sem("bc_ready")
        cb_ready = sem("cb_ready")
        seg_ready = sem("seg_ready")
        exp_ready = sem("exp_ready")
        w_ready = sem("w_ready")
        y_done = sem("y_done")
        y_free = sem("y_free")
        score_ready = sem("score_ready")
        mask_done = sem("mask_done")
        max_ready = sem("max_ready")
        pexp_ready = sem("pexp_ready")
        p_ready = sem("p_ready")
        t_done = sem("t_done")
        pt_ready = sem("pt_ready")
        o_done = sem("o_done")
        v_done = sem("v_done")
        s_done = sem("s_done")
        g_done = sem("g_done")
        out_stored = sem("out_stored")

        block = ctx.enter_context(nc.Block())

        NSA_HEADS = [(j // 4 * 2 + half) * 4 + j % 4 for j in range(KD) for half in (0, 1)]

        def units_moba():
            for h in range(AH):
                base = (h % 2) * HD
                yield dict(q=Q, k=K, kt=h // 2, qt=h // 2, base=base, vcol=h * HD, slope=2.0 ** (-8.0 * (h + 1) / AH),
                           gate=None, first=True, last=True, tile=h // 2, cmp=None)

        def units_nsa():
            for n, h in enumerate(NSA_HEADS):
                g = h // 4
                for b, (k, vc) in enumerate(((KS, 0), (KW, 256))):
                    yield dict(q=QR, k=k, kt=g // 2, qt=n // 2, base=(n % 2) * HD, vcol=vc + g * HD, slope=None,
                               gate=h * NB + 1 + b, first=b == 0, last=b == 1, tile=n // 2, cmp=h)

        @block.sync
        def _(sp):
            sp.dma_start(vec[:, :], vec_in).then_inc(vec_landed, 16)

            def load_mod(n, m, wait):
                if wait is not None:
                    sp.wait_ge(mod_used, wait)
                sp.dma_start(mring[:, n % MRING, :, :], mod_in[m]).then_inc(mod_landed[n % MRING], 16)

            for n in range(MRING):
                load_mod(n, n, None)
            sp.dma_start(X[:, :, :], x_in).then_inc(x_landed, 16)
            sp.dma_start(con[:, :], con_in).then_inc(con_landed, 16)
            sp.dma_start(small[:, :], small_in).then_inc(small_landed, 16)
            for n in range(MRING, MSLOTS):
                load_mod(n, n, n - MRING + 1)
            for j in range(RING):
                sp.dma_start(ring[:, j, :], w_in[j]).then_inc(slot_landed[j], 16)
            MIX = (NMOD - 1) * MSLOTS // MRING
            with sp.Fori(1, MIX + 1) as it:
                for j in range(RING):
                    sp.wait_ge(slot_done, (it - 1) * RING + j + 1)
                    sp.dma_start(ring[:, j, :], w_in[it * RING + j]).then_inc(slot_landed[j], 16)
                for j in range(MRING):
                    load_mod(j, it * MRING + (MSLOTS - MRING) + j, it * MRING + (MSLOTS - 2 * MRING) + j + 1)
            with sp.Fori(MIX + 1, SLOTS // RING) as it:
                for j in range(RING):
                    sp.wait_ge(slot_done, (it - 1) * RING + j + 1)
                    sp.dma_start(ring[:, j, :], w_in[it * RING + j]).then_inc(slot_landed[j], 16)
            sp.wait_ge(x_ready, XR["end"])
            sp.dma_start(out, X[:, :, :]).then_inc(out_stored, 16)
            sp.wait_ge(out_stored, 16)

        @block.gpsimd
        def _(pool):
            order = Chain(pool, g_done)
            pool.wait_ge(mod_used, MSLOTS)
            pool.wait_ge(cact_ready, 1)

            def fold(m, it):
                n0 = m * MSLOTS
                for i in range(MSLOTS):
                    seg, kp = i // 4, i % 4
                    dst = modacc[:, m % 2, seg * D:(seg + 1) * D]
                    pool.wait_ge(mod_landed[i % MRING], 16 * ((n0 + i) // MRING + 1) + it * (16 * 2 * MSLOTS // MRING))
                    for e in range(2):
                        k = 2 * kp + e
                        w = mring[:, i % MRING, e, :]
                        if k == 0:
                            order.link(pool.tensor_tensor(dst, w, cact[:, k:k + 1].to_broadcast([P, D]), ALU.mult))
                        else:
                            order.link(pool.tensor_tensor(modprod[:, :], w, cact[:, k:k + 1].to_broadcast([P, D]), ALU.mult))
                            ins = pool.tensor_tensor(dst, dst, modprod[:, :], ALU.add)
                            if e == 1:
                                ins.then_inc(mod_used, 1)
                                pool.wait_ge(mod_used, n0 + i + 1 + it * 2 * MSLOTS)
                            else:
                                order.link(ins)

            fold(1, 0)
            links = order.n
            with pool.Fori(0, 2) as it:
                for m in (2, 3):
                    pool.wait_ge(mod_reduced, it * 2 + m - 1)
                    order.off = it * (2 * links)
                    fold(m, it)

        @block.tensor
        def _(pe):
            state = dict(h=0, free=0, sq=0, mod=0, misc=0)
            mm = pe.matmul

            def landed(n, it=0):
                pe.wait_ge(slot_landed[n % RING], 16 * (n // RING + 1) + it * 16)
                return ring[:, n % RING, :]

            def reduce_mod():
                m = state["mod"]
                pe.wait_ge(mod_used, MSLOTS * (m + 1))
                for j in range(24):
                    ins = mm(misc[:, j:j + 1], modacc[:, m % 2, j * P:(j + 1) * P], ones[:, 0:1],
                             start=True, stop=True, skip_group_check=True)
                ins.then_inc(mod_reduced, 1)
                state["mod"] += 1

            def sum_tiles(src, n):
                for m in range(n):
                    state["sq"] += 1
                    pe.wait_ge(sq_ready, state["sq"])
                    ins = mm(stat[:, 0:L], ones[:, :], src[:, m, :], start=(m == 0), stop=(m == n - 1),
                             skip_group_check=True)
                ins.then_inc(stat_ready, 1)

            def norm(mod):
                if mod:
                    reduce_mod()
                sum_tiles(H, KD)

            def pair(n, bank, src, it=0, first=False, inc=True):
                w = landed(n, it)
                for k in range(KD):
                    if first:
                        state["h"] += 1
                        pe.wait_ge(h_ready, state["h"])
                    for e in range(2):
                        ins = mm(bank[:, e * L:(e + 1) * L], w[:, k * L + e * P:k * L + (e + 1) * P], src[:, k, :],
                                 start=(k == 0 and e == 0), stop=(k == KD - 1), skip_group_check=True)
                ins.then_inc(slot_done, 1)

            def ffn(n0):
                f0 = state["free"]
                for b in range(4):
                    mm(acc[:, b, :], zeros[:, 0:P], zeros[:, :], start=True, stop=True, skip_group_check=True)

                def down(p, n, hb, it=0, split=False):
                    w = landed(n, it)
                    pe.wait_ge(pair_free, f0 + 2 * p + 2 + it * 4)
                    for m in range(KD):
                        for e in range(2):
                            ins = mm(acc_t(m), w[:, (e * KD + m) * P:(e * KD + m + 1) * P], hid_buf[:, hb + e, :],
                                     start=False, stop=False, skip_group_check=True)
                        if split and m % 2 and m < KD - 1:
                            ins.then_inc(down_ready, 1)
                    ins.then_inc(slot_done, 1)

                pair(n0, up[:, 0, :], H, first=True)
                pair(n0 + 1, up[:, 1, :], H)
                with pe.Fori(0, (PAIRS - 1) // 2) as it:
                    for q in range(2):
                        p = 1 + q
                        for e in range(2):
                            pe.wait_ge(pair_free, f0 + 2 * p + e - 1 + it * 4)
                            pair(n0 + 2 + 3 * q + e, up[:, e, :], H, it)
                        down(p - 1, n0 + 4 + 3 * q, 2 * q, it)
                down(PAIRS - 1, n0 + FSLOTS - 1, 0, split=True)
                state["free"] += NF

            def project_out(n0, src):
                for j in range(4):
                    w = landed(n0 + j)
                    for k in range(KD):
                        if j == 0:
                            state["h"] += 1
                            pe.wait_ge(h_ready, state["h"])
                        for e in range(2):
                            ins = mm(acc[:, j, e * L:(e + 1) * L], w[:, k * L + e * P:k * L + (e + 1) * P],
                                     src[:, k, :], start=(k == 0 and e == 0), stop=(k == KD - 1),
                                     skip_group_check=True)
                    ins.then_inc(slot_done, 1)

            def misc_step(ins):
                ins.then_inc(misc_ready, 1)
                state["misc"] += 1

            def misc_wait():
                pe.wait_ge(misc_used, state["misc"])

            def ssm(n0):
                pe.wait_ge(small_landed, 16)
                wdt = small[:, 0:KD * SH].rearrange("p (k n) -> p k n", k=KD)
                for k in range(KD):
                    state["h"] += 1
                    pe.wait_ge(h_ready, state["h"])
                    ins = mm(misc[0:SH, 0:L], wdt[:, k, :], H[:, k, :], start=(k == 0), stop=(k == KD - 1),
                             skip_group_check=True)
                misc_step(ins)
                f0 = state["free"]
                pair(n0, up[:, 0, :], H)
                pair(n0 + 1, up[:, 1, :], H)
                for n in range(2, RING):
                    pe.wait_ge(pair_free, f0 + n - 1)
                    pair(n0 + n, up[:, n % 2, :], H)
                with pe.Fori(0, 3) as it:
                    for n in range(RING, 2 * RING):
                        pe.wait_ge(pair_free, f0 + n - 1 + it * RING)
                        pair(n0 + n, up[:, n % 2, :], H, it)
                state["free"] += 24
                misc_wait()
                for q in range(2):
                    for tt in range(2):
                        j = 2 * q + tt
                        ins = pe.transpose(misc[:, j * SH:(j + 1) * SH], dts[0:SH, q, tt * P:(tt + 1) * P],
                                           ident[0:SH, 0:SH])
                misc_step(ins)
                misc_wait()
                tri0, tri1 = cs("tri", 0, L), cs("tri", L, TRI)
                mm(misc[:, 0:SH], tri0[:, 0:P], dtT[:, 2, :], start=True, stop=True, skip_group_check=True)
                mm(misc[:, SH:2 * SH], tri0[:, P:L], dtT[:, 2, :], start=True, stop=False, skip_group_check=True)
                misc_step(mm(misc[:, SH:2 * SH], tri1, dtT[:, 3, :], start=False, stop=True,
                             skip_group_check=True))
                pe.wait_ge(pair_free, state["free"])
                for j in range(8):
                    if j >= 2:
                        pe.wait_ge(pair_free, state["free"] - 1)
                    for tt in range(2):
                        for e in range(2):
                            ins = pe.transpose(up[:, j % 2, (2 * tt + e) * P:(2 * tt + e + 1) * P],
                                               XBC[:, 2 * j + e, tt * P:(tt + 1) * P], ident)
                    ins.then_inc(xt_ready, 1)
                    state["free"] += 1
                pe.wait_ge(pair_free, state["free"])

                def y(h):
                    pe.wait_ge(w_ready, h + 1)
                    if h % 2 == 0 and h >= 4:
                        pe.wait_ge(y_free, h // 2 - 1)
                    dst = up[(h % 2) * HD:(h % 2 + 1) * HD, (h // 2) % 2, 0:L]
                    mm(dst, XT[:, 0, h * HD:(h + 1) * HD], Wd[:, h % 2, 0:L], start=True, stop=False,
                       skip_group_check=True)
                    mm(dst[:, P:L], XT[:, 1, h * HD:(h + 1) * HD], Wd[:, h % 2, L:TRI], start=False, stop=True,
                       skip_group_check=True).then_inc(y_done, 1)

                for h in range(SH):
                    g = h // HPG
                    if h % HPG == 0:
                        if g >= 2:
                            pe.wait_ge(w_ready, HPG * (g - 1))
                        Bg, Cg = XBC[:, KI + g, :], XBC[:, KI + GRP + g, :]
                        mm(acc[:, 2 + g % 2, 0:L], Bg[:, 0:P], Cg, start=True, stop=True, skip_group_check=True)
                        mm(acc[:, 2 + g % 2, L:TRI], Bg[:, P:L], Cg[:, P:L], start=False, stop=True,
                           skip_group_check=True).then_inc(cb_ready, 1)
                    if h >= 2:
                        pe.wait_ge(seg_ready, h - 1)
                    mm(acc[:, h % 2, 0:L], dtT[:, 2, h:h + 1].to_broadcast([P, P]), tri0, start=True, stop=False,
                       skip_group_check=True)
                    mm(acc[:, h % 2, P:L], dtT[:, 3, h:h + 1].to_broadcast([P, P]), tri1, start=False,
                       stop=True, skip_group_check=True).then_inc(bc_ready, 1)
                    if h >= 1:
                        y(h - 1)
                y(SH - 1)
                sum_tiles(XBC, KI)
                for m in range(KD):
                    w = landed(n0 + 24 + m)
                    for k in range(KI):
                        if m == 0:
                            state["h"] += 1
                            pe.wait_ge(h_ready, state["h"])
                        ins = mm(acc_t(m), w[:, k * P:(k + 1) * P], Z[:, k, :], start=(k == 0 and m % 2 == 0),
                                 stop=(k == KI - 1), skip_group_check=True)
                    ins.then_inc(slot_done, 1)

            def value_pairs(n0, count):
                for j in range(count):
                    pe.wait_ge(pair_free, state["free"] - 1)
                    w = landed(n0 + j)
                    for k in range(KD):
                        for tt in range(2):
                            ins = mm(up[:, state["free"] % 2, tt * L:(tt + 1) * L], H[:, k, tt * P:(tt + 1) * P],
                                     w[:, k * L:(k + 1) * L], start=(k == 0 and tt == 0), stop=(k == KD - 1),
                                     skip_group_check=True)
                    ins.then_inc(slot_done, 1)
                    state["free"] += 1

            def pairs(n0, count):
                for j in range(count):
                    if j >= 2:
                        pe.wait_ge(pair_free, state["free"] - 1)
                    pair(n0 + j, up[:, state["free"] % 2, :], H, first=(j == 0))
                    state["free"] += 1

            def attention(units, base):
                units = list(units)
                n = len(units)
                for u in range(n + 2):
                    if u < n:
                        a = units[u]
                        if u >= 2:
                            pe.wait_ge(mask_done, base["u"] + u - 1)
                        q = a["q"][a["base"]:a["base"] + HD, a["qt"], :]
                        k = a["k"][a["base"]:a["base"] + HD, a["kt"], :]
                        mm(acc[:, u % 2, 0:P], q[:, 0:P], k[:, 0:P], start=True, stop=True, skip_group_check=True)
                        mm(acc[:, u % 2, P:TRI], q[:, P:L], k, start=False, stop=True,
                           skip_group_check=True).then_inc(score_ready, 1)
                    if 1 <= u <= n:
                        t = u - 1
                        pe.wait_ge(p_ready, base["u"] + t + 1)
                        if t >= 2:
                            pe.wait_ge(pt_ready, base["u"] + t - 1)
                        pb = Pb[:, t % 3, :]
                        pe.transpose(acc[:, 2 + t % 2, 0:P], pb[:, 0:P], ident)
                        pe.transpose(acc[:, 2 + t % 2, P:L], pb[:, P:L], ident)
                        pe.transpose(acc[:, 2 + t % 2, L:TRI], pb[:, L:TRI], ident).then_inc(t_done, 1)
                    if u >= 2:
                        t = u - 2
                        a = units[t]
                        pe.wait_ge(pt_ready, base["u"] + t + 1)
                        if a["first"] and a["base"] == 0 and a["tile"] >= 2:
                            pe.wait_ge(h_ready, state["h"] + a["tile"] - 1)
                        dst = up[a["base"]:a["base"] + HD, a["tile"] % 2, 0:L]
                        v = a["vcol"]
                        if a["cmp"] is not None and a["first"]:
                            r, g = a["cmp"] % 4, a["cmp"] // 4
                            mm(dst, vcmp[32 * r:32 * r + 32, g, :], PC[32 * r:32 * r + 32, g, :], start=True,
                               stop=False, skip_group_check=True)
                        mm(dst, V[:, 0, v:v + HD], PT[:, t % 2, 0:L], start=(a["first"] and a["cmp"] is None),
                           stop=False, skip_group_check=True)
                        mm(dst[:, P:L], V[:, 1, v:v + HD], PT[:, t % 2, L:TRI], start=False, stop=a["last"],
                           skip_group_check=True).then_inc(o_done, 1)

            def moba(n0):
                pairs(n0, 8)
                value_pairs(n0 + 8, 4)
                pe.wait_ge(pair_free, state["free"])
                attention(units_moba(), UNITS["moba"])
                project_out(n0 + 12, O)

            def conformer(n0):
                pairs(n0, 8)
                sum_tiles_plain(CV)
                sum_tiles(H, KD)
                project_out(n0 + 8, CV)

            def sum_tiles_plain(src):
                for m in range(KD):
                    state["h"] += 1
                    pe.wait_ge(h_ready, state["h"])
                    ins = mm(stat[:, 0:L], ones[:, :], src[:, m, :], start=(m == 0), stop=(m == KD - 1),
                             skip_group_check=True)
                ins.then_inc(stat_ready, 1)

            def head_stat(rhs, n):
                misc_wait()
                state["sq"] += 1
                pe.wait_ge(sq_ready, state["sq"])
                misc_step(mm(misc[:, 0:n], cs("block", 0, P), rhs, start=True, stop=True, skip_group_check=True))

            def nsa(n0):
                qk = [(0, Q), (2, Q), (4, Q), (6, Q), (0, KS), (0, KW)]

                def rotate(j):
                    head_stat(sqb[:, 0:512], 512)
                    misc_wait()
                    t0, buf = qk[j]
                    for e in range(2):
                        ins = mm(misc[:, e * L:(e + 1) * L], cs("rope", 0, P), buf[:, t0 + e, :],
                                 start=(e == 0), stop=True, skip_group_check=True)
                    misc_step(ins)

                pe.wait_ge(con_landed, 16)
                wgl = small[:, SMALL["w_gl"]:SMALL["w_gl"] + KD * 48].rearrange("p (k n) -> p k n", k=KD)
                misc_wait()
                for k in range(KD):
                    state["h"] += 1
                    pe.wait_ge(h_ready, state["h"])
                    for tt in range(2):
                        ins = mm(misc[:, tt * 48:(tt + 1) * 48], H[:, k, tt * P:(tt + 1) * P], wgl[:, k, :],
                                 start=(k == 0 and tt == 0), stop=(k == KD - 1), skip_group_check=True)
                misc_step(ins)
                for j in range(8):
                    if j >= 2:
                        pe.wait_ge(pair_free, state["free"] - 1)
                    pair(n0 + j, up[:, state["free"] % 2, :], H)
                    state["free"] += 1
                    if 1 <= j <= 6:
                        rotate(j - 1)
                value_pairs(n0 + 8, 2)
                for c, (src, second) in enumerate(((KC, "ck2"), (VC, "cv2"))):
                    pe.wait_ge(pair_free, state["free"])
                    for g in range(4):
                        ins = mm(up[:, g // 2, (g % 2) * L:(g % 2 + 1) * L], cs(f"pick{g % 2}", 0, P),
                                 src[:, g // 2, :], start=(g % 2 == 0), stop=True, skip_group_check=True)
                    misc_step(ins)
                    misc_wait()
                    for m in range(2):
                        w = landed(n0 + 10 + 2 * c + m)
                        for k in range(16):
                            ins = mm(stat[:, 60 * m:60 * m + 60], w[:, k * P:(k + 1) * P], zk[:, k, :],
                                     start=(k == 0 and m == 0), stop=(k == 15), skip_group_check=True)
                        ins.then_inc(slot_done, 1)
                    w2 = small[:, SMALL[second]:SMALL[second] + 2 * HD].rearrange("p (k n) -> p k n", k=2)
                    state["h"] += 1
                    pe.wait_ge(h_ready, state["h"])
                    if c == 0:
                        hk = hidc.rearrange("p m (a b n) -> p m a b n", a=2, b=2)
                        for par in range(2):
                            for m in range(2):
                                ins = mm(misc[par * HD:(par + 1) * HD, 0:30], w2[:, m, :], hk[:, m, :, par, :],
                                         start=(m == 0), stop=(m == 1), skip_group_check=True)
                        misc_step(ins)
                        head_stat(sqb[:, 0:30], 30)
                    else:
                        misc_wait()
                        for g in range(4):
                            for m in range(2):
                                ins = mm(misc[:, g * HD:(g + 1) * HD], hidr[:, m, g * P:(g + 1) * P], w2[:, m, :],
                                         start=(g == 0 and m == 0), stop=(m == 1), skip_group_check=True)
                        misc_step(ins)
                misc_wait()
                kc3 = kcmp.rearrange("p (a n) -> p a n", a=2)
                for tt in range(2):
                    for base in (0, 1):
                        for j in range(KD):
                            ins = mm(acc[:, 2 * tt + base, j * 32:j * 32 + NCMP],
                                     Q[base * HD:(base + 1) * HD, j, tt * P:(tt + 1) * P],
                                     kc3[base * HD:(base + 1) * HD, j // 4, :], start=(j == 0),
                                     stop=True, skip_group_check=True)
                misc_step(ins)
                misc_wait()
                for g in range(4):
                    for tt in range(2):
                        ins = pe.transpose(up[:, g // 2, ((g % 2) * 2 + tt) * P:((g % 2) * 2 + tt + 1) * P],
                                           pc[:, tt, g * P:(g + 1) * P], ident)
                misc_step(ins)
                misc_wait()
                attention(units_nsa(), UNITS["nsa"])
                project_out(n0 + 14, O)

            pe.wait_ge(setup_done, 3)
            norm(True)
            ffn(AT_SLOT["ffn0"])
            norm(True)
            pe.wait_ge(con_landed, 16)
            ssm(AT_SLOT["ssm"])
            norm(True)
            ffn(AT_SLOT["ffn1"])
            norm(True)
            ffn(AT_SLOT["ffn2"])
            norm(True)
            moba(AT_SLOT["moba"])
            norm(True)
            ffn(AT_SLOT["ffn3"])
            norm(False)
            state["h"] += KD
            norm(False)
            conformer(AT_SLOT["conf"])
            norm(False)
            ffn(AT_SLOT["cffn0"])
            norm(False)
            nsa(AT_SLOT["nsa"])
            norm(False)
            ffn(AT_SLOT["cffn1"])

        @block.scalar
        def _(act):
            state = dict(x=0, h=0, xn=0, stat=0, free=0, silu=0, dwc=0, misc=0, aux_v=0, mod=0)
            order = Chain(act, s_done)

            def root(width, n=L):
                state["stat"] += 1
                act.wait_ge(stat_ready, state["stat"])
                act.activation(rstd[:, 0:n], stat[:, 0:n], ACT.Sqrt, scale=1.0 / width,
                               bias=eps[:, 0:1]).then_inc(root_ready, 1)

            def norm(scale, shift=None, mod=False, dest=H, own=False, first=False):
                for m in range(KD):
                    if own:
                        act.wait_ge(h_ready, state["h"] - KD + m + 1)
                    elif first:
                        act.wait_ge(x_landed, 16)
                    else:
                        state["x"] += 1
                        act.wait_ge(x_ready, state["x"])
                    act.activation(H[:, m, :], X[:, m, :], ACT.Square).then_inc(sq_ready, 1)
                root(D)
                if mod:
                    state["mod"] += 1
                    act.wait_ge(modvec_ready, state["mod"])
                for m in range(KD):
                    state["xn"] += 1
                    act.wait_ge(xn_ready, state["xn"])
                    if shift is None:
                        ins = act.activation(dest[:, m, :], H[:, m, :], ACT.Copy, scale=scale(m))
                    else:
                        ins = act.activation(dest[:, m, :], H[:, m, :], ACT.Identity, scale=scale(m), bias=shift(m))
                    ins.then_inc(h_ready, 1)
                    state["h"] += 1

            def mod_norm(first=False):
                norm(lambda m: modsc[:, m:m + 1], lambda m: modv[:, m:m + 1], mod=True, first=first)

            def slot_of(n0, f):
                return n0 + f if f < 2 else n0 + 2 + 3 * (f // 2 - 1) + f % 2

            def over_hidden(n0, one):
                for f in range(2):
                    one(f, 0)
                with act.Fori(0, (NF - 2) // 4) as it:
                    for f in range(2, 6):
                        one(f, it)

            def ffn(n0):
                def one(f, it):
                    act.wait_ge(slot_done, slot_of(n0, f) + 1 + it * 6)
                    if f >= 2:
                        act.wait_ge(pair_free, state["free"] + f - 1 + it * 4)
                    act.activation(act_buf[:, f % 2, :], up[:, f % 2, 0:L], ACT.Silu).then_inc(silu_ready, 1)

                over_hidden(n0, one)
                state["free"] += NF

            def conv_ffn(n0):
                def one(f, it):
                    act.wait_ge(dwc_ready, state["dwc"] + f + 1 + it * 4)
                    a = act_buf[:, f % 2, :]
                    act.activation(a, a, ACT.Silu).then_inc(silu_ready, 1)

                over_hidden(n0, one)
                state["dwc"] += NF
                state["free"] += NF

            def aux_wait():
                state["aux_v"] += 1
                act.wait_ge(aux_v, state["aux_v"])

            def ssm(n0):
                aux_wait()
                act.activation(dts[0:SH, 1, :], dts[0:SH, 1, :], ACT.Exp).then_inc(aux_s, 1)
                act.activation(negA, v1("a_log")[0:SH, :], ACT.Exp).then_inc(aux_s, 1)
                act.wait_ge(aux_s, 2)
                act.activation(Wd[0:SH, 0, 0:L], dts[0:SH, 1, :], ACT.Ln, bias=ones[0:SH, 0:1]).then_inc(aux_s, 1)
                f0 = state["free"]
                with act.Fori(0, 8) as it:
                    for j in range(2):
                        act.wait_ge(pair_free, f0 + 1 + j + it * 2)
                        v = XBC[:, bass.ds(it * 4 + 2 * j, 2), :]
                        act.activation(v, v, ACT.Silu).then_inc(silu_ready, 1)
                with act.Fori(0, 4) as it:
                    for j in range(2):
                        act.wait_ge(slot_done, n0 + 17 + j + it * 2)
                        act.activation(Z[:, bass.ds(it * 4 + 2 * j, 2), :], up[:, j, :].rearrange("p (a t) -> p a t", a=2),
                                       ACT.Silu).then_inc(pair_free, 1)
                state["free"] += 24 + 8
                state["silu"] += 16

                def square(m):
                    act.wait_ge(y_free, 0 + m + 1)
                    act.activation(XBC[:, m, :], Z[:, m, :], ACT.Square).then_inc(sq_ready, 1)

                for h in range(SH):
                    act.wait_ge(seg_ready, h + 1)
                    act.activation(Wd[:, h % 2, :], Wd[:, h % 2, :], ACT.Exp).then_inc(exp_ready, 1)
                    if h >= 5 and h % 2:
                        square((h - 5) // 2)
                for m in range(SH // 2 - 2, SH // 2):
                    square(m)
                root(INNER)

            def attention(units, base):
                units = list(units)
                n = len(units)
                for u in range(n + 1):
                    if u < n:
                        act.wait_ge(max_ready, base["u"] + u + 1)
                        b = u % 3
                        for tt, (c0, c1) in enumerate(((0, P), (P, TRI))):
                            ins = act.activation(Pb[:, b, c0:c1], Pb[:, b, c0:c1], ACT.Exp, bias=nmax[:, b, tt:tt + 1],
                                                 accum_out=psum_[:, b, tt:tt + 1])
                        ins.then_inc(pexp_ready, 1)
                    if u >= 1:
                        t = u - 1
                        act.wait_ge(t_done, base["u"] + t + 1)
                        if t >= 2:
                            act.wait_ge(o_done, base["u"] + t - 1)
                        act.activation(PT[:, t % 2, :], acc[:, 2 + t % 2, 0:TRI], ACT.Copy).then_inc(pt_ready, 1)

            def evacuate(n, dst, scale=1.0):
                act.wait_ge(slot_done, n + 1)
                act.activation(dst, up[:, state["free"] % 2, :].rearrange("p (a t) -> p a t", a=2), ACT.Copy,
                               scale=scale).then_inc(pair_free, 1)
                state["free"] += 1

            def moba(n0):
                for j in range(4):
                    evacuate(n0 + j, Q[:, 2 * j:2 * j + 2, :], HD ** -0.5)
                for j in range(4):
                    evacuate(n0 + 4 + j, K[:, 2 * j:2 * j + 2, :])
                for j in range(4):
                    evacuate(n0 + 8 + j, V[:, :, j * L:(j + 1) * L])
                attention(units_moba(), UNITS["moba"])
                state["h"] += KD

            def conformer(n0):
                for m in range(KD):
                    act.wait_ge(slot_done, n0 + m + 1)
                    if m >= 2:
                        act.wait_ge(pair_free, state["free"] - 1)
                    act.activation(sgb[:, m % 2, :], up[:, state["free"] % 2, L:2 * L], ACT.Sigmoid,
                                   bias=v1("b_pw1", KD + m)).then_inc(silu_ready, 1)
                    state["free"] += 1
                state["h"] += KD
                state["stat"] += 1
                for m in range(KD):
                    aux_wait()
                    act.activation(H[:, m, :], CV[:, m, :], ACT.Square).then_inc(sq_ready, 1)
                root(D)
                for m in range(KD):
                    state["xn"] += 1
                    act.wait_ge(xn_ready, state["xn"])
                    act.activation(CV[:, m, :], CV[:, m, :], ACT.Silu, scale=v1("ln_g", m),
                                   bias=v1("ln_b", m)).then_inc(h_ready, 1)
                    state["h"] += 1

            def head_root(n):
                state["misc"] += 1
                act.wait_ge(misc_ready, state["misc"])
                act.activation(rstd[:, 0:n], misc[:, 0:n], ACT.Sqrt, scale=1.0 / HD,
                               bias=eps[:, 0:1]).then_inc(root_ready, 1)

            def nsa(n0):
                base = UNITS["misc_at_nsa"]
                state["misc"] = base + 1
                act.wait_ge(misc_ready, state["misc"])
                act.activation(gates.rearrange("p a b -> p (a b)"), misc[:, 0:96], ACT.Sigmoid).then_inc(misc_used, 1)
                dst = [Q[:, 2 * j:2 * j + 2, :] for j in range(4)] + [KS, KW, KC, VC]
                for j in range(8):
                    if 1 <= j <= 5:
                        act.wait_ge(misc_used, base + 1 + 2 * j)
                    evacuate(n0 + j, dst[j])
                    if j < 6:
                        act.wait_ge(pair_free, state["free"])
                        act.activation(sqb[:, :], dst[j].rearrange("p a t -> p (a t)"), ACT.Square).then_inc(sq_ready, 1)
                        head_root(512)
                        state["misc"] += 1
                for j in range(2):
                    evacuate(n0 + 8 + j, V[:, :, j * L:(j + 1) * L])
                for c in range(2):
                    state["misc"] += 1
                    act.wait_ge(slot_done, n0 + 12 + 2 * c)
                    if c == 0:
                        act.activation(hidc.rearrange("p m n -> p (m n)"), stat[:, 0:120], ACT.Silu).then_inc(h_ready, 1)
                        state["misc"] += 1
                        act.wait_ge(misc_used, state["misc"])
                        act.activation(sqb[:, 0:30], kcmp, ACT.Square).then_inc(sq_ready, 1)
                        head_root(30)
                    else:
                        act.activation(hidc.rearrange("p m n -> p (m n)"), stat[:, 0:120], ACT.Silu).then_inc(aux_s, 1)
                    state["h"] += 1
                aux_wait()
                act.activation(pc, pc, ACT.Exp).then_inc(aux_s, 1)
                attention(units_nsa(), UNITS["nsa"])
                state["h"] += KD

            act.wait_ge(vec_landed, 16)
            act.activation(cact[:, :], v1("c", 0, KD), ACT.Silu).then_inc(cact_ready, 1)
            act.wait_ge(setup_done, 3)
            mod_norm(first=True)
            ffn(AT_SLOT["ffn0"])
            mod_norm()
            ssm(AT_SLOT["ssm"])
            state["h"] += KI
            mod_norm()
            ffn(AT_SLOT["ffn1"])
            mod_norm()
            ffn(AT_SLOT["ffn2"])
            mod_norm()
            moba(AT_SLOT["moba"])
            mod_norm()
            ffn(AT_SLOT["ffn3"])
            norm(lambda m: v1("final_g", m), dest=X)
            norm(lambda m: v1("mix_g", m), own=True)
            conformer(AT_SLOT["conf"])
            norm(lambda m: v1("ffn_g", m))
            conv_ffn(AT_SLOT["cffn0"])
            norm(lambda m: v1("mix_g", KD + m))
            nsa(AT_SLOT["nsa"])
            norm(lambda m: v1("ffn_g", KD + m))
            conv_ffn(AT_SLOT["cffn1"])

        @block.vector
        def _(dve):
            state = dict(root=0, free=0, silu=0, misc=0, mod=0, down=0, aux_s=3, xn=0)
            order = Chain(dve, v_done)
            link = order.link

            def norm(mod=None, half=1.0):
                if mod is not None:
                    state["mod"] += 1
                    dve.wait_ge(mod_reduced, state["mod"])
                    link(dve.tensor_tensor(modv[:, :], misc[:, 0:24], v1("mod_b", mod * 24, 24), ALU.add))
                    link(dve.tensor_scalar(gate[:, :], modv[:, 16:24], half, None, ALU.mult))
                    dve.scalar_tensor_tensor(out=modsc[:, :], in0=modv[:, 8:16], scalar=1.0,
                                             in1=v1("norm_g", mod * KD, KD), op0=ALU.add,
                                             op1=ALU.mult).then_inc(modvec_ready, 1)
                state["root"] += 1
                dve.wait_ge(root_ready, state["root"])
                link(dve.reciprocal(rstd[:, 0:L], rstd[:, 0:L]))
                for m in range(KD):
                    dve.tensor_tensor(H[:, m, :], X[:, m, :], rstd[:, 0:L], ALU.mult).then_inc(xn_ready, 1)
                state["xn"] += KD

            def update(m, how):
                if how == "gate":
                    ins = dve.scalar_tensor_tensor(out=X[:, m, :], in0=acc_t(m), scalar=gate[:, m:m + 1],
                                                   in1=X[:, m, :], op0=ALU.mult, op1=ALU.add)
                elif how == "bias":
                    ins = dve.scalar_tensor_tensor(out=X[:, m, :], in0=acc_t(m), scalar=v1("b_pw2", m),
                                                   in1=X[:, m, :], op0=ALU.add, op1=ALU.add)
                else:
                    ins = dve.tensor_tensor(X[:, m, :], acc_t(m), X[:, m, :], ALU.add)
                ins.then_inc(x_ready, 1)

            def update_ffn(n0, how):
                for m in range(KD):
                    if m < KD - 2 and m % 2 == 0:
                        state["down"] += 1
                        dve.wait_ge(down_ready, state["down"])
                    elif m == KD - 2:
                        dve.wait_ge(slot_done, n0 + FSLOTS)
                    update(m, how)

            def update_slots(n0, per, how):
                for m in range(KD):
                    if m % 2 == 0:
                        dve.wait_ge(slot_done, n0 + (m + 2) // per)
                    update(m, how)

            def over_hidden(one, links):
                for f in range(2):
                    one(f, 0)
                before = order.n
                with dve.Fori(0, (NF - 2) // 4) as it:
                    for f in range(2, 6):
                        order.off = it * links if links else 0
                        one(f, it)
                assert order.n - before == links
                order.n = before + links * ((NF - 2) // 4)
                order.off = 0

            def hidden_free(n0, f, it):
                if f >= 2:
                    dve.wait_ge(slot_done, n0 + 3 * (f // 2) - 1 + it * 6)

            def ffn(n0):
                def one(f, it):
                    dve.wait_ge(silu_ready, state["silu"] + f + 1 + it * 4)
                    hidden_free(n0, f, it)
                    dve.tensor_tensor(hid_buf[:, f % 4, :], act_buf[:, f % 2, :], up[:, f % 2, L:2 * L],
                                      ALU.mult).then_inc(pair_free, 1)

                over_hidden(one, 0)
                state["silu"] += NF
                state["free"] += NF
                update_ffn(n0, "gate")

            def conv_ffn(n0, i):
                def one(f, it):
                    slot = n0 + f if f < 2 else n0 + 2 + 3 * (f // 2 - 1) + f % 2
                    dve.wait_ge(slot_done, slot + 1 + it * 6)
                    o, a = act_buf[:, f % 2, :], up[:, f % 2, 0:L]

                    def col(name, c):
                        return vec[:, bass.ds(it * 4 + (VEC[name] + c + f), 1)] if f >= 2 else v1(name, c + f)

                    w = [col("ffn_dw", (3 * i + j) * NF) for j in range(3)]
                    link(dve.tensor_scalar(o, a, w[2], col("ffn_db", i * NF), ALU.mult, ALU.add))
                    link(dve.scalar_tensor_tensor(out=o[:, 1:L], in0=a[:, 0:L - 1], scalar=w[1], in1=o[:, 1:L],
                                                  op0=ALU.mult, op1=ALU.add))
                    dve.scalar_tensor_tensor(out=o[:, 2:L], in0=a[:, 0:L - 2], scalar=w[0], in1=o[:, 2:L],
                                             op0=ALU.mult, op1=ALU.add).then_inc(dwc_ready, 1)
                    dve.wait_ge(silu_ready, state["silu"] + f + 1 + it * 4)
                    hidden_free(n0, f, it)
                    dve.tensor_tensor(hid_buf[:, f % 4, :], o, up[:, f % 2, L:2 * L], ALU.mult).then_inc(pair_free, 1)

                over_hidden(one, 8)
                state["silu"] += NF
                state["free"] += NF
                update_ffn(n0, "plain")

            def misc_wait():
                state["misc"] += 1
                dve.wait_ge(misc_ready, state["misc"])

            def ssm(n0):
                misc_wait()
                v, e, lnu = dts[0:SH, 0, :], dts[0:SH, 1, :], Wd[0:SH, 0, 0:L]
                u, dt = Wd[0:SH, 1, 0:L], dts[0:SH, 0, :]
                link(dve.tensor_scalar(v, misc[0:SH, 0:L], v1("dt_bias")[0:SH, :], None, ALU.add))
                dve.scalar_tensor_tensor(out=e, in0=v, scalar=-1.0, in1=v, op0=ALU.mult,
                                         op1=ALU.min).then_inc(aux_v, 1)
                dve.wait_ge(aux_s, 3)
                link(dve.tensor_scalar(u, e, 1.0, -1.0, ALU.add, ALU.add))
                link(dve.tensor_tensor(lnu, lnu, e, ALU.mult))
                link(dve.scalar_tensor_tensor(out=e, in0=u, scalar=0.0, in1=e, op0=ALU.is_equal, op1=ALU.mult))
                link(dve.tensor_scalar(u, u, 1e-30, None, ALU.max))
                link(dve.reciprocal(u, u))
                link(dve.tensor_tensor(lnu, lnu, u, ALU.mult))
                link(dve.tensor_tensor(lnu, lnu, e, ALU.add))
                link(dve.scalar_tensor_tensor(out=dt, in0=v, scalar=0.0, in1=lnu, op0=ALU.max, op1=ALU.add))
                link(dve.tensor_scalar(negA, negA, -1.0, None, ALU.mult))
                dve.tensor_scalar(e, dt, negA, None, ALU.mult).then_inc(misc_used, 1)
                per = 14
                before = order.n
                with dve.Fori(0, 8) as it:
                    for j in range(2):
                        dve.wait_ge(slot_done, n0 + 1 + j + it * 2)
                        order.off = it * per
                        for tap in range(4):
                            for t in range(2):
                                c = it * 4 + 2 * j + t
                                a = up[:, j, t * L:(t + 1) * L]
                                o = XBC[:, bass.ds(c, 1), :].rearrange("p a t -> p (a t)")
                                w = vec[:, bass.ds(c + (VEC["conv_w"] + (3 - tap) * 32), 1)]
                                if tap == 0:
                                    ins = dve.tensor_scalar(o, a, w, vec[:, bass.ds(c + VEC["conv_b"], 1)],
                                                            ALU.mult, ALU.add)
                                else:
                                    ins = dve.scalar_tensor_tensor(out=o[:, tap:L], in0=a[:, 0:L - tap], scalar=w,
                                                                   in1=o[:, tap:L], op0=ALU.mult, op1=ALU.add)
                                if tap == 3 and t == 1:
                                    ins.then_inc(pair_free, 1)
                                else:
                                    link(ins)
                assert order.n - before == per
                order.n, order.off = before + per * 8, 0
                state["free"] += 24
                state["silu"] += 16
                misc_wait()
                dve.tensor_copy(dtT.rearrange("p a h -> p (a h)"), misc[:, 0:4 * SH]).then_inc(misc_used, 1)
                dve.wait_ge(misc_used, 2)
                misc_wait()
                dve.tensor_copy(acT.rearrange("p a h -> p (a h)"), misc[:, 0:2 * SH]).then_inc(misc_used, 1)
                dve.wait_ge(misc_used, 3)
                for j in range(8):
                    dve.wait_ge(xt_ready, j + 1)
                    dve.tensor_tensor(
                        XT[:, :, j * L:(j + 1) * L].rearrange("p a (h c) -> p a h c", c=HD),
                        up[:, j % 2, :].rearrange("p (a h c) -> p a h c", a=2, c=HD),
                        dtT[:, 0:2, 4 * j:4 * j + 4].unsqueeze(3).to_broadcast([P, 2, 4, HD]),
                        ALU.mult).then_inc(pair_free, 1)
                state["free"] += 8

                def weight(h):
                    dve.wait_ge(exp_ready, h + 1)
                    if h % HPG == 0:
                        dve.wait_ge(cb_ready, h // HPG + 1)
                    dve.tensor_tensor(Wd[:, h % 2, :], Wd[:, h % 2, :], acc[:, 2 + (h // HPG) % 2, 0:TRI],
                                      ALU.mult).then_inc(w_ready, 1)

                def gated(m):
                    dve.wait_ge(y_done, 2 * m + 2)
                    Yt = H[:, m % 4, :]
                    link(dve.scalar_tensor_tensor(out=Yt, in0=XBC[:, m, :], scalar=v1("ssm_d", m),
                                                  in1=up[:, m % 2, 0:L], op0=ALU.mult, op1=ALU.add))
                    dve.tensor_tensor(Z[:, m, :], Z[:, m, :], Yt, ALU.mult).then_inc(y_free, 1)

                for h in range(SH):
                    dve.wait_ge(bc_ready, h + 1)
                    if h >= 2:
                        dve.wait_ge(y_done, h - 1)
                    dve.scalar_tensor_tensor(out=Wd[:, h % 2, 0:L], in0=acc[:, h % 2, 0:L], scalar=acT[:, 0, h:h + 1],
                                             in1=cs("mask_sq", 0, L), op0=ALU.subtract, op1=ALU.add)
                    dve.scalar_tensor_tensor(out=Wd[:, h % 2, L:TRI], in0=acc[:, h % 2, P:L],
                                             scalar=acT[:, 1, h:h + 1], in1=cs("mask_sq", L, TRI), op0=ALU.subtract,
                                             op1=ALU.add).then_inc(seg_ready, 1)
                    if h >= 1:
                        weight(h - 1)
                    if h >= 4 and h % 2 == 0:
                        gated((h - 4) // 2)
                weight(SH - 1)
                gated(SH // 2 - 2)
                gated(SH // 2 - 1)
                state["root"] += 1
                dve.wait_ge(root_ready, state["root"])
                link(dve.reciprocal(rstd[:, 0:L], rstd[:, 0:L]))
                for m in range(KI):
                    dve.scalar_tensor_tensor(out=Z[:, m, :], in0=Z[:, m, :], scalar=v1("ssm_norm", m),
                                             in1=rstd[:, 0:L], op0=ALU.mult, op1=ALU.mult).then_inc(h_ready, 1)
                update_slots(n0 + 24, 1, "gate")

            def attention(units, base):
                units = list(units)
                n = len(units)

                def normalise(t):
                    a, b = units[t], t % 3
                    dve.wait_ge(pexp_ready, base["u"] + t + 1)
                    link(dve.reciprocal(psum_[:, b, :], psum_[:, b, :]))
                    if a["gate"] is not None:
                        link(dve.tensor_tensor(psum_[:, b, :], psum_[:, b, :], gates[:, :, a["gate"]], ALU.mult))
                    for tt, (c0, c1) in enumerate(((0, P), (P, TRI))):
                        ins = dve.tensor_scalar(Pb[:, b, c0:c1], Pb[:, b, c0:c1], psum_[:, b, tt:tt + 1], None, ALU.mult)
                    ins.then_inc(p_ready, 1)

                def take(t):
                    a = units[t]
                    if a["last"] and a["base"] == HD:
                        dve.wait_ge(o_done, base["u"] + t + 1)
                        dve.tensor_copy(O[:, a["tile"], :], up[:, a["tile"] % 2, 0:L]).then_inc(h_ready, 1)

                for u in range(n + 3):
                    if u < n:
                        a, b = units[u], u % 3
                        dve.wait_ge(score_ready, base["u"] + u + 1)
                        if u >= 3:
                            dve.wait_ge(t_done, base["u"] + u - 2)
                        if a["slope"] is not None:
                            dve.scalar_tensor_tensor(out=Pb[:, b, :], in0=cs("dist", 0, TRI), scalar=a["slope"],
                                                     in1=acc[:, u % 2, 0:TRI], op0=ALU.mult,
                                                     op1=ALU.add).then_inc(mask_done, 1)
                        else:
                            dve.tensor_tensor(Pb[:, b, :], acc[:, u % 2, 0:TRI], cs("mask_qk", 0, TRI),
                                              ALU.add).then_inc(mask_done, 1)
                        dve.wait_ge(mask_done, base["u"] + u + 1)
                        dve.tensor_reduce(nmax[:, b, 0:1], Pb[:, b, 0:P], AX_X, ALU.max, negate=True)
                        dve.tensor_reduce(nmax[:, b, 1:2], Pb[:, b, P:TRI], AX_X, ALU.max,
                                          negate=True).then_inc(max_ready, 1)
                    if 1 <= u <= n:
                        normalise(u - 1)
                    if u >= 3:
                        take(u - 3)

            def moba(n0):
                state["free"] += 12
                attention(units_moba(), UNITS["moba"])
                update_slots(n0 + 12, 2, "gate")

            def conformer(n0):
                link(dve.memset(UP[:, :, 0:30], 0.0))
                for m in range(KD):
                    state["silu"] += 1
                    dve.wait_ge(silu_ready, state["silu"])
                    dve.scalar_tensor_tensor(out=UP[:, m, 30:30 + L], in0=up[:, state["free"] % 2, 0:L],
                                             scalar=v1("b_pw1", m), in1=sgb[:, m % 2, :], op0=ALU.add,
                                             op1=ALU.mult).then_inc(pair_free, 1)
                    state["free"] += 1
                    dve.wait_ge(pair_free, state["free"])
                    link(dve.tensor_scalar(CV[:, m, :], UP[:, m, 0:L], v1("w_dw", m), v1("b_dw", m), ALU.mult, ALU.add))
                    for tap in range(1, 31):
                        ins = dve.scalar_tensor_tensor(out=CV[:, m, :], in0=UP[:, m, tap:tap + L],
                                                       scalar=v1("w_dw", tap * KD + m), in1=CV[:, m, :], op0=ALU.mult,
                                                       op1=ALU.add)
                        if tap < 30:
                            link(ins)
                        else:
                            ins.then_inc(h_ready, 1)
                state["stat"] = UNITS["stat_at_conf"] + 1
                dve.wait_ge(stat_ready, state["stat"])
                link(dve.tensor_scalar(rstd[:, L:2 * L], stat[:, 0:L], 1.0 / D, None, ALU.mult))
                for m in range(KD):
                    dve.tensor_tensor(CV[:, m, :], CV[:, m, :], rstd[:, L:2 * L], ALU.subtract).then_inc(aux_v, 1)
                state["root"] += 1
                dve.wait_ge(root_ready, state["root"])
                link(dve.reciprocal(rstd[:, 0:L], rstd[:, 0:L]))
                for m in range(KD):
                    dve.tensor_tensor(CV[:, m, :], CV[:, m, :], rstd[:, 0:L], ALU.mult).then_inc(xn_ready, 1)
                state["xn"] += KD
                update_slots(n0 + 8, 2, "bias")

            def head_norm(v, n, g, scale):
                state["root"] += 1
                dve.wait_ge(root_ready, state["root"])
                link(dve.reciprocal(rstd[:, 0:n], rstd[:, 0:n]))
                link(dve.tensor_scalar(rstd[:, 0:n], rstd[:, 0:n], v1(g), scale, ALU.mult, ALU.mult))
                return dve.tensor_tensor(v, v, rstd[:, 0:n], ALU.mult)

            def nsa(n0):
                state["misc"] = UNITS["misc_at_nsa"] + 1
                link(dve.memset(pc, 0.0))
                link(dve.memset(hidr, 0.0))
                gains = ["q_norm"] * 4 + ["ks_norm", "kw_norm"]
                cos = cs("cos", 0, L).unsqueeze(1).to_broadcast([P, 2, L])
                sin = cs("sin", 0, L).unsqueeze(1).to_broadcast([P, 2, L])
                for j in range(6):
                    v = Q[:, 2 * j:2 * j + 2, :] if j < 4 else (KS, KW)[j - 4]
                    state["misc"] += 1
                    head_norm(v.rearrange("p a t -> p (a t)"), 512, gains[j],
                              HD ** -0.5 if j < 4 else 1.0).then_inc(misc_used, 1)
                    state["misc"] += 1
                    dve.wait_ge(misc_ready, state["misc"])
                    rot = rstd[:, :].rearrange("p (a t) -> p a t", a=2)
                    link(dve.tensor_tensor(rot, misc[:, :].rearrange("p (a t) -> p a t", a=2), sin, ALU.mult))
                    dst = QR[:, 2 * j:2 * j + 2, :] if j < 4 else v
                    link(dve.tensor_tensor(dst, v, cos, ALU.mult))
                    dve.tensor_tensor(dst, dst, rot, ALU.add).then_inc(misc_used, 1)
                state["free"] += 10
                for c, (pe_name, src) in enumerate((("pe_k", KC), ("pe_v", VC))):
                    state["misc"] += 1
                    dve.wait_ge(misc_ready, state["misc"])
                    z4 = zk.rearrange("p l (g n) -> p l g n", g=4)
                    for g in range(4):
                        for par in range(2):
                            rows = slice(par * HD, (par + 1) * HD)
                            tok = up[rows, g // 2, (g % 2) * L:(g % 2 + 1) * L]
                            tok = bass.AP(tok.tensor, tok.offset + par, [list(tok.ap[0]), [2, 16], [16, NCMP]])
                            pe_b = v1(pe_name, 0, 16)[rows].unsqueeze(2).to_broadcast([HD, 16, NCMP])
                            ins = dve.tensor_tensor(z4[rows, :, g, :], tok, pe_b, ALU.add)
                    ins.then_inc(misc_used, 1)
                    if c == 0:
                        state["misc"] += 1
                        dve.wait_ge(misc_ready, state["misc"])
                        dve.tensor_copy(kcmp, misc[:, 0:30]).then_inc(misc_used, 1)
                        dve.wait_ge(misc_used, state["misc"])
                        state["misc"] += 1
                        head_norm(kcmp, 30, "kc_norm", 1.0).then_inc(misc_used, 1)
                    else:
                        state["aux_s"] += 1
                        dve.wait_ge(aux_s, state["aux_s"])
                        hr = hidr.rearrange("p m (g r n) -> p m g r n", g=4, r=4)
                        hc = hidc.rearrange("p m (g n) -> p m g n", g=4)
                        for m in range(2):
                            for g in range(4):
                                ins = dve.tensor_copy(hr[:, m, g, :, 0:NCMP],
                                                      hc[:, m, g, :].unsqueeze(1).to_broadcast([P, 4, NCMP]))
                        ins.then_inc(h_ready, 1)
                        state["misc"] += 1
                        dve.wait_ge(misc_ready, state["misc"])
                        dve.tensor_copy(vcmp.rearrange("p g c -> p (g c)"), misc[:, 0:L]).then_inc(misc_used, 1)
                state["misc"] += 1
                dve.wait_ge(misc_ready, state["misc"])
                p3 = pc.rearrange("p a (h n) -> p a h n", n=32)
                for tt in range(2):
                    add = cs("cmp_add", tt * 32, tt * 32 + NCMP).unsqueeze(1).unsqueeze(1).to_broadcast([P, 2, 4, NCMP])
                    for half in range(2):
                        link(dve.tensor_tensor(
                            p3[:, tt].rearrange("p (a b r) n -> p a b r n", a=2, b=2)[:, :, half, :, 0:NCMP],
                            acc[:, 2 * tt + half, 0:L].rearrange("p (a r n) -> p a r n", a=2, n=32)[:, :, :, 0:NCMP],
                            add, ALU.add))
                    link(dve.tensor_reduce(st32[:, 0, tt * AH:(tt + 1) * AH], p3[:, tt, :, 0:NCMP], AX_X, ALU.max))
                    ins = dve.tensor_tensor(
                        p3[:, tt, :, 0:NCMP], p3[:, tt, :, 0:NCMP],
                        st32[:, 0, tt * AH:(tt + 1) * AH].unsqueeze(2).to_broadcast([P, AH, NCMP]), ALU.subtract)
                    if tt == 0:
                        link(ins)
                ins.then_inc(aux_v, 1)
                state["aux_s"] += 1
                dve.wait_ge(aux_s, state["aux_s"])
                for tt in range(2):
                    one = cs("cmp_one", tt * 32, tt * 32 + 32).unsqueeze(1).to_broadcast([P, AH, 32])
                    link(dve.tensor_tensor(p3[:, tt], p3[:, tt], one, ALU.mult))
                    link(dve.tensor_reduce(st32[:, 0, tt * AH:(tt + 1) * AH], p3[:, tt], AX_X, ALU.add))
                link(dve.tensor_scalar(st32[:, 0, :], st32[:, 0, :], 1e-30, None, ALU.max))
                link(dve.reciprocal(st32[:, 0, :], st32[:, 0, :]))
                g3 = gates.rearrange("p a (h b) -> p a h b", b=NB)[:, :, :, 0]
                link(dve.tensor_tensor(st32[:, 0, :].rearrange("p (a h) -> p a h", a=2),
                                       st32[:, 0, :].rearrange("p (a h) -> p a h", a=2), g3, ALU.mult))
                for tt in range(2):
                    ins = dve.tensor_tensor(
                        p3[:, tt], p3[:, tt],
                        st32[:, 0, tt * AH:(tt + 1) * AH].unsqueeze(2).to_broadcast([P, AH, 32]), ALU.mult)
                ins.then_inc(misc_used, 1)
                state["misc"] += 1
                dve.wait_ge(misc_ready, state["misc"])
                dve.tensor_copy(PC.rearrange("p g t -> p (g t)"),
                                up[:, :, :].rearrange("p a t -> p (a t)")).then_inc(misc_used, 1)
                attention(units_nsa(), UNITS["nsa"])
                update_slots(n0 + 14, 2, "plain")

            dve.memset(ones[:, :], 1.0).then_inc(setup_done, 1)
            dve.memset(eps[:, :], EPS).then_inc(setup_done, 1)
            dve.memset(zeros[:, :], 0.0).then_inc(setup_done, 1)
            dve.wait_ge(cact_ready, 1)
            for i in range(MSLOTS):
                seg, kp = i // 4, i % 4
                dst = modacc[:, 0, seg * D:(seg + 1) * D]
                dve.wait_ge(mod_landed[i % MRING], 16 * (i // MRING + 1))
                for e in range(2):
                    k = 2 * kp + e
                    w = mring[:, i % MRING, e, :]
                    if k == 0:
                        link(dve.tensor_scalar(dst, w, cact[:, k:k + 1], None, ALU.mult))
                        continue
                    ins = dve.scalar_tensor_tensor(out=dst, in0=w, scalar=cact[:, k:k + 1], in1=dst, op0=ALU.mult,
                                                   op1=ALU.add)
                    if e == 1:
                        ins.then_inc(mod_used, 1)
                        dve.wait_ge(mod_used, i + 1)
                    else:
                        link(ins)
            dve.wait_ge(vec_landed, 16)
            dve.wait_ge(con_landed, 16)
            norm(0, 0.5)
            ffn(AT_SLOT["ffn0"])
            norm(1)
            ssm(AT_SLOT["ssm"])
            norm(2, 0.5)
            ffn(AT_SLOT["ffn1"])
            norm(3, 0.5)
            ffn(AT_SLOT["ffn2"])
            norm(4)
            moba(AT_SLOT["moba"])
            norm(5, 0.5)
            ffn(AT_SLOT["ffn3"])
            norm()
            norm()
            conformer(AT_SLOT["conf"])
            norm()
            conv_ffn(AT_SLOT["cffn0"], 0)
            norm()
            nsa(AT_SLOT["nsa"])
            norm()
            conv_ffn(AT_SLOT["cffn1"], 1)


XR = {"end": 10 * KD}
UNITS = {
    "moba": dict(u=0),
    "nsa": dict(u=AH),
    "misc_at_nsa": 3,
    "stat_at_conf": 9,
}


def kernel(x, c, norm_g, mod_w, mod_b, ffn_w_gate, ffn_w_up, ffn_w_down, ssm_w_in, ssm_conv_w, ssm_conv_b,
           ssm_dt_bias, ssm_a_log, ssm_d, ssm_norm_w, ssm_w_out, attn_w_qkv, attn_w_out, final_norm_g,
           mix_norm_g_2, ffn_norm_g_2, conv_w_pw1_2, conv_b_pw1_2, conv_w_dw_2, conv_b_dw_2, conv_ln_g_2,
           conv_ln_b_2, conv_w_pw2_2, conv_b_pw2_2, nsa_w_in_2, nsa_q_norm_2, nsa_kc_norm_2, nsa_ks_norm_2,
           nsa_kw_norm_2, nsa_pe_k_2, nsa_pe_v_2, nsa_ck_w1_2, nsa_ck_w2_2, nsa_cv_w1_2, nsa_cv_w2_2,
           nsa_w_out_2, ffn_w_up_2, ffn_w_dw_2, ffn_b_dw_2, ffn_w_down_2):
    import concourse.bacc as bacc
    from concourse.bass_utils import run_bass_kernel_spmd

    A = np.asarray

    def cols(a):
        a = A(a).reshape(-1, A(a).shape[-1])
        return a.reshape(a.shape[0], -1, P).transpose(2, 0, 1).reshape(P, -1)

    def pad(a):
        out = np.zeros((P, 1), np.float32)
        out[:A(a).size, 0] = A(a).reshape(-1)
        return out

    def twice(a):
        return np.tile(A(a).reshape(-1), 2).reshape(P, 1)

    def pe_pairs(a):
        return A(a).reshape(16, 2, HD).transpose(1, 2, 0).reshape(P, 16)

    vecs = dict(c=cols(c), norm_g=cols(norm_g), mod_b=cols(mod_b), conv_w=cols(A(ssm_conv_w)[0, :, 0]),
                conv_b=cols(ssm_conv_b), dt_bias=pad(ssm_dt_bias), a_log=pad(ssm_a_log),
                ssm_d=cols(np.repeat(A(ssm_d)[0], HD)[None]), ssm_norm=cols(ssm_norm_w),
                final_g=cols(A(final_norm_g)[None]), mix_g=cols(mix_norm_g_2), ffn_g=cols(ffn_norm_g_2),
                b_pw1=cols(conv_b_pw1_2), w_dw=cols(A(conv_w_dw_2)[0]), b_dw=cols(conv_b_dw_2),
                ln_g=cols(conv_ln_g_2), ln_b=cols(conv_ln_b_2), b_pw2=cols(conv_b_pw2_2),
                q_norm=twice(nsa_q_norm_2), kc_norm=twice(nsa_kc_norm_2), ks_norm=twice(nsa_ks_norm_2),
                kw_norm=twice(nsa_kw_norm_2), pe_k=pe_pairs(A(nsa_pe_k_2)[0]), pe_v=pe_pairs(A(nsa_pe_v_2)[0]),
                ffn_dw=cols(ffn_w_dw_2), ffn_db=cols(ffn_b_dw_2))
    vec = np.concatenate([vecs[k] for k in VEC], 1)

    def ktiles(w):
        w = A(w)
        return w.reshape(w.shape[0] // P, P, w.shape[1]).transpose(1, 0, 2)

    w_in = ktiles(ssm_w_in[0])
    nsa_in = ktiles(nsa_w_in_2[0])
    at = np.cumsum([0, 1024] + [256] * 6 + [48])
    small = np.concatenate([w_in[:, :, INNER + 4096:].reshape(P, -1), nsa_in[:, :, at[7]:].reshape(P, -1),
                            ktiles(nsa_ck_w2_2[0]).reshape(P, -1), ktiles(nsa_cv_w2_2[0]).reshape(P, -1)], 1)

    def wide(w, width=L):
        return [w[:, :, j:j + width].reshape(P, -1) for j in range(0, w.shape[2], width)]

    def both(a, b):
        return [np.concatenate([a[:, :, j:j + P], b[:, :, j:j + P]], 2).reshape(P, -1)
                for j in range(0, a.shape[2], P)]

    def feed_forward(a, b, down):
        ups = both(a, b)
        d = ktiles(down)
        downs = [d[:, 2 * p:2 * p + 2, :].reshape(P, -1) for p in range(PAIRS)]
        out = ups[0:2]
        for p in range(1, PAIRS):
            out += [ups[2 * p], ups[2 * p + 1], downs[p - 1]]
        return out + [downs[-1]]

    def swiglu(i, j):
        return feed_forward(ktiles(ffn_w_gate[i, j]), ktiles(ffn_w_up[i, j]), ffn_w_down[i, j])

    def conv_ffn(i):
        w = ktiles(ffn_w_up_2[i])
        return feed_forward(w[:, :, :FF], w[:, :, FF:], ffn_w_down_2[i])

    heads = [(j // 4 * 2 + half) * 4 + j % 4 for j in range(KD) for half in (0, 1)]
    q_cols = np.concatenate([np.arange(h * HD, (h + 1) * HD) for h in heads])
    pw1 = ktiles(conv_w_pw1_2[0])
    stream = {
        "ffn0": swiglu(0, 0),
        "ssm": wide(w_in[:, :, INNER:INNER + 4096]) + wide(w_in[:, :, :INNER]) + wide(ktiles(ssm_w_out[0]), P),
        "ffn1": swiglu(0, 1),
        "ffn2": swiglu(1, 0),
        "moba": wide(ktiles(attn_w_qkv[0])) + wide(ktiles(attn_w_out[0])),
        "ffn3": swiglu(1, 1),
        "conf": both(pw1[:, :, :D], pw1[:, :, D:]) + wide(ktiles(conv_w_pw2_2[0])),
        "cffn0": conv_ffn(0),
        "nsa": wide(nsa_in[:, :, q_cols]) + [nsa_in[:, :, at[i]:at[i + 1]].reshape(P, -1) for i in (3, 5, 1, 2, 4, 6)]
        + wide(ktiles(nsa_ck_w1_2[0]), P) + wide(ktiles(nsa_cv_w1_2[0]), P) + wide(ktiles(A(nsa_w_out_2[0])[q_cols])),
        "cffn1": conv_ffn(1),
    }
    weights = np.stack([s for name, _ in LAYERS for s in stream[name]])
    mods = np.stack([ktiles(w)[:, 2 * kp:2 * kp + 2, seg * D:(seg + 1) * D]
                     for w in A(mod_w).reshape(NMOD, D, 3 * D) for seg in range(3) for kp in range(4)])
    arrays = {"in_x": cols(A(x)[0]).reshape(P, L, KD).transpose(0, 2, 1), "in_vectors": vec, "in_small": small, "in_constants": constants(),
              "in_mods": mods, "in_weights": weights}
    arrays = {k: np.ascontiguousarray(v) for k, v in arrays.items()}

    nc = bacc.Bacc("TRN2", target_bir_lowering=False, num_devices=1)
    args = [nc.dram_tensor(n, a.shape, F32, kind="ExternalInput").ap() for n, a in arrays.items()]
    out = nc.dram_tensor("out", (P, KD, L), F32, kind="ExternalOutput").ap()
    build(nc, *args, out)
    r = run_bass_kernel_spmd(nc, [arrays], core_ids=[0])
    y = r.results[0]["out"]
    return y.transpose(2, 1, 0).reshape(1, L, D)
```

```python
from contextlib import ExitStack

import numpy as np
import concourse.bass as bass
from concourse import mybir

F32 = mybir.dt.float32
BF16 = mybir.dt.bfloat16
F32R = mybir.dt.float32r
ALU = mybir.AluOpType
ACT = mybir.ActivationFunctionType
AX_X = mybir.AxisListType.X

P = 128
L = 256
D = 1024
KD = D // P
FF = 2816
NF = FF // P
PAIRS = NF // 2
INNER = 2048
KI = INNER // P
SH = 32
GRP = 8
HPG = SH // GRP
AH = 16
HD = 64
NB = 3
NCMP = 15
EPS = 1e-6
TRI = L + P
SLOT = 2048
RING = 6
MRING = 3
MPART = 8
MSLOTS = 12
NMOD = 6
FSLOTS = 3 * PAIRS

LAYERS = [("ffn0", FSLOTS), ("ssm", 24 + 8), ("ffn1", FSLOTS), ("ffn2", FSLOTS), ("moba", 12 + 4),
          ("ffn3", FSLOTS), ("conf", 8 + 4), ("cffn0", FSLOTS), ("nsa", 10 + 4 + 4), ("cffn1", FSLOTS)]
AT_SLOT = {}
SLOTS = 0
for _name, _n in LAYERS:
    AT_SLOT[_name] = SLOTS
    SLOTS += _n
assert SLOTS % RING == 0

VEC = {}
NVEC = 0
for _name, _n in [("norm_g", 6 * KD), ("mod_b", 6 * 24), ("conv_w", 4 * 32), ("conv_b", 32),
                  ("dt_bias", 1), ("a_log", 1), ("ssm_d", KI), ("ssm_norm", KI), ("final_g", KD),
                  ("mix_g", 2 * KD), ("ffn_g", 2 * KD), ("b_pw1", 16), ("w_dw", 31 * KD), ("b_dw", KD),
                  ("ln_g", KD), ("ln_b", KD), ("b_pw2", KD), ("q_norm", 1), ("kc_norm", 1), ("ks_norm", 1),
                  ("kw_norm", 1), ("pe_k", 16), ("pe_v", 16), ("ffn_dw", 2 * 3 * NF), ("ffn_db", 2 * NF)]:
    VEC[_name] = NVEC
    NVEC += _n

SMALL = {"w_dt": 0, "w_gl": KD * SH, "ck2": KD * SH + KD * 48, "cv2": KD * SH + KD * 48 + 2 * HD}
NSMALL = KD * SH + KD * 48 + 4 * HD

CON = {}
NCON = 0
for _name, _n in [("ident", P), ("block", P), ("tri", TRI), ("mask_sq", TRI), ("mask_qk", TRI), ("dist", TRI),
                  ("cmp_add", 2 * 32), ("cmp_one", 2 * 32), ("cos", L), ("sin", L), ("rope", P),
                  ("pick0", P), ("pick1", P)]:
    CON[_name] = NCON
    NCON += _n


def constants():
    con = np.zeros((P, NCON), np.float32)

    def put(name, a):
        con[:a.shape[0], CON[name]:CON[name] + a.shape[1]] = a

    i = np.arange(P)
    t = np.arange(L)
    put("ident", np.eye(P))
    put("block", (i[:, None] // HD == i[None, :] // HD).astype(np.float32))
    tri = [(s0 + i[:, None] <= t[None, :]).astype(np.float32) for s0 in (0, P)]
    put("tri", np.concatenate([tri[0], tri[1][:, P:]], 1))
    sq = np.concatenate([1 - tri[0], (1 - tri[1])[:, P:]], 1) * np.float32(-1e30)
    put("mask_sq", sq)
    ok = np.concatenate([i[:, None] >= i[None, :], P + i[:, None] >= t[None, :]], 1)
    put("mask_qk", np.where(ok, 0.0, -1e30))
    dist = np.concatenate([i[None, :] - i[:, None], t[None, :] - (P + i[:, None])], 1)
    put("dist", np.where(ok, dist, -1e30))
    end = np.arange(32) * 16 + 31
    seen = np.concatenate([(end[None, :] <= q0 + i[:, None]) & (np.arange(32) < NCMP)[None, :] for q0 in (0, P)], 1)
    put("cmp_add", np.where(seen, 0.0, -1e30))
    put("cmp_one", seen.astype(np.float32))
    inv = (np.float32(500000.0) ** (-np.arange(8, dtype=np.float32) * np.float32(2.0 / 16))).astype(np.float32)
    ang = (t.astype(np.float32)[None, :] * inv[:, None]).astype(np.float32).astype(np.float64)
    cos, sin, rope = np.ones((P, L)), np.zeros((P, L)), np.zeros((P, P))
    for h in (0, HD):
        for half in (0, 8):
            cos[h + half:h + half + 8] = np.cos(ang)
            sin[h + half:h + half + 8] = np.sin(ang)
        for j in range(8):
            rope[h + 8 + j, h + j] = -1.0
            rope[h + j, h + 8 + j] = 1.0
    put("cos", cos)
    put("sin", sin)
    put("rope", rope)
    for par in (0, 1):
        put(f"pick{par}", (i[:, None] == par * HD + i[None, :] % HD).astype(np.float32))
    return con


class Chain:

    def __init__(self, eng, sem):
        self.eng, self.sem, self.n, self.off = eng, sem, 0, 0

    def link(self, ins):
        ins.then_inc(self.sem, 1)
        self.n += 1
        self.eng.wait_ge(self.sem, self.n + self.off)


def build(nc, x_in, c_in, vec_in, small_in, con_in, mod_in, w_in, out):
    with ExitStack() as ctx:
        def sb(name, shape, dt=F32):
            return ctx.enter_context(nc.sbuf_tensor(name, shape, dt))

        def sem(name):
            return ctx.enter_context(nc.semaphore(name))

        ring = sb("ring", [P, RING, SLOT])
        mring = sb("mring", [P, MRING, 2, D])
        modsum = sb("modsum", [P, 2, 24, MPART])
        vec = sb("vec", [P, NVEC])
        small = sb("small", [P, NSMALL])
        con = sb("con", [P, NCON])
        ones = sb("ones", [P, P])
        eps = sb("eps", [P, 1])
        zeros = sb("zeros", [P, 512], BF16)
        X = sb("X", [P, KD, L])
        h_at = nc.sbuf_base
        H = sb("H", [P, KD, L])
        rstd = sb("rstd", [P, 2 * L])
        rtok = sb("rtok", [P, 2])
        modv = sb("modv", [P, 24])
        modsc = sb("modsc", [P, KD])
        gate = sb("gate", [P, KD])
        modraw = sb("modraw", [P, 24])
        cact = sb("cact", [P, D])
        ARENA = 23000
        arena_at = nc.sbuf_base
        arena = sb("arena", [P, ARENA])

        def part(at, *shape):
            n = int(np.prod(shape))
            assert at + n <= ARENA
            v = arena[:, at:at + n]
            if len(shape) == 2:
                return v.rearrange("p (a b) -> p a b", a=shape[0])
            if len(shape) == 3:
                return v.rearrange("p (a b c) -> p a b c", a=shape[0], b=shape[1])
            return v

        def rounded(name, at, *shape):
            assert at + int(np.prod(shape)) <= ARENA
            return nc.alloc_sbuf_tensor_at(name, [P, *shape], F32R, offset=arena_at + 4 * at)

        act_buf = part(0, 2, L)
        hid_hi = rounded("hid_hi", 2 * L, 4, L)
        hid_lo = rounded("hid_lo", 6 * L, 4, L)
        H_hi = rounded("H_hi", 10 * L, KD, L)
        H_lo = nc.alloc_sbuf_tensor_at("H_lo", [P, KD, L], F32R, offset=h_at)
        SPLIT_AT = [18 * L + 2 * SLOT * i for i in (2, 1, 0)]
        w_hi = [rounded(f"w_hi{i}", a, SLOT) for i, a in enumerate(SPLIT_AT)]
        w_lo = [rounded(f"w_lo{i}", a + SLOT, SLOT) for i, a in enumerate(SPLIT_AT)]
        Z = part(0, KI, L)
        XBC = part(KI * L, 2 * KI, L)
        XT = part(3 * KI * L, 2, INNER)
        at = 4 * KI * L
        Wd = H.rearrange("p k t -> p (k t)")[:, 0:4 * TRI].rearrange("p (b t) -> p b t", b=4)
        Yt = H.rearrange("p k t -> p (k t)")[:, 4 * TRI:4 * TRI + 2 * L].rearrange("p (b t) -> p b t", b=2)
        dtx = part(at, 2, L)
        tri_r = rounded("tri_r", at, TRI)
        dta_hi = rounded("dta_hi", at + TRI, 2, SH)
        dta_lo = rounded("dta_lo", at + TRI + 2 * SH, 2, SH)
        dtT = part(at + 2 * TRI, 4, SH)
        acT = part(at + 2 * TRI + 4 * SH, 2, SH)
        dts = part(at + 2 * TRI + 6 * SH, 2, L)
        negA = modv[0:SH, 0:1]
        Q = part(0, KD, L)
        K = part(2048, KD, L)
        QR = part(2048, KD, L)
        V = part(4096, 2, D)
        O = part(6144, KD, L)
        LAG = 4
        PBUF = LAG + 1
        PT = part(8192, 2, TRI)
        nmax = part(8960, PBUF, 2)
        psum_ = part(8980, PBUF, 2)
        Pb = part(17888, PBUF, TRI)
        KS = part(10130, 2, L)
        KW = part(10642, 2, L)
        KC = part(11154, 2, L)
        VC = part(11666, 2, L)
        gates = part(12178, 2, 48)
        zk = part(12274, 16, 60)
        hidc = part(13234, 2, 60)
        hidr = part(13354, 2, 512)
        kcmp = part(14378, 30)
        vcmp = part(14408, 4, HD)
        pc = part(14664, 2, 512)
        PC = part(15688, 4, L)
        st32 = part(16712, 2, 32)
        sqb = part(16776, 512)
        UP = part(0, KD, 30 + L)
        CV = part(2304, KD, L)
        sgb = part(4352, 2, L)
        TAPS = 8
        taps = part(4864, TAPS, L)

        acc = ctx.enter_context(nc.psum_tensor("acc", [P, 4, 512], F32))
        up = ctx.enter_context(nc.psum_tensor("up", [P, 2, 512], F32))
        stat = ctx.enter_context(nc.psum_tensor("stat", [P, 512], F32))
        misc = ctx.enter_context(nc.psum_tensor("misc", [P, 512], F32))

        def acc_t(m):
            return acc[:, m // 2, (m % 2) * L:(m % 2 + 1) * L]

        def v1(name, col=0, n=1):
            return vec[:, VEC[name] + col:VEC[name] + col + n]

        def cs(name, a, b):
            return con[:, CON[name] + a:CON[name] + b]

        ident = cs("ident", 0, P)

        vec_landed, con_landed, small_landed, x_landed = (sem(s) for s in (
            "vec_landed", "con_landed", "small_landed", "x_landed"))
        slot_landed = [sem(f"slot_landed{i}") for i in range(RING)]
        mod_landed = [sem(f"mod_landed{i}") for i in range(MRING)]
        slot_done = sem("slot_done")
        mod_used = sem("mod_used")
        mod_reduced = sem("mod_reduced")
        modvec_ready = sem("modvec_ready")
        setup_done = sem("setup_done")
        c_landed = sem("c_landed")
        cact_ready = sem("cact_ready")
        x_ready = sem("x_ready")
        down_ready = sem("down_ready")
        sq_ready = sem("sq_ready")
        stat_ready = sem("stat_ready")
        rcp_ready = sem("rcp_ready")
        spread_ready = sem("spread_ready")
        root_ready = sem("root_ready")
        xn_ready = sem("xn_ready")
        h_ready = sem("h_ready")
        pair_free = sem("pair_free")
        silu_ready = sem("silu_ready")
        dwc_ready = sem("dwc_ready")
        hi_ready = sem("hi_ready")
        split_ready = sem("split_ready")
        hid_hi_ready = sem("hid_hi_ready")
        hid_ready = sem("hid_ready")
        presum_ready = sem("presum_ready")
        tap_ready = sem("tap_ready")
        tap_added = sem("tap_added")
        raw_ready = sem("raw_ready")
        misc_ready = sem("misc_ready")
        xt_ready = sem("xt_ready")
        misc_used = sem("misc_used")
        aux_v = sem("aux_v")
        aux_s = sem("aux_s")
        dta_ready = sem("dta_ready")
        bc_ready = sem("bc_ready")
        cb_ready = sem("cb_ready")
        seg_ready = sem("seg_ready")
        exp_ready = sem("exp_ready")
        w_ready = sem("w_ready")
        y_done = sem("y_done")
        y_free = sem("y_free")
        score_ready = sem("score_ready")
        mask_done = sem("mask_done")
        max_ready = sem("max_ready")
        pexp_ready = sem("pexp_ready")
        norm_ready = sem("norm_ready")
        p_ready = sem("p_ready")
        t_done = sem("t_done")
        pt_ready = sem("pt_ready")
        o_done = sem("o_done")
        v_done = sem("v_done")
        s_done = sem("s_done")
        g_done = sem("g_done")
        out_stored = sem("out_stored")

        block = ctx.enter_context(nc.Block())

        CONV_DVE, CONV_POOL, CONV_ORDER = (0, 1, 3, 5, 7), (2, 4, 6), (0, 1, 2, 3, 4, 5, 6, 7)
        GLU_TAPS = 13

        PRE = {KD: 4, KI: KI - 2}

        def hidden_tile(s):
            return s if s < 2 else None if (s - 2) % 3 == 2 else 2 + 2 * ((s - 2) // 3) + (s - 2) % 3

        ROUNDS = (PAIRS - 1) // 2

        NSA_HEADS = [(j // 4 * 2 + half) * 4 + j % 4 for j in range(KD) for half in (0, 1)]

        def units_moba():
            for h in range(AH):
                base = (h % 2) * HD
                yield dict(q=Q, k=K, kt=h // 2, qt=h // 2, base=base, vcol=h * HD, slope=2.0 ** (-8.0 * (h + 1) / AH),
                           gate=None, first=True, last=True, tile=h // 2, cmp=None)

        def units_nsa():
            for n, h in enumerate(NSA_HEADS):
                g = h // 4
                for b, (k, vc) in enumerate(((KS, 0), (KW, 256))):
                    yield dict(q=QR, k=k, kt=g // 2, qt=n // 2, base=(n % 2) * HD, vcol=vc + g * HD, slope=None,
                               gate=h * NB + 1 + b, first=b == 0, last=b == 1, tile=n // 2, cmp=h)

        @block.sync
        def _(sp):
            sp.dma_start(cact[:, :], c_in).then_inc(c_landed, 16)
            sp.dma_start(vec[:, :], vec_in).then_inc(vec_landed, 16)

            def load_mod(n, m, wait):
                if wait is not None:
                    sp.wait_ge(mod_used, wait)
                sp.dma_start(mring[:, n % MRING, :, :], mod_in[m]).then_inc(mod_landed[n % MRING], 16)

            for n in range(MRING):
                load_mod(n, n, None)
            sp.dma_start(X[:, :, :], x_in).then_inc(x_landed, 16)
            sp.dma_start(con[:, :], con_in).then_inc(con_landed, 16)
            for n in range(MRING, MSLOTS):
                load_mod(n, n, n - MRING + 1)
            for j in range(RING):
                sp.dma_start(ring[:, j, :], w_in[j]).then_inc(slot_landed[j], 16)
            sp.dma_start(small[:, :], small_in).then_inc(small_landed, 16)
            MIX = (NMOD - 1) * MSLOTS // MRING
            with sp.Fori(1, MIX + 1) as it:
                for j in range(RING):
                    sp.wait_ge(slot_done, (it - 1) * RING + j + 1)
                    sp.dma_start(ring[:, j, :], w_in[it * RING + j]).then_inc(slot_landed[j], 16)
                for j in range(MRING):
                    load_mod(j, it * MRING + (MSLOTS - MRING) + j, it * MRING + (MSLOTS - 2 * MRING) + j + 1)
            with sp.Fori(MIX + 1, SLOTS // RING) as it:
                for j in range(RING):
                    sp.wait_ge(slot_done, (it - 1) * RING + j + 1)
                    sp.dma_start(ring[:, j, :], w_in[it * RING + j]).then_inc(slot_landed[j], 16)
            sp.wait_ge(x_ready, XR["end"])
            sp.dma_start(out, X[:, :, :]).then_inc(out_stored, 16)
            sp.wait_ge(out_stored, 16)

        @block.gpsimd
        def _(pool):
            order = Chain(pool, g_done)
            pool.wait_ge(mod_used, MSLOTS)
            pool.wait_ge(cact_ready, 1)

            def fold(m, it):
                n0 = m * MSLOTS
                for i in range(MSLOTS):
                    w = mring[:, i % MRING, :, :]
                    pool.wait_ge(mod_landed[i % MRING], 16 * ((n0 + i) // MRING + 1) + it * (16 * 2 * MSLOTS // MRING))
                    order.link(pool.tensor_tensor(w, w, cact[:, :].unsqueeze(1).to_broadcast([P, 2, D]), ALU.mult))
                    half = D // 2
                    while half > MPART:
                        order.link(pool.tensor_tensor(w[:, :, 0:half], w[:, :, 0:half], w[:, :, half:2 * half], ALU.add))
                        half //= 2
                    pool.tensor_tensor(modsum[:, m % 2, 2 * i:2 * i + 2, :], w[:, :, 0:half], w[:, :, half:2 * half],
                                       ALU.add).then_inc(mod_used, 1)
                    pool.wait_ge(mod_used, n0 + i + 1 + it * 2 * MSLOTS)

            fold(1, 0)
            links = order.n
            with pool.Fori(0, 2) as it:
                for m in (2, 3):
                    pool.wait_ge(mod_reduced, it * 2 + m - 1)
                    order.off = it * (2 * links)
                    fold(m, it)
            def attention(units, base):
                for u, a in enumerate(units):
                    b = u % PBUF
                    pool.wait_ge(norm_ready, base["u"] + u + 1)
                    for tt, (c0, c1) in enumerate(((0, P), (P, TRI))):
                        ins = pool.tensor_tensor(Pb[:, b, c0:c1], Pb[:, b, c0:c1],
                                                 psum_[:, b, tt:tt + 1].to_broadcast([P, c1 - c0]), ALU.mult)
                    ins.then_inc(p_ready, 1)

            attention(units_moba(), UNITS["moba"])
            for i, m in enumerate(CONV_POOL):
                pool.wait_ge(tap_ready, 31 * i + 1)
                for tap in range(1, 31):
                    n = 30 * i + tap - 1
                    pool.wait_ge(tap_ready, 31 * i + tap + 1)
                    pool.tensor_tensor(CV[:, m, :], CV[:, m, :], taps[:, n % TAPS, :], ALU.add).then_inc(tap_added, 1)
                    pool.wait_ge(tap_added, n + 1)
            attention(units_nsa(), UNITS["nsa"])

        @block.tensor
        def _(pe):
            state = dict(h=0, free=0, sq=0, misc=0, split=0, hid=0, rcp=0, presum=0, conv=0)
            mm = pe.matmul

            def landed(n, it=0):
                pe.wait_ge(slot_landed[n % RING], 16 * (n // RING + 1) + it * 16)
                return ring[:, n % RING, :]

            def sum_tiles(src, n, presum=True):
                if presum:
                    state["presum"] += 1
                    pe.wait_ge(presum_ready, state["presum"])
                for m in range(n):
                    state["sq"] += 1
                    if presum and 1 <= m < PRE[n]:
                        continue
                    if not presum or m:
                        pe.wait_ge(sq_ready, state["sq"])
                    for tt in range(2):
                        ins = mm(stat[:, tt:tt + 1], src[:, m, tt * P:(tt + 1) * P], ones[:, 0:1],
                                 start=(m == 0 and tt == 0), stop=(m == n - 1), skip_group_check=True)
                ins.then_inc(stat_ready, 1)
                state["rcp"] += 1
                pe.wait_ge(rcp_ready, state["rcp"])
                for tt in range(2):
                    ins = mm(stat[:, L + tt * P:L + (tt + 1) * P], rtok[:, tt:tt + 1].to_broadcast([P, P]), ident,
                             start=(tt == 0), stop=True, skip_group_check=True)
                ins.then_inc(spread_ready, 1)

            def norm(presum=True):
                sum_tiles(H, KD, presum)

            def pair(n, bank, src, it=0, first=False, inc=True):
                w = landed(n, it)
                for k in range(KD):
                    if first:
                        state["h"] += 1
                        pe.wait_ge(h_ready, state["h"])
                    for e in range(2):
                        ins = mm(bank[:, e * L:(e + 1) * L], w[:, k * L + e * P:k * L + (e + 1) * P], src[:, k, :],
                                 start=(k == 0 and e == 0), stop=(k == KD - 1), skip_group_check=True)
                ins.then_inc(slot_done, 1)

            def three(dst, w, cols, x_hi, x_lo, start, stop):
                hi, lo = w_hi[w][:, cols], w_lo[w][:, cols]
                mm(dst, hi, x_hi, start=start, stop=False, skip_group_check=True)
                mm(dst, hi, x_lo, start=False, stop=False, skip_group_check=True)
                return mm(dst, lo, x_hi, start=False, stop=stop, skip_group_check=True)

            def ffn():
                f0, s0 = state["free"], state["split"]
                for b in range(4):
                    mm(acc[:, b, :], zeros[:, 0:P], zeros[:, :], start=True, stop=True, skip_group_check=True)

                def gate_up(s, it=0):
                    f = hidden_tile(s)
                    pe.wait_ge(split_ready, s0 + s + 1 + it * 6)
                    if f >= 2:
                        pe.wait_ge(pair_free, f0 + f - 1 + it * 4)
                    for k in range(KD):
                        if s == 0:
                            state["h"] += 1
                            pe.wait_ge(h_ready, state["h"])
                        for e in range(2):
                            ins = three(up[:, f % 2, e * L:(e + 1) * L], s % 3,
                                        slice(k * L + e * P, k * L + (e + 1) * P), H_hi[:, k, :], H_lo[:, k, :],
                                        start=(k == 0 and e == 0), stop=(k == KD - 1))
                    ins.then_inc(slot_done, 1)

                def down(s, p, it=0, last=False):
                    pe.wait_ge(split_ready, s0 + s + 1 + it * 6)
                    pe.wait_ge(hid_ready, f0h + 2 * p + 2 + it * 4)
                    for m in range(KD):
                        for e in range(2):
                            h = (2 * p + e) % 4
                            ins = three(acc_t(m), s % 3, slice((e * KD + m) * P, (e * KD + m + 1) * P),
                                        hid_hi[:, h, :], hid_lo[:, h, :], start=False, stop=False)
                        if last and m % 2 and m < KD - 1:
                            ins.then_inc(down_ready, 1)
                    ins.then_inc(slot_done, 1)

                f0h = state["hid"]
                gate_up(0)
                gate_up(1)
                with pe.Fori(0, ROUNDS) as it:
                    for s in (2, 5):
                        gate_up(s, it)
                        gate_up(s + 1, it)
                        down(s + 2, (s - 2) // 3, it)
                down(FSLOTS - 1, PAIRS - 1, last=True)
                state["free"] += NF
                state["hid"] += NF
                state["split"] += FSLOTS

            def project_out(n0, src):
                for j in range(4):
                    w = landed(n0 + j)
                    for k in range(KD):
                        if j == 0:
                            state["h"] += 1
                            pe.wait_ge(h_ready, state["h"])
                        for e in range(2):
                            ins = mm(acc[:, j, e * L:(e + 1) * L], w[:, k * L + e * P:k * L + (e + 1) * P],
                                     src[:, k, :], start=(k == 0 and e == 0), stop=(k == KD - 1),
                                     skip_group_check=True)
                    ins.then_inc(slot_done, 1)

            def misc_step(ins):
                ins.then_inc(misc_ready, 1)
                state["misc"] += 1

            def misc_wait():
                pe.wait_ge(misc_used, state["misc"])

            def ssm(n0):
                pe.wait_ge(small_landed, 16)
                wdt = small[:, 0:KD * SH].rearrange("p (k n) -> p k n", k=KD)
                for k in range(KD):
                    state["h"] += 1
                    pe.wait_ge(h_ready, state["h"])
                    ins = mm(misc[0:SH, 0:L], wdt[:, k, :], H[:, k, :], start=(k == 0), stop=(k == KD - 1),
                             skip_group_check=True)
                misc_step(ins)
                f0 = state["free"]
                pair(n0, up[:, 0, :], H)
                pair(n0 + 1, up[:, 1, :], H)
                for n in range(2, RING):
                    pe.wait_ge(pair_free, f0 + n - 1)
                    pair(n0 + n, up[:, n % 2, :], H)
                with pe.Fori(0, 3) as it:
                    for n in range(RING, 2 * RING):
                        pe.wait_ge(pair_free, f0 + n - 1 + it * RING)
                        pair(n0 + n, up[:, n % 2, :], H, it)
                state["free"] += 24
                misc_wait()
                for q in range(2):
                    for tt in range(2):
                        j = 2 * q + tt
                        ins = pe.transpose(misc[:, j * SH:(j + 1) * SH], dts[0:SH, q, tt * P:(tt + 1) * P],
                                           ident[0:SH, 0:SH])
                misc_step(ins)
                misc_wait()
                tri0, tri1 = cs("tri", 0, L), cs("tri", L, TRI)
                mm(misc[:, 0:SH], tri0[:, 0:P], dtT[:, 2, :], start=True, stop=True, skip_group_check=True)
                mm(misc[:, SH:2 * SH], tri0[:, P:L], dtT[:, 2, :], start=True, stop=False, skip_group_check=True)
                misc_step(mm(misc[:, SH:2 * SH], tri1, dtT[:, 3, :], start=False, stop=True,
                             skip_group_check=True))
                pe.wait_ge(pair_free, state["free"])
                for j in range(8):
                    if j >= 2:
                        pe.wait_ge(pair_free, state["free"] - 1)
                    for tt in range(2):
                        for e in range(2):
                            ins = pe.transpose(up[:, j % 2, (2 * tt + e) * P:(2 * tt + e + 1) * P],
                                               XBC[:, 2 * j + e, tt * P:(tt + 1) * P], ident)
                    ins.then_inc(xt_ready, 1)
                    state["free"] += 1
                pe.wait_ge(pair_free, state["free"])

                pe.wait_ge(dta_ready, 1)

                def y(h):
                    pe.wait_ge(w_ready, h + 1)
                    if h % 2 == 0 and h >= 4:
                        pe.wait_ge(y_free, h // 2 - 1)
                    dst = up[(h % 2) * HD:(h % 2 + 1) * HD, (h // 2) % 2, 0:L]
                    mm(dst, XT[:, 0, h * HD:(h + 1) * HD], Wd[:, h % 4, 0:L], start=True, stop=False,
                       skip_group_check=True)
                    mm(dst[:, P:L], XT[:, 1, h * HD:(h + 1) * HD], Wd[:, h % 4, L:TRI], start=False, stop=True,
                       skip_group_check=True).then_inc(y_done, 1)

                for h in range(SH):
                    g = h // HPG
                    if h % HPG == 0:
                        if g >= 2:
                            pe.wait_ge(w_ready, HPG * (g - 1))
                        Bg, Cg = XBC[:, KI + g, :], XBC[:, KI + GRP + g, :]
                        mm(acc[:, 2 + g % 2, 0:L], Bg[:, 0:P], Cg, start=True, stop=True, skip_group_check=True)
                        mm(acc[:, 2 + g % 2, L:TRI], Bg[:, P:L], Cg[:, P:L], start=False, stop=True,
                           skip_group_check=True).then_inc(cb_ready, 1)
                    if h >= 2:
                        pe.wait_ge(seg_ready, h - 1)
                    bc = acc[:, h % 2, :]
                    mm(bc[:, 0:L], dta_hi[:, 0, h:h + 1].to_broadcast([P, P]), tri_r[:, 0:L], start=True, stop=False,
                       skip_group_check=True)
                    mm(bc[:, 0:L], dta_lo[:, 0, h:h + 1].to_broadcast([P, P]), tri_r[:, 0:L], start=False, stop=False,
                       skip_group_check=True)
                    mm(bc[:, P:L], dta_hi[:, 1, h:h + 1].to_broadcast([P, P]), tri_r[:, L:TRI], start=False,
                       stop=False, skip_group_check=True)
                    mm(bc[:, P:L], dta_lo[:, 1, h:h + 1].to_broadcast([P, P]), tri_r[:, L:TRI], start=False,
                       stop=True, skip_group_check=True).then_inc(bc_ready, 1)
                    if h >= 2:
                        y(h - 2)
                y(SH - 2)
                y(SH - 1)
                sum_tiles(XBC, KI)
                for m in range(KD):
                    w = landed(n0 + 24 + m)
                    for k in range(KI):
                        if m == 0:
                            state["h"] += 1
                            pe.wait_ge(h_ready, state["h"])
                        ins = mm(acc_t(m), w[:, k * P:(k + 1) * P], Z[:, k, :], start=(k == 0 and m % 2 == 0),
                                 stop=(k == KI - 1), skip_group_check=True)
                    ins.then_inc(slot_done, 1)

            def value_pairs(n0, count):
                for j in range(count):
                    pe.wait_ge(pair_free, state["free"] - 1)
                    w = landed(n0 + j)
                    for k in range(KD):
                        for tt in range(2):
                            ins = mm(up[:, state["free"] % 2, tt * L:(tt + 1) * L], H[:, k, tt * P:(tt + 1) * P],
                                     w[:, k * L:(k + 1) * L], start=(k == 0 and tt == 0), stop=(k == KD - 1),
                                     skip_group_check=True)
                    ins.then_inc(slot_done, 1)
                    state["free"] += 1

            def pairs(n0, count):
                for j in range(count):
                    if j >= 2:
                        pe.wait_ge(pair_free, state["free"] - 1)
                    pair(n0 + j, up[:, state["free"] % 2, :], H, first=(j == 0))
                    state["free"] += 1

            def attention(units, base):
                units = list(units)
                n = len(units)
                for u in range(n + LAG + 2):
                    if u < n:
                        a = units[u]
                        if u >= 2:
                            pe.wait_ge(mask_done, base["u"] + u - 1)
                        q = a["q"][a["base"]:a["base"] + HD, a["qt"], :]
                        k = a["k"][a["base"]:a["base"] + HD, a["kt"], :]
                        mm(acc[:, u % 2, 0:P], q[:, 0:P], k[:, 0:P], start=True, stop=True, skip_group_check=True)
                        mm(acc[:, u % 2, P:TRI], q[:, P:L], k, start=False, stop=True,
                           skip_group_check=True).then_inc(score_ready, 1)
                    if LAG <= u < n + LAG:
                        t = u - LAG
                        pe.wait_ge(p_ready, base["u"] + t + 1)
                        if t >= 2:
                            pe.wait_ge(pt_ready, base["u"] + t - 1)
                        pb = Pb[:, t % PBUF, :]
                        pe.transpose(acc[:, 2 + t % 2, 0:P], pb[:, 0:P], ident)
                        pe.transpose(acc[:, 2 + t % 2, P:L], pb[:, P:L], ident)
                        pe.transpose(acc[:, 2 + t % 2, L:TRI], pb[:, L:TRI], ident).then_inc(t_done, 1)
                    if u >= LAG + 2:
                        t = u - LAG - 2
                        a = units[t]
                        pe.wait_ge(pt_ready, base["u"] + t + 1)
                        if a["first"] and a["base"] == 0 and a["tile"] >= 2:
                            pe.wait_ge(h_ready, state["h"] + a["tile"] - 1)
                        dst = up[a["base"]:a["base"] + HD, a["tile"] % 2, 0:L]
                        v = a["vcol"]
                        if a["cmp"] is not None and a["first"]:
                            r, g = a["cmp"] % 4, a["cmp"] // 4
                            mm(dst, vcmp[32 * r:32 * r + 32, g, :], PC[32 * r:32 * r + 32, g, :], start=True,
                               stop=False, skip_group_check=True)
                        mm(dst, V[:, 0, v:v + HD], PT[:, t % 2, 0:L], start=(a["first"] and a["cmp"] is None),
                           stop=False, skip_group_check=True)
                        mm(dst[:, P:L], V[:, 1, v:v + HD], PT[:, t % 2, L:TRI], start=False, stop=a["last"],
                           skip_group_check=True).then_inc(o_done, 1)

            def moba(n0):
                pairs(n0, 8)
                value_pairs(n0 + 8, 4)
                pe.wait_ge(pair_free, state["free"])
                attention(units_moba(), UNITS["moba"])
                project_out(n0 + 12, O)

            def conformer(n0):
                pairs(n0, 8)
                sum_tiles_plain(CV)
                sum_tiles(H, KD)
                project_out(n0 + 8, CV)

            def sum_tiles_plain(src):
                for i, m in enumerate(CONV_ORDER):
                    if m in CONV_DVE:
                        state["h"] += 1
                        pe.wait_ge(h_ready, state["h"])
                    else:
                        pe.wait_ge(tap_added, 30 * (CONV_POOL.index(m) + 1))
                    ins = mm(stat[:, 0:L], ones[:, :], src[:, m, :], start=(i == 0), stop=(i == KD - 1),
                             skip_group_check=True)
                ins.then_inc(stat_ready, 1)

            def head_stat(rhs, n):
                misc_wait()
                state["sq"] += 1
                pe.wait_ge(sq_ready, state["sq"])
                misc_step(mm(misc[:, 0:n], cs("block", 0, P), rhs, start=True, stop=True, skip_group_check=True))

            def nsa(n0):
                qk = [(0, Q), (2, Q), (4, Q), (6, Q), (0, KS), (0, KW)]

                def rotate(j):
                    head_stat(sqb[:, 0:512], 512)
                    misc_wait()
                    t0, buf = qk[j]
                    for e in range(2):
                        ins = mm(misc[:, e * L:(e + 1) * L], cs("rope", 0, P), buf[:, t0 + e, :],
                                 start=(e == 0), stop=True, skip_group_check=True)
                    misc_step(ins)

                pe.wait_ge(con_landed, 16)
                wgl = small[:, SMALL["w_gl"]:SMALL["w_gl"] + KD * 48].rearrange("p (k n) -> p k n", k=KD)
                misc_wait()
                for k in range(KD):
                    state["h"] += 1
                    pe.wait_ge(h_ready, state["h"])
                    for tt in range(2):
                        ins = mm(misc[:, tt * 48:(tt + 1) * 48], H[:, k, tt * P:(tt + 1) * P], wgl[:, k, :],
                                 start=(k == 0 and tt == 0), stop=(k == KD - 1), skip_group_check=True)
                misc_step(ins)
                for j in range(8):
                    if j >= 2:
                        pe.wait_ge(pair_free, state["free"] - 1)
                    pair(n0 + j, up[:, state["free"] % 2, :], H)
                    state["free"] += 1
                    if 1 <= j <= 6:
                        rotate(j - 1)
                value_pairs(n0 + 8, 2)
                for c, (src, second) in enumerate(((KC, "ck2"), (VC, "cv2"))):
                    pe.wait_ge(pair_free, state["free"])
                    for g in range(4):
                        ins = mm(up[:, g // 2, (g % 2) * L:(g % 2 + 1) * L], cs(f"pick{g % 2}", 0, P),
                                 src[:, g // 2, :], start=(g % 2 == 0), stop=True, skip_group_check=True)
                    misc_step(ins)
                    misc_wait()
                    for m in range(2):
                        w = landed(n0 + 10 + 2 * c + m)
                        for k in range(16):
                            ins = mm(stat[:, 60 * m:60 * m + 60], w[:, k * P:(k + 1) * P], zk[:, k, :],
                                     start=(k == 0 and m == 0), stop=(k == 15), skip_group_check=True)
                        ins.then_inc(slot_done, 1)
                    w2 = small[:, SMALL[second]:SMALL[second] + 2 * HD].rearrange("p (k n) -> p k n", k=2)
                    state["h"] += 1
                    pe.wait_ge(h_ready, state["h"])
                    if c == 0:
                        hk = hidc.rearrange("p m (a b n) -> p m a b n", a=2, b=2)
                        for par in range(2):
                            for m in range(2):
                                ins = mm(misc[par * HD:(par + 1) * HD, 0:30], w2[:, m, :], hk[:, m, :, par, :],
                                         start=(m == 0), stop=(m == 1), skip_group_check=True)
                        misc_step(ins)
                        head_stat(sqb[:, 0:30], 30)
                    else:
                        misc_wait()
                        for g in range(4):
                            for m in range(2):
                                ins = mm(misc[:, g * HD:(g + 1) * HD], hidr[:, m, g * P:(g + 1) * P], w2[:, m, :],
                                         start=(g == 0 and m == 0), stop=(m == 1), skip_group_check=True)
                        misc_step(ins)
                misc_wait()
                kc3 = kcmp.rearrange("p (a n) -> p a n", a=2)
                for tt in range(2):
                    for base in (0, 1):
                        for j in range(KD):
                            ins = mm(acc[:, 2 * tt + base, j * 32:j * 32 + NCMP],
                                     Q[base * HD:(base + 1) * HD, j, tt * P:(tt + 1) * P],
                                     kc3[base * HD:(base + 1) * HD, j // 4, :], start=(j == 0),
                                     stop=True, skip_group_check=True)
                misc_step(ins)
                misc_wait()
                for g in range(4):
                    for tt in range(2):
                        ins = pe.transpose(up[:, g // 2, ((g % 2) * 2 + tt) * P:((g % 2) * 2 + tt + 1) * P],
                                           pc[:, tt, g * P:(g + 1) * P], ident)
                misc_step(ins)
                misc_wait()
                attention(units_nsa(), UNITS["nsa"])
                project_out(n0 + 14, O)

            pe.wait_ge(setup_done, 3)
            pe.wait_ge(con_landed, 16)
            norm(presum=False)
            ffn()
            norm()
            ssm(AT_SLOT["ssm"])
            norm()
            ffn()
            norm()
            ffn()
            norm()
            moba(AT_SLOT["moba"])
            norm()
            ffn()
            norm()
            state["h"] += KD
            norm()
            conformer(AT_SLOT["conf"])
            norm()
            ffn()
            norm()
            nsa(AT_SLOT["nsa"])
            norm()
            ffn()

        @block.scalar
        def _(act):
            state = dict(x=0, h=0, xn=0, stat=0, free=0, hid=0, silu=0, dwc=0, misc=0, aux_v=0, mod=0)
            order = Chain(act, s_done)

            def root(width):
                state["stat"] += 1
                act.wait_ge(stat_ready, state["stat"])
                act.activation(rtok[:, :], stat[:, 0:2], ACT.Sqrt, scale=1.0 / width,
                               bias=eps[:, 0:1]).then_inc(root_ready, 1)

            def norm(scale, shift=None, mod=False, dest=H, own=False, first=False, parts=False):
                for m in range(KD):
                    if own:
                        act.wait_ge(h_ready, state["h"] - KD + m + 1)
                    elif first:
                        act.wait_ge(x_landed, 16)
                    else:
                        state["x"] += 1
                        act.wait_ge(x_ready, state["x"])
                    act.activation(H[:, m, :], X[:, m, :], ACT.Square).then_inc(sq_ready, 1)
                root(D)
                if mod:
                    state["mod"] += 1
                    act.wait_ge(modvec_ready, state["mod"])
                for m in range(KD):
                    state["xn"] += 1
                    act.wait_ge(xn_ready, state["xn"])
                    if parts and shift is None:
                        ins = act.activation(H_hi[:, m, :], H[:, m, :], ACT.Copy)
                    elif parts:
                        ins = act.activation(H_hi[:, m, :], H[:, m, :], ACT.Identity, bias=shift(m))
                    elif shift is None:
                        ins = act.activation(dest[:, m, :], H[:, m, :], ACT.Copy, scale=scale(m))
                    else:
                        ins = act.activation(dest[:, m, :], H[:, m, :], ACT.Identity, scale=scale(m), bias=shift(m))
                    ins.then_inc(raw_ready if parts else h_ready, 1)
                    state["h"] += 1

            def mod_norm(first=False, parts=False):
                norm(lambda m: modsc[:, m:m + 1], lambda m: modv[:, m:m + 1], mod=True, first=first, parts=parts)

            def high(n0, s, it=0):
                if n0 + s >= 3:
                    act.wait_ge(slot_done, n0 + s - 2 + it * 6)
                n = n0 + s
                act.wait_ge(slot_landed[n % RING], 16 * (n // RING + 1) + it * 16)
                act.activation(w_hi[s % 3][:, :], ring[:, n % RING, :], ACT.Copy).then_inc(hi_ready, 1)

            def ffn(n0, conv=False):
                high(n0, 2)

                def after(s, it):
                    f = hidden_tile(s)
                    if f is not None:
                        a = act_buf[:, f % 2, :]
                        if conv:
                            act.wait_ge(dwc_ready, state["dwc"] + f + 1 + it * 4)
                            act.activation(a, a, ACT.Silu).then_inc(silu_ready, 1)
                        else:
                            act.wait_ge(slot_done, n0 + s + 1 + it * 6)
                            if f >= 2:
                                act.wait_ge(hid_ready, state["hid"] + f - 1 + it * 4)
                            act.activation(a, up[:, f % 2, 0:L], ACT.Silu).then_inc(silu_ready, 1)
                    if s + 3 + 6 * (it if isinstance(it, int) else 0) < FSLOTS:
                        high(n0, s + 3, it)
                    if f is not None:
                        act.wait_ge(pair_free, state["free"] + f + 1 + it * 4)
                        if f >= 2:
                            act.wait_ge(slot_done, n0 + 3 * (f // 2) - 1 + it * 6)
                        act.activation(hid_hi[:, f % 4, :], a, ACT.Copy).then_inc(hid_hi_ready, 1)

                for s in range(2):
                    after(s, 0)
                with act.Fori(0, ROUNDS - 1) as it:
                    for s in range(2, 8):
                        after(s, it)
                for s in range(2, 8):
                    after(s, ROUNDS - 1)
                state["free"] += NF
                state["hid"] += NF
                if conv:
                    state["dwc"] += NF

            def aux_wait():
                state["aux_v"] += 1
                act.wait_ge(aux_v, state["aux_v"])

            def ssm(n0):
                aux_wait()
                act.activation(dts[0:SH, 1, :], dts[0:SH, 1, :], ACT.Exp).then_inc(aux_s, 1)
                act.activation(negA, v1("a_log")[0:SH, :], ACT.Exp).then_inc(aux_s, 1)
                act.wait_ge(aux_s, 2)
                act.activation(dtx[0:SH, 0, :], dts[0:SH, 1, :], ACT.Ln, bias=ones[0:SH, 0:1]).then_inc(aux_s, 1)
                f0 = state["free"]
                with act.Fori(0, 8) as it:
                    for j in range(2):
                        act.wait_ge(pair_free, f0 + 1 + j + it * 2)
                        v = XBC[:, bass.ds(it * 4 + 2 * j, 2), :]
                        act.activation(v, v, ACT.Silu).then_inc(silu_ready, 1)
                with act.Fori(0, 4) as it:
                    for j in range(2):
                        act.wait_ge(slot_done, n0 + 17 + j + it * 2)
                        act.activation(Z[:, bass.ds(it * 4 + 2 * j, 2), :], up[:, j, :].rearrange("p (a t) -> p a t", a=2),
                                       ACT.Silu).then_inc(pair_free, 1)
                state["free"] += 24 + 8
                state["silu"] += 16
                act.wait_ge(misc_used, 1)
                act.activation(tri_r[:, :], cs("tri", 0, TRI), ACT.Copy).then_inc(aux_s, 1)

                def square(m):
                    act.wait_ge(y_free, 0 + m + 1)
                    act.activation(XBC[:, m, :], Z[:, m, :], ACT.Square).then_inc(sq_ready, 1)

                for h in range(SH):
                    act.wait_ge(seg_ready, h + 1)
                    act.activation(Wd[:, h % 4, :], Wd[:, h % 4, :], ACT.Exp).then_inc(exp_ready, 1)
                    if h >= 6 and h % 2 == 0:
                        square((h - 6) // 2)
                for m in range(SH // 2 - 3, SH // 2):
                    square(m)
                root(INNER)

            def attention(units, base):
                units = list(units)
                n = len(units)
                for u in range(n + LAG + 1):
                    if u > LAG:
                        t = u - LAG - 1
                        act.wait_ge(t_done, base["u"] + t + 1)
                        if t >= 2:
                            act.wait_ge(o_done, base["u"] + t - 1)
                        act.activation(PT[:, t % 2, :], acc[:, 2 + t % 2, 0:TRI], ACT.Copy).then_inc(pt_ready, 1)
                    if u < n:
                        act.wait_ge(max_ready, base["u"] + u + 1)
                        b = u % PBUF
                        for tt, (c0, c1) in enumerate(((0, P), (P, TRI))):
                            ins = act.activation(Pb[:, b, c0:c1], Pb[:, b, c0:c1], ACT.Exp, bias=nmax[:, b, tt:tt + 1],
                                                 accum_out=psum_[:, b, tt:tt + 1])
                        ins.then_inc(pexp_ready, 1)

            def evacuate(n, dst, scale=1.0):
                act.wait_ge(slot_done, n + 1)
                act.activation(dst, up[:, state["free"] % 2, :].rearrange("p (a t) -> p a t", a=2), ACT.Copy,
                               scale=scale).then_inc(pair_free, 1)
                state["free"] += 1

            def moba(n0):
                for j in range(4):
                    evacuate(n0 + j, Q[:, 2 * j:2 * j + 2, :], HD ** -0.5)
                for j in range(4):
                    evacuate(n0 + 4 + j, K[:, 2 * j:2 * j + 2, :])
                for j in range(4):
                    evacuate(n0 + 8 + j, V[:, :, j * L:(j + 1) * L])
                attention(units_moba(), UNITS["moba"])
                state["h"] += KD

            def conformer(n0):
                free0 = state["free"]
                todo = [(i, tap) for i in range(len(CONV_POOL)) for tap in range(31)]

                def products(count):
                    for i, tap in todo[:count]:
                        m, n = CONV_POOL[i], 30 * i + tap - 1
                        if tap == 0:
                            act.wait_ge(pair_free, free0 + m + 1)
                            act.activation(CV[:, m, :], UP[:, m, 0:L], ACT.Identity, scale=v1("w_dw", m),
                                           bias=v1("b_dw", m)).then_inc(tap_ready, 1)
                            continue
                        if n >= TAPS:
                            act.wait_ge(tap_added, n - TAPS + 1)
                        act.activation(taps[:, n % TAPS, :], UP[:, m, tap:tap + L], ACT.Copy,
                                       scale=v1("w_dw", tap * KD + m)).then_inc(tap_ready, 1)
                    del todo[:count]

                for m in range(KD):
                    act.wait_ge(slot_done, n0 + m + 1)
                    if m >= 2:
                        act.wait_ge(pair_free, state["free"] - 1)
                    act.activation(sgb[:, m % 2, :], up[:, state["free"] % 2, L:2 * L], ACT.Sigmoid,
                                   bias=v1("b_pw1", KD + m)).then_inc(silu_ready, 1)
                    state["free"] += 1
                    if m >= CONV_POOL[0]:
                        products(12)
                products(len(todo))
                state["h"] += len(CONV_DVE)
                state["stat"] += 1
                for m in range(KD):
                    aux_wait()
                    act.activation(H[:, m, :], CV[:, m, :], ACT.Square).then_inc(sq_ready, 1)
                root(D)
                for m in range(KD):
                    state["xn"] += 1
                    act.wait_ge(xn_ready, state["xn"])
                    act.activation(CV[:, m, :], CV[:, m, :], ACT.Silu, scale=v1("ln_g", m),
                                   bias=v1("ln_b", m)).then_inc(h_ready, 1)
                    state["h"] += 1

            def head_root(n):
                state["misc"] += 1
                act.wait_ge(misc_ready, state["misc"])
                act.activation(rstd[:, 0:n], misc[:, 0:n], ACT.Sqrt, scale=1.0 / HD,
                               bias=eps[:, 0:1]).then_inc(root_ready, 1)

            def nsa(n0):
                base = UNITS["misc_at_nsa"]
                state["misc"] = base + 1
                act.wait_ge(misc_ready, state["misc"])
                act.activation(gates.rearrange("p a b -> p (a b)"), misc[:, 0:96], ACT.Sigmoid).then_inc(misc_used, 1)
                dst = [Q[:, 2 * j:2 * j + 2, :] for j in range(4)] + [KS, KW, KC, VC]
                for j in range(8):
                    if 1 <= j <= 5:
                        act.wait_ge(misc_used, base + 1 + 2 * j)
                    evacuate(n0 + j, dst[j])
                    if j < 6:
                        act.wait_ge(pair_free, state["free"])
                        act.activation(sqb[:, :], dst[j].rearrange("p a t -> p (a t)"), ACT.Square).then_inc(sq_ready, 1)
                        head_root(512)
                        state["misc"] += 1
                for j in range(2):
                    evacuate(n0 + 8 + j, V[:, :, j * L:(j + 1) * L])
                for c in range(2):
                    state["misc"] += 1
                    act.wait_ge(slot_done, n0 + 12 + 2 * c)
                    if c == 0:
                        act.activation(hidc.rearrange("p m n -> p (m n)"), stat[:, 0:120], ACT.Silu).then_inc(h_ready, 1)
                        state["misc"] += 1
                        act.wait_ge(misc_used, state["misc"])
                        act.activation(sqb[:, 0:30], kcmp, ACT.Square).then_inc(sq_ready, 1)
                        head_root(30)
                    else:
                        act.activation(hidc.rearrange("p m n -> p (m n)"), stat[:, 0:120], ACT.Silu).then_inc(aux_s, 1)
                    state["h"] += 1
                aux_wait()
                act.activation(pc, pc, ACT.Exp).then_inc(aux_s, 1)
                attention(units_nsa(), UNITS["nsa"])
                state["h"] += KD

            act.wait_ge(vec_landed, 16)
            act.wait_ge(c_landed, 16)
            act.activation(cact[:, :], cact[:, :], ACT.Silu).then_inc(cact_ready, 1)
            act.wait_ge(setup_done, 3)

            def gated_ffn(name, first=False):
                if not first:
                    high(AT_SLOT[name], 0)
                    high(AT_SLOT[name], 1)
                mod_norm(first=first, parts=True)
                if first:
                    high(AT_SLOT[name], 0)
                    high(AT_SLOT[name], 1)
                ffn(AT_SLOT[name])

            def plain_ffn(name, i):
                high(AT_SLOT[name], 0)
                high(AT_SLOT[name], 1)
                norm(lambda m: v1("ffn_g", i * KD + m), parts=True)
                ffn(AT_SLOT[name], conv=True)

            gated_ffn("ffn0", first=True)
            mod_norm()
            ssm(AT_SLOT["ssm"])
            state["h"] += KI
            gated_ffn("ffn1")
            gated_ffn("ffn2")
            mod_norm()
            moba(AT_SLOT["moba"])
            gated_ffn("ffn3")
            norm(lambda m: v1("final_g", m), dest=X)
            norm(lambda m: v1("mix_g", m), own=True)
            conformer(AT_SLOT["conf"])
            plain_ffn("cffn0", 0)
            norm(lambda m: v1("mix_g", KD + m))
            nsa(AT_SLOT["nsa"])
            plain_ffn("cffn1", 1)

        @block.vector
        def _(dve):
            state = dict(root=0, free=0, silu=0, misc=0, mod=0, down=0, aux_s=3, split=0, hid=0, raw=0, rcp=0, sq=KD,
                         xn=0)
            order = Chain(dve, v_done)
            link = order.link

            def low(n0, s, it=0):
                n = n0 + s
                dve.wait_ge(hi_ready, state["split"] + s + 1 + it * 6)
                dve.tensor_tensor(w_lo[s % 3][:, :], ring[:, n % RING, :], w_hi[s % 3][:, :].bitcast(F32),
                                  ALU.subtract).then_inc(split_ready, 1)

            def add_square(m, buf=H, n=KD):
                if not 1 <= m < PRE[n]:
                    return
                dve.wait_ge(sq_ready, state["sq"] + m + 1)
                ins = dve.tensor_tensor(buf[:, 0, :], buf[:, 0, :], buf[:, m, :], ALU.add)
                if m == PRE[n] - 1:
                    ins.then_inc(presum_ready, 1)
                    state["sq"] += n
                else:
                    link(ins)

            def inverse_root():
                state["root"] += 1
                dve.wait_ge(root_ready, state["root"])
                dve.reciprocal(rtok[:, :], rtok[:, :]).then_inc(rcp_ready, 1)
                state["rcp"] += 1
                dve.wait_ge(spread_ready, state["rcp"])

            def norm(mod=None, half=1.0, parts=False, gain=None, col=0, own=False):
                if own:
                    for m in range(PRE[KD]):
                        add_square(m)
                if mod is not None:
                    state["mod"] += 1
                    if mod:
                        dve.wait_ge(mod_used, MSLOTS * (mod + 1))
                        link(dve.tensor_reduce(modraw[:, :], modsum[:, mod % 2, :, :], AX_X, ALU.add))
                    dve.tensor_tensor(modv[:, :], modraw[:, :], v1("mod_b", mod * 24, 24), ALU.add).then_inc(mod_reduced, 1)
                    dve.wait_ge(mod_reduced, mod + 1)
                    link(dve.tensor_scalar(gate[:, :], modv[:, 16:24], half, None, ALU.mult))
                    dve.scalar_tensor_tensor(out=modsc[:, :], in0=modv[:, 8:16], scalar=1.0,
                                             in1=v1("norm_g", mod * KD, KD), op0=ALU.add,
                                             op1=ALU.mult).then_inc(modvec_ready, 1)
                inverse_root()
                if mod is not None:
                    dve.wait_ge(modvec_ready, state["mod"])
                if not parts:
                    for m in range(KD):
                        dve.tensor_tensor(H[:, m, :], X[:, m, :], stat[:, L:2 * L], ALU.mult).then_inc(xn_ready, 1)
                    return

                def scaled(m):
                    sc = v1(gain, col + m) if gain else modsc[:, m:m + 1]
                    dve.scalar_tensor_tensor(out=H[:, m, :], in0=X[:, m, :], scalar=sc, in1=stat[:, L:2 * L],
                                             op0=ALU.mult, op1=ALU.mult).then_inc(xn_ready, 1)

                scaled(0)
                scaled(1)
                for m in range(KD):
                    state["raw"] += 1
                    dve.wait_ge(raw_ready, state["raw"])
                    if gain:
                        ins = dve.tensor_tensor(H_lo[:, m, :], H[:, m, :], H_hi[:, m, :].bitcast(F32), ALU.subtract)
                    else:
                        ins = dve.scalar_tensor_tensor(out=H_lo[:, m, :], in0=H[:, m, :], scalar=modv[:, m:m + 1],
                                                       in1=H_hi[:, m, :].bitcast(F32), op0=ALU.add, op1=ALU.subtract)
                    ins.then_inc(h_ready, 1)
                    if m + 2 < KD:
                        scaled(m + 2)

            def update(m, how):
                if how == "gate":
                    ins = dve.scalar_tensor_tensor(out=X[:, m, :], in0=acc_t(m), scalar=gate[:, m:m + 1],
                                                   in1=X[:, m, :], op0=ALU.mult, op1=ALU.add)
                elif how == "bias":
                    ins = dve.scalar_tensor_tensor(out=X[:, m, :], in0=acc_t(m), scalar=v1("b_pw2", m),
                                                   in1=X[:, m, :], op0=ALU.add, op1=ALU.add)
                else:
                    ins = dve.tensor_tensor(X[:, m, :], acc_t(m), X[:, m, :], ALU.add)
                ins.then_inc(x_ready, 1)

            def update_ffn(n0, how, then=None, square=True):
                if then is not None:
                    low(then, 0)
                    low(then, 1)
                for m in range(KD):
                    if m < KD - 2 and m % 2 == 0:
                        state["down"] += 1
                        dve.wait_ge(down_ready, state["down"])
                    elif m == KD - 2:
                        dve.wait_ge(slot_done, n0 + FSLOTS)
                    update(m, how)
                    if m >= 2 and square:
                        add_square(m - 2)

            def update_slots(n0, per, how):
                for m in range(KD):
                    if m % 2 == 0:
                        dve.wait_ge(slot_done, n0 + (m + 2) // per)
                    update(m, how)
                    if m >= 2:
                        add_square(m - 2)
                    if m in (3, 5):
                        low(n0 + KD // per, (m - 3) // 2)

            def ffn(n0, i=None, then=None):
                low(n0, 2)
                links = 0 if i is None else 8

                def after(s, it):
                    f = hidden_tile(s)
                    if f is not None:
                        o, a = act_buf[:, f % 2, :], up[:, f % 2, 0:L]
                        if i is not None:
                            def col(name, c):
                                if f < 2:
                                    return v1(name, c + f)
                                return vec[:, bass.ds(it * 4 + (VEC[name] + c + f), 1)]

                            if f >= 2:
                                dve.wait_ge(hid_ready, state["hid"] + f - 1 + it * 4)
                            dve.wait_ge(slot_done, n0 + s + 1 + it * 6)
                            w = [col("ffn_dw", (3 * i + j) * NF) for j in range(3)]
                            link(dve.tensor_scalar(o, a, w[2], col("ffn_db", i * NF), ALU.mult, ALU.add))
                            link(dve.scalar_tensor_tensor(out=o[:, 1:L], in0=a[:, 0:L - 1], scalar=w[1],
                                                          in1=o[:, 1:L], op0=ALU.mult, op1=ALU.add))
                            dve.scalar_tensor_tensor(out=o[:, 2:L], in0=a[:, 0:L - 2], scalar=w[0], in1=o[:, 2:L],
                                                     op0=ALU.mult, op1=ALU.add).then_inc(dwc_ready, 1)
                        dve.wait_ge(silu_ready, state["silu"] + f + 1 + it * 4)
                        dve.tensor_tensor(o, o, up[:, f % 2, L:2 * L], ALU.mult).then_inc(pair_free, 1)
                    if s + 3 + 6 * (it if isinstance(it, int) else 0) < FSLOTS:
                        low(n0, s + 3, it)
                    if f is not None:
                        dve.wait_ge(hid_hi_ready, state["hid"] + f + 1 + it * 4)
                        dve.tensor_tensor(hid_lo[:, f % 4, :], o, hid_hi[:, f % 4, :].bitcast(F32),
                                          ALU.subtract).then_inc(hid_ready, 1)

                for s in range(2):
                    after(s, 0)
                before = order.n
                with dve.Fori(0, ROUNDS - 1) as it:
                    if links:
                        order.off = it * links
                    for s in range(2, 8):
                        after(s, it)
                assert order.n - before == links
                order.n, order.off = before + links * (ROUNDS - 1), 0
                for s in range(2, 8):
                    after(s, ROUNDS - 1)
                state["silu"] += NF
                state["free"] += NF
                state["hid"] += NF
                state["split"] += FSLOTS
                update_ffn(n0, "gate" if i is None else "plain", then, square=i != 1)

            def misc_wait():
                state["misc"] += 1
                dve.wait_ge(misc_ready, state["misc"])

            def ssm(n0):
                misc_wait()
                v, e, lnu = dts[0:SH, 0, :], dts[0:SH, 1, :], dtx[0:SH, 0, :]
                u, dt = dtx[0:SH, 1, :], dts[0:SH, 0, :]
                link(dve.tensor_scalar(v, misc[0:SH, 0:L], v1("dt_bias")[0:SH, :], None, ALU.add))
                dve.scalar_tensor_tensor(out=e, in0=v, scalar=-1.0, in1=v, op0=ALU.mult,
                                         op1=ALU.min).then_inc(aux_v, 1)
                dve.wait_ge(aux_s, 3)
                link(dve.tensor_scalar(u, e, 1.0, -1.0, ALU.add, ALU.add))
                link(dve.tensor_tensor(lnu, lnu, e, ALU.mult))
                link(dve.scalar_tensor_tensor(out=e, in0=u, scalar=0.0, in1=e, op0=ALU.is_equal, op1=ALU.mult))
                link(dve.tensor_scalar(u, u, 1e-30, None, ALU.max))
                link(dve.reciprocal(u, u))
                link(dve.tensor_tensor(lnu, lnu, u, ALU.mult))
                link(dve.tensor_tensor(lnu, lnu, e, ALU.add))
                link(dve.scalar_tensor_tensor(out=dt, in0=v, scalar=0.0, in1=lnu, op0=ALU.max, op1=ALU.add))
                link(dve.tensor_scalar(negA, negA, -1.0, None, ALU.mult))
                dve.tensor_scalar(e, dt, negA, None, ALU.mult).then_inc(misc_used, 1)
                per = 14
                before = order.n
                with dve.Fori(0, 8) as it:
                    for j in range(2):
                        dve.wait_ge(slot_done, n0 + 1 + j + it * 2)
                        order.off = it * per
                        for tap in range(4):
                            for t in range(2):
                                c = it * 4 + 2 * j + t
                                a = up[:, j, t * L:(t + 1) * L]
                                o = XBC[:, bass.ds(c, 1), :].rearrange("p a t -> p (a t)")
                                w = vec[:, bass.ds(c + (VEC["conv_w"] + (3 - tap) * 32), 1)]
                                if tap == 0:
                                    ins = dve.tensor_scalar(o, a, w, vec[:, bass.ds(c + VEC["conv_b"], 1)],
                                                            ALU.mult, ALU.add)
                                else:
                                    ins = dve.scalar_tensor_tensor(out=o[:, tap:L], in0=a[:, 0:L - tap], scalar=w,
                                                                   in1=o[:, tap:L], op0=ALU.mult, op1=ALU.add)
                                if tap == 3 and t == 1:
                                    ins.then_inc(pair_free, 1)
                                else:
                                    link(ins)
                assert order.n - before == per
                order.n, order.off = before + per * 8, 0
                state["free"] += 24
                state["silu"] += 16
                misc_wait()
                dve.tensor_copy(dtT.rearrange("p a h -> p (a h)"), misc[:, 0:4 * SH]).then_inc(misc_used, 1)
                dve.wait_ge(misc_used, 2)
                misc_wait()
                dve.tensor_copy(acT.rearrange("p a h -> p (a h)"), misc[:, 0:2 * SH]).then_inc(misc_used, 1)
                dve.wait_ge(misc_used, 3)
                state["aux_s"] += 1
                dve.wait_ge(aux_s, state["aux_s"])
                link(dve.tensor_copy(dta_hi[:, :, :], dtT[:, 2:4, :]))
                dve.tensor_tensor(dta_lo[:, :, :], dtT[:, 2:4, :], dta_hi[:, :, :].bitcast(F32),
                                  ALU.subtract).then_inc(dta_ready, 1)
                for j in range(8):
                    dve.wait_ge(xt_ready, j + 1)
                    dve.tensor_tensor(
                        XT[:, :, j * L:(j + 1) * L].rearrange("p a (h c) -> p a h c", c=HD),
                        up[:, j % 2, :].rearrange("p (a h c) -> p a h c", a=2, c=HD),
                        dtT[:, 0:2, 4 * j:4 * j + 4].unsqueeze(3).to_broadcast([P, 2, 4, HD]),
                        ALU.mult).then_inc(pair_free, 1)
                state["free"] += 8

                def weight(h):
                    dve.wait_ge(exp_ready, h + 1)
                    if h % HPG == 0:
                        dve.wait_ge(cb_ready, h // HPG + 1)
                    dve.tensor_tensor(Wd[:, h % 4, :], Wd[:, h % 4, :], acc[:, 2 + (h // HPG) % 2, 0:TRI],
                                      ALU.mult).then_inc(w_ready, 1)

                def gated(m):
                    dve.wait_ge(y_done, 2 * m + 2)
                    link(dve.scalar_tensor_tensor(out=Yt[:, m % 2, :], in0=XBC[:, m, :], scalar=v1("ssm_d", m),
                                                  in1=up[:, m % 2, 0:L], op0=ALU.mult, op1=ALU.add))
                    dve.tensor_tensor(Z[:, m, :], Z[:, m, :], Yt[:, m % 2, :], ALU.mult).then_inc(y_free, 1)

                for h in range(SH):
                    dve.wait_ge(bc_ready, h + 1)
                    if h >= 4:
                        dve.wait_ge(y_done, h - 3)
                    dve.scalar_tensor_tensor(out=Wd[:, h % 4, 0:L], in0=acc[:, h % 2, 0:L], scalar=acT[:, 0, h:h + 1],
                                             in1=cs("mask_sq", 0, L), op0=ALU.subtract, op1=ALU.add)
                    dve.scalar_tensor_tensor(out=Wd[:, h % 4, L:TRI], in0=acc[:, h % 2, P:L],
                                             scalar=acT[:, 1, h:h + 1], in1=cs("mask_sq", L, TRI), op0=ALU.subtract,
                                             op1=ALU.add).then_inc(seg_ready, 1)
                    if h >= 1:
                        weight(h - 1)
                    if h >= 5 and h % 2:
                        gated((h - 5) // 2)
                    if h >= 9 and h % 2:
                        add_square((h - 9) // 2, XBC, KI)
                weight(SH - 1)
                for m in (KI - 2, KI - 1):
                    gated(m)
                    add_square(m - 2, XBC, KI)
                inverse_root()
                for m in range(KI):
                    dve.scalar_tensor_tensor(out=Z[:, m, :], in0=Z[:, m, :], scalar=v1("ssm_norm", m),
                                             in1=stat[:, L:2 * L], op0=ALU.mult, op1=ALU.mult).then_inc(h_ready, 1)
                update_slots(n0 + 24, 1, "gate")

            def attention(units, base):
                units = list(units)
                n = len(units)

                def normalise(t):
                    a, b = units[t], t % PBUF
                    dve.wait_ge(pexp_ready, base["u"] + t + 1)
                    ins = dve.reciprocal(psum_[:, b, :], psum_[:, b, :])
                    if a["gate"] is not None:
                        link(ins)
                        ins = dve.tensor_tensor(psum_[:, b, :], psum_[:, b, :], gates[:, :, a["gate"]], ALU.mult)
                    ins.then_inc(norm_ready, 1)

                def take(t):
                    a = units[t]
                    if a["last"] and a["base"] == HD:
                        dve.wait_ge(o_done, base["u"] + t + 1)
                        dve.tensor_copy(O[:, a["tile"], :], up[:, a["tile"] % 2, 0:L]).then_inc(h_ready, 1)

                for u in range(n + LAG + 3):
                    if u < n:
                        a, b = units[u], u % PBUF
                        dve.wait_ge(score_ready, base["u"] + u + 1)
                        if u >= PBUF:
                            dve.wait_ge(t_done, base["u"] + u - PBUF + 1)
                        if a["slope"] is not None:
                            dve.scalar_tensor_tensor(out=Pb[:, b, :], in0=cs("dist", 0, TRI), scalar=a["slope"],
                                                     in1=acc[:, u % 2, 0:TRI], op0=ALU.mult,
                                                     op1=ALU.add).then_inc(mask_done, 1)
                        else:
                            dve.tensor_tensor(Pb[:, b, :], acc[:, u % 2, 0:TRI], cs("mask_qk", 0, TRI),
                                              ALU.add).then_inc(mask_done, 1)
                        dve.wait_ge(mask_done, base["u"] + u + 1)
                        dve.tensor_reduce(nmax[:, b, 0:1], Pb[:, b, 0:P], AX_X, ALU.max, negate=True)
                        dve.tensor_reduce(nmax[:, b, 1:2], Pb[:, b, P:TRI], AX_X, ALU.max,
                                          negate=True).then_inc(max_ready, 1)
                    if 1 <= u <= n:
                        normalise(u - 1)
                    if u >= LAG + 3:
                        take(u - LAG - 3)

            def moba(n0):
                state["free"] += 12
                attention(units_moba(), UNITS["moba"])
                update_slots(n0 + 12, 2, "gate")

            def conformer(n0):
                link(dve.memset(UP[:, :, 0:30], 0.0))
                free0 = state["free"]

                def glu():
                    m = state["free"] - free0
                    state["silu"] += 1
                    dve.wait_ge(silu_ready, state["silu"])
                    dve.scalar_tensor_tensor(out=UP[:, m, 30:30 + L], in0=up[:, state["free"] % 2, 0:L],
                                             scalar=v1("b_pw1", m), in1=sgb[:, m % 2, :], op0=ALU.add,
                                             op1=ALU.mult).then_inc(pair_free, 1)
                    state["free"] += 1

                done = 0
                for m in CONV_DVE:
                    for tap in range(31):
                        while state["free"] - free0 < KD and (state["free"] - free0 <= m
                                                              or done >= GLU_TAPS * (state["free"] - free0)):
                            glu()
                        done += 1
                        if tap == 0:
                            dve.wait_ge(pair_free, free0 + m + 1)
                            ins = dve.tensor_scalar(CV[:, m, :], UP[:, m, 0:L], v1("w_dw", m), v1("b_dw", m), ALU.mult,
                                                    ALU.add)
                        else:
                            ins = dve.scalar_tensor_tensor(out=CV[:, m, :], in0=UP[:, m, tap:tap + L],
                                                           scalar=v1("w_dw", tap * KD + m), in1=CV[:, m, :],
                                                           op0=ALU.mult, op1=ALU.add)
                        if tap < 30:
                            link(ins)
                        else:
                            ins.then_inc(h_ready, 1)
                state["stat"] = UNITS["stat_at_conf"] + 1
                dve.wait_ge(stat_ready, state["stat"])
                link(dve.tensor_scalar(rstd[:, L:2 * L], stat[:, 0:L], 1.0 / D, None, ALU.mult))
                for m in range(KD):
                    dve.tensor_tensor(CV[:, m, :], CV[:, m, :], rstd[:, L:2 * L], ALU.subtract).then_inc(aux_v, 1)
                    if m >= 2:
                        add_square(m - 2)
                inverse_root()
                for m in range(KD):
                    dve.tensor_tensor(CV[:, m, :], CV[:, m, :], stat[:, L:2 * L], ALU.mult).then_inc(xn_ready, 1)
                update_slots(n0 + 8, 2, "bias")

            def head_norm(v, n, g, scale):
                state["root"] += 1
                dve.wait_ge(root_ready, state["root"])
                link(dve.reciprocal(rstd[:, 0:n], rstd[:, 0:n]))
                link(dve.tensor_scalar(rstd[:, 0:n], rstd[:, 0:n], v1(g), scale, ALU.mult, ALU.mult))
                return dve.tensor_tensor(v, v, rstd[:, 0:n], ALU.mult)

            def nsa(n0):
                state["misc"] = UNITS["misc_at_nsa"] + 1
                state["sq"] += 7
                link(dve.memset(pc, 0.0))
                link(dve.memset(hidr, 0.0))
                gains = ["q_norm"] * 4 + ["ks_norm", "kw_norm"]
                cos = cs("cos", 0, L).unsqueeze(1).to_broadcast([P, 2, L])
                sin = cs("sin", 0, L).unsqueeze(1).to_broadcast([P, 2, L])
                for j in range(6):
                    v = Q[:, 2 * j:2 * j + 2, :] if j < 4 else (KS, KW)[j - 4]
                    state["misc"] += 1
                    head_norm(v.rearrange("p a t -> p (a t)"), 512, gains[j],
                              HD ** -0.5 if j < 4 else 1.0).then_inc(misc_used, 1)
                    state["misc"] += 1
                    dve.wait_ge(misc_ready, state["misc"])
                    rot = rstd[:, :].rearrange("p (a t) -> p a t", a=2)
                    link(dve.tensor_tensor(rot, misc[:, :].rearrange("p (a t) -> p a t", a=2), sin, ALU.mult))
                    dst = QR[:, 2 * j:2 * j + 2, :] if j < 4 else v
                    link(dve.tensor_tensor(dst, v, cos, ALU.mult))
                    dve.tensor_tensor(dst, dst, rot, ALU.add).then_inc(misc_used, 1)
                state["free"] += 10
                for c, (pe_name, src) in enumerate((("pe_k", KC), ("pe_v", VC))):
                    state["misc"] += 1
                    dve.wait_ge(misc_ready, state["misc"])
                    z4 = zk.rearrange("p l (g n) -> p l g n", g=4)
                    for g in range(4):
                        for par in range(2):
                            rows = slice(par * HD, (par + 1) * HD)
                            tok = up[rows, g // 2, (g % 2) * L:(g % 2 + 1) * L]
                            tok = bass.AP(tok.tensor, tok.offset + par, [list(tok.ap[0]), [2, 16], [16, NCMP]])
                            pe_b = v1(pe_name, 0, 16)[rows].unsqueeze(2).to_broadcast([HD, 16, NCMP])
                            ins = dve.tensor_tensor(z4[rows, :, g, :], tok, pe_b, ALU.add)
                    ins.then_inc(misc_used, 1)
                    if c == 0:
                        state["misc"] += 1
                        dve.wait_ge(misc_ready, state["misc"])
                        dve.tensor_copy(kcmp, misc[:, 0:30]).then_inc(misc_used, 1)
                        dve.wait_ge(misc_used, state["misc"])
                        state["misc"] += 1
                        head_norm(kcmp, 30, "kc_norm", 1.0).then_inc(misc_used, 1)
                    else:
                        state["aux_s"] += 1
                        dve.wait_ge(aux_s, state["aux_s"])
                        hr = hidr.rearrange("p m (g r n) -> p m g r n", g=4, r=4)
                        hc = hidc.rearrange("p m (g n) -> p m g n", g=4)
                        for m in range(2):
                            for g in range(4):
                                ins = dve.tensor_copy(hr[:, m, g, :, 0:NCMP],
                                                      hc[:, m, g, :].unsqueeze(1).to_broadcast([P, 4, NCMP]))
                        ins.then_inc(h_ready, 1)
                        state["misc"] += 1
                        dve.wait_ge(misc_ready, state["misc"])
                        dve.tensor_copy(vcmp.rearrange("p g c -> p (g c)"), misc[:, 0:L]).then_inc(misc_used, 1)
                state["misc"] += 1
                dve.wait_ge(misc_ready, state["misc"])
                p3 = pc.rearrange("p a (h n) -> p a h n", n=32)
                for tt in range(2):
                    add = cs("cmp_add", tt * 32, tt * 32 + NCMP).unsqueeze(1).unsqueeze(1).to_broadcast([P, 2, 4, NCMP])
                    for half in range(2):
                        link(dve.tensor_tensor(
                            p3[:, tt].rearrange("p (a b r) n -> p a b r n", a=2, b=2)[:, :, half, :, 0:NCMP],
                            acc[:, 2 * tt + half, 0:L].rearrange("p (a r n) -> p a r n", a=2, n=32)[:, :, :, 0:NCMP],
                            add, ALU.add))
                    link(dve.tensor_reduce(st32[:, 0, tt * AH:(tt + 1) * AH], p3[:, tt, :, 0:NCMP], AX_X, ALU.max))
                    ins = dve.tensor_tensor(
                        p3[:, tt, :, 0:NCMP], p3[:, tt, :, 0:NCMP],
                        st32[:, 0, tt * AH:(tt + 1) * AH].unsqueeze(2).to_broadcast([P, AH, NCMP]), ALU.subtract)
                    if tt == 0:
                        link(ins)
                ins.then_inc(aux_v, 1)
                state["aux_s"] += 1
                dve.wait_ge(aux_s, state["aux_s"])
                for tt in range(2):
                    one = cs("cmp_one", tt * 32, tt * 32 + 32).unsqueeze(1).to_broadcast([P, AH, 32])
                    link(dve.tensor_tensor(p3[:, tt], p3[:, tt], one, ALU.mult))
                    link(dve.tensor_reduce(st32[:, 0, tt * AH:(tt + 1) * AH], p3[:, tt], AX_X, ALU.add))
                link(dve.tensor_scalar(st32[:, 0, :], st32[:, 0, :], 1e-30, None, ALU.max))
                link(dve.reciprocal(st32[:, 0, :], st32[:, 0, :]))
                g3 = gates.rearrange("p a (h b) -> p a h b", b=NB)[:, :, :, 0]
                link(dve.tensor_tensor(st32[:, 0, :].rearrange("p (a h) -> p a h", a=2),
                                       st32[:, 0, :].rearrange("p (a h) -> p a h", a=2), g3, ALU.mult))
                for tt in range(2):
                    ins = dve.tensor_tensor(
                        p3[:, tt], p3[:, tt],
                        st32[:, 0, tt * AH:(tt + 1) * AH].unsqueeze(2).to_broadcast([P, AH, 32]), ALU.mult)
                ins.then_inc(misc_used, 1)
                state["misc"] += 1
                dve.wait_ge(misc_ready, state["misc"])
                dve.tensor_copy(PC.rearrange("p g t -> p (g t)"),
                                up[:, :, :].rearrange("p a t -> p (a t)")).then_inc(misc_used, 1)
                attention(units_nsa(), UNITS["nsa"])
                update_slots(n0 + 14, 2, "plain")

            dve.memset(ones[:, :], 1.0).then_inc(setup_done, 1)
            dve.memset(eps[:, :], EPS).then_inc(setup_done, 1)
            dve.memset(zeros[:, :], 0.0).then_inc(setup_done, 1)
            dve.wait_ge(cact_ready, 1)
            for i in range(MSLOTS):
                dve.wait_ge(mod_landed[i % MRING], 16 * (i // MRING + 1))
                for e in range(2):
                    w = mring[:, i % MRING, e, :]
                    ins = dve.scalar_tensor_tensor(out=w, in0=w, scalar=1.0, in1=cact[:, :], op0=ALU.mult, op1=ALU.mult,
                                                   accum_out=modraw[:, 2 * i + e:2 * i + e + 1])
                ins.then_inc(mod_used, 1)
            dve.wait_ge(mod_used, MSLOTS)
            dve.wait_ge(vec_landed, 16)
            dve.wait_ge(con_landed, 16)
            norm(0, 0.5, parts=True)
            low(0, 0)
            low(0, 1)
            ffn(AT_SLOT["ffn0"])
            norm(1)
            ssm(AT_SLOT["ssm"])
            norm(2, 0.5, parts=True)
            ffn(AT_SLOT["ffn1"], then=AT_SLOT["ffn2"])
            norm(3, 0.5, parts=True)
            ffn(AT_SLOT["ffn2"])
            norm(4)
            moba(AT_SLOT["moba"])
            norm(5, 0.5, parts=True)
            ffn(AT_SLOT["ffn3"])
            norm()
            norm(own=True)
            conformer(AT_SLOT["conf"])
            norm(parts=True, gain="ffn_g")
            ffn(AT_SLOT["cffn0"], i=0)
            norm()
            nsa(AT_SLOT["nsa"])
            norm(parts=True, gain="ffn_g", col=KD)
            ffn(AT_SLOT["cffn1"], i=1)


XR = {"end": 10 * KD}
UNITS = {
    "moba": dict(u=0),
    "nsa": dict(u=AH),
    "misc_at_nsa": 3,
    "stat_at_conf": 9,
}


def kernel(x, c, norm_g, mod_w, mod_b, ffn_w_gate, ffn_w_up, ffn_w_down, ssm_w_in, ssm_conv_w, ssm_conv_b,
           ssm_dt_bias, ssm_a_log, ssm_d, ssm_norm_w, ssm_w_out, attn_w_qkv, attn_w_out, final_norm_g,
           mix_norm_g_2, ffn_norm_g_2, conv_w_pw1_2, conv_b_pw1_2, conv_w_dw_2, conv_b_dw_2, conv_ln_g_2,
           conv_ln_b_2, conv_w_pw2_2, conv_b_pw2_2, nsa_w_in_2, nsa_q_norm_2, nsa_kc_norm_2, nsa_ks_norm_2,
           nsa_kw_norm_2, nsa_pe_k_2, nsa_pe_v_2, nsa_ck_w1_2, nsa_ck_w2_2, nsa_cv_w1_2, nsa_cv_w2_2,
           nsa_w_out_2, ffn_w_up_2, ffn_w_dw_2, ffn_b_dw_2, ffn_w_down_2):
    import concourse.bacc as bacc
    from concourse.bass_utils import run_bass_kernel_spmd

    A = np.asarray

    def cols(a):
        a = A(a).reshape(-1, A(a).shape[-1])
        return a.reshape(a.shape[0], -1, P).transpose(2, 0, 1).reshape(P, -1)

    def pad(a):
        out = np.zeros((P, 1), np.float32)
        out[:A(a).size, 0] = A(a).reshape(-1)
        return out

    def twice(a):
        return np.tile(A(a).reshape(-1), 2).reshape(P, 1)

    def pe_pairs(a):
        return A(a).reshape(16, 2, HD).transpose(1, 2, 0).reshape(P, 16)

    vecs = dict(norm_g=cols(norm_g), mod_b=cols(mod_b), conv_w=cols(A(ssm_conv_w)[0, :, 0]),
                conv_b=cols(ssm_conv_b), dt_bias=pad(ssm_dt_bias), a_log=pad(ssm_a_log),
                ssm_d=cols(np.repeat(A(ssm_d)[0], HD)[None]), ssm_norm=cols(ssm_norm_w),
                final_g=cols(A(final_norm_g)[None]), mix_g=cols(mix_norm_g_2), ffn_g=cols(ffn_norm_g_2),
                b_pw1=cols(conv_b_pw1_2), w_dw=cols(A(conv_w_dw_2)[0]), b_dw=cols(conv_b_dw_2),
                ln_g=cols(conv_ln_g_2), ln_b=cols(conv_ln_b_2), b_pw2=cols(conv_b_pw2_2),
                q_norm=twice(nsa_q_norm_2), kc_norm=twice(nsa_kc_norm_2), ks_norm=twice(nsa_ks_norm_2),
                kw_norm=twice(nsa_kw_norm_2), pe_k=pe_pairs(A(nsa_pe_k_2)[0]), pe_v=pe_pairs(A(nsa_pe_v_2)[0]),
                ffn_dw=cols(ffn_w_dw_2), ffn_db=cols(ffn_b_dw_2))
    vec = np.concatenate([vecs[k] for k in VEC], 1)

    def ktiles(w):
        w = A(w)
        return w.reshape(w.shape[0] // P, P, w.shape[1]).transpose(1, 0, 2)

    w_in = ktiles(ssm_w_in[0])
    nsa_in = ktiles(nsa_w_in_2[0])
    at = np.cumsum([0, 1024] + [256] * 6 + [48])
    small = np.concatenate([w_in[:, :, INNER + 4096:].reshape(P, -1), nsa_in[:, :, at[7]:].reshape(P, -1),
                            ktiles(nsa_ck_w2_2[0]).reshape(P, -1), ktiles(nsa_cv_w2_2[0]).reshape(P, -1)], 1)

    def wide(w, width=L):
        return [w[:, :, j:j + width].reshape(P, -1) for j in range(0, w.shape[2], width)]

    def both(a, b):
        return [np.concatenate([a[:, :, j:j + P], b[:, :, j:j + P]], 2).reshape(P, -1)
                for j in range(0, a.shape[2], P)]

    def feed_forward(a, b, down):
        ups = both(a, b)
        d = ktiles(down)
        downs = [d[:, 2 * p:2 * p + 2, :].reshape(P, -1) for p in range(PAIRS)]
        out = ups[0:2]
        for p in range(1, PAIRS):
            out += [ups[2 * p], ups[2 * p + 1], downs[p - 1]]
        return out + [downs[-1]]

    def swiglu(i, j):
        return feed_forward(ktiles(ffn_w_gate[i, j]), ktiles(ffn_w_up[i, j]), ffn_w_down[i, j])

    def conv_ffn(i):
        w = ktiles(ffn_w_up_2[i])
        return feed_forward(w[:, :, :FF], w[:, :, FF:], ffn_w_down_2[i])

    heads = [(j // 4 * 2 + half) * 4 + j % 4 for j in range(KD) for half in (0, 1)]
    q_cols = np.concatenate([np.arange(h * HD, (h + 1) * HD) for h in heads])
    pw1 = ktiles(conv_w_pw1_2[0])
    stream = {
        "ffn0": swiglu(0, 0),
        "ssm": wide(w_in[:, :, INNER:INNER + 4096]) + wide(w_in[:, :, :INNER]) + wide(ktiles(ssm_w_out[0]), P),
        "ffn1": swiglu(0, 1),
        "ffn2": swiglu(1, 0),
        "moba": wide(ktiles(attn_w_qkv[0])) + wide(ktiles(attn_w_out[0])),
        "ffn3": swiglu(1, 1),
        "conf": both(pw1[:, :, :D], pw1[:, :, D:]) + wide(ktiles(conv_w_pw2_2[0])),
        "cffn0": conv_ffn(0),
        "nsa": wide(nsa_in[:, :, q_cols]) + [nsa_in[:, :, at[i]:at[i + 1]].reshape(P, -1) for i in (3, 5, 1, 2, 4, 6)]
        + wide(ktiles(nsa_ck_w1_2[0]), P) + wide(ktiles(nsa_cv_w1_2[0]), P) + wide(ktiles(A(nsa_w_out_2[0])[q_cols])),
        "cffn1": conv_ffn(1),
    }
    weights = np.stack([s for name, _ in LAYERS for s in stream[name]])
    mods = A(mod_w).reshape(NMOD, D, MSLOTS, 2, P).transpose(0, 2, 4, 3, 1).reshape(NMOD * MSLOTS, P, 2, D)
    arrays = {"in_x": cols(A(x)[0]).reshape(P, L, KD).transpose(0, 2, 1),
              "in_c": np.broadcast_to(A(c).reshape(1, D), (P, D)), "in_vectors": vec, "in_small": small, "in_constants": constants(),
              "in_mods": mods, "in_weights": weights}
    arrays = {k: np.ascontiguousarray(v) for k, v in arrays.items()}

    nc = bacc.Bacc("TRN2", target_bir_lowering=False, num_devices=1)
    args = [nc.dram_tensor(n, a.shape, F32, kind="ExternalInput").ap() for n, a in arrays.items()]
    out = nc.dram_tensor("out", (P, KD, L), F32, kind="ExternalOutput").ap()
    build(nc, *args, out)
    r = run_bass_kernel_spmd(nc, [arrays], core_ids=[0])
    y = r.results[0]["out"]
    return y.transpose(2, 1, 0).reshape(1, L, D)
```

```python
from contextlib import ExitStack

import numpy as np
import concourse.bass as bass
from concourse import mybir

F32 = mybir.dt.float32
BF16 = mybir.dt.bfloat16
F32R = mybir.dt.float32r
ALU = mybir.AluOpType
ACT = mybir.ActivationFunctionType
AX_X = mybir.AxisListType.X

P = 128
L = 256
D = 1024
KD = D // P
FF = 2816
NF = FF // P
PAIRS = NF // 2
INNER = 2048
KI = INNER // P
SH = 32
GRP = 8
HPG = SH // GRP
AH = 16
HD = 64
NB = 3
NCMP = 15
EPS = 1e-6
TRI = L + P
SLOT = 2048
RING = 6
MRING = 3
MPART = 8
GATE_SLOT = 8
MSLOTS = 12
NMOD = 6
FSLOTS = 3 * PAIRS

LAYERS = [("ffn0", FSLOTS), ("ssm", 24 + 8), ("ffn1", FSLOTS), ("ffn2", FSLOTS), ("moba", 12 + 4),
          ("ffn3", FSLOTS), ("conf", 8 + 4), ("cffn0", FSLOTS), ("nsa", 10 + 4 + 4), ("cffn1", FSLOTS)]
AT_SLOT = {}
SLOTS = 0
for _name, _n in LAYERS:
    AT_SLOT[_name] = SLOTS
    SLOTS += _n
assert SLOTS % RING == 0

VEC = {}
NVEC = 0
for _name, _n in [("norm_g", 6 * KD), ("mod_b", 6 * 24), ("conv_w", 4 * 32), ("conv_b", 32),
                  ("dt_bias", 1), ("a_log", 1), ("ssm_d", KI), ("ssm_norm", KI), ("final_g", KD),
                  ("mix_g", 2 * KD), ("ffn_g", 2 * KD), ("b_pw1", 16), ("w_dw", 31 * KD), ("b_dw", KD),
                  ("ln_g", KD), ("ln_b", KD), ("b_pw2", KD), ("q_norm", 1), ("kc_norm", 1), ("ks_norm", 1),
                  ("kw_norm", 1), ("pe_k", 16), ("pe_v", 16), ("ffn_dw", 2 * 3 * NF), ("ffn_db", 2 * NF)]:
    VEC[_name] = NVEC
    NVEC += _n

SMALL = {"w_dt": 0, "w_gl": KD * SH, "ck2": KD * SH + KD * 48, "cv2": KD * SH + KD * 48 + 2 * HD}
NSMALL = KD * SH + KD * 48 + 4 * HD

CON = {}
NCON = 0
for _name, _n in [("ident", P), ("block", P), ("tri", TRI), ("mask_sq", TRI), ("mask_qk", TRI), ("dist", TRI),
                  ("cmp_add", 2 * 32), ("cmp_one", 2 * 32), ("cos", L), ("sin", L), ("rope", P),
                  ("pick0", P), ("pick1", P)]:
    CON[_name] = NCON
    NCON += _n


def constants():
    con = np.zeros((P, NCON), np.float32)

    def put(name, a):
        con[:a.shape[0], CON[name]:CON[name] + a.shape[1]] = a

    i = np.arange(P)
    t = np.arange(L)
    put("ident", np.eye(P))
    put("block", (i[:, None] // HD == i[None, :] // HD).astype(np.float32))
    tri = [(s0 + i[:, None] <= t[None, :]).astype(np.float32) for s0 in (0, P)]
    put("tri", np.concatenate([tri[0], tri[1][:, P:]], 1))
    sq = np.concatenate([1 - tri[0], (1 - tri[1])[:, P:]], 1) * np.float32(-1e30)
    put("mask_sq", sq)
    ok = np.concatenate([i[:, None] >= i[None, :], P + i[:, None] >= t[None, :]], 1)
    put("mask_qk", np.where(ok, 0.0, -1e30))
    dist = np.concatenate([i[None, :] - i[:, None], t[None, :] - (P + i[:, None])], 1)
    put("dist", np.where(ok, dist, -1e30))
    end = np.arange(32) * 16 + 31
    seen = np.concatenate([(end[None, :] <= q0 + i[:, None]) & (np.arange(32) < NCMP)[None, :] for q0 in (0, P)], 1)
    put("cmp_add", np.where(seen, 0.0, -1e30))
    put("cmp_one", seen.astype(np.float32))
    inv = (np.float32(500000.0) ** (-np.arange(8, dtype=np.float32) * np.float32(2.0 / 16))).astype(np.float32)
    ang = (t.astype(np.float32)[None, :] * inv[:, None]).astype(np.float32).astype(np.float64)
    cos, sin, rope = np.ones((P, L)), np.zeros((P, L)), np.zeros((P, P))
    for h in (0, HD):
        for half in (0, 8):
            cos[h + half:h + half + 8] = np.cos(ang)
            sin[h + half:h + half + 8] = np.sin(ang)
        for j in range(8):
            rope[h + 8 + j, h + j] = -1.0
            rope[h + j, h + 8 + j] = 1.0
    put("cos", cos)
    put("sin", sin)
    put("rope", rope)
    for par in (0, 1):
        put(f"pick{par}", (i[:, None] == par * HD + i[None, :] % HD).astype(np.float32))
    return con


class Chain:

    def __init__(self, eng, sem):
        self.eng, self.sem, self.n, self.off = eng, sem, 0, 0

    def link(self, ins, behind=0):
        ins.then_inc(self.sem, 1)
        self.n += 1
        self.eng.wait_ge(self.sem, self.n + self.off - behind)


def build(nc, x_in, c_in, vec_in, small_in, con_in, mod_in, w_in, out):
    with ExitStack() as ctx:
        def sb(name, shape, dt=F32):
            return ctx.enter_context(nc.sbuf_tensor(name, shape, dt))

        def sem(name):
            return ctx.enter_context(nc.semaphore(name))

        ring = sb("ring", [P, RING, SLOT])
        mring = sb("mring", [P, MRING, 2, D])
        modsum = sb("modsum", [P, 2, 24, MPART])
        vec = sb("vec", [P, NVEC])
        small = sb("small", [P, NSMALL])
        con = sb("con", [P, NCON])
        ones = sb("ones", [P, P])
        eps = sb("eps", [P, 1])
        zeros = sb("zeros", [P, 512], BF16)
        X = sb("X", [P, KD, L])
        h_at = nc.sbuf_base
        H = sb("H", [P, KD, L])
        rstd = sb("rstd", [P, 2 * L])
        rtok = sb("rtok", [P, 2])
        modv = sb("modv", [P, 24])
        modsc = sb("modsc", [P, KD])
        gate = sb("gate", [P, KD])
        modraw = sb("modraw", [P, 24])
        cact = sb("cact", [P, D])
        ARENA = 23460
        arena_at = nc.sbuf_base
        arena = sb("arena", [P, ARENA])

        def part(at, *shape):
            n = int(np.prod(shape))
            assert at + n <= ARENA
            v = arena[:, at:at + n]
            if len(shape) == 2:
                return v.rearrange("p (a b) -> p a b", a=shape[0])
            if len(shape) == 3:
                return v.rearrange("p (a b c) -> p a b c", a=shape[0], b=shape[1])
            return v

        def rounded(name, at, *shape):
            assert at + int(np.prod(shape)) <= ARENA
            return nc.alloc_sbuf_tensor_at(name, [P, *shape], F32R, offset=arena_at + 4 * at)

        act_buf = part(0, 2, L)
        hid_hi = rounded("hid_hi", 2 * L, 4, L)
        hid_lo = rounded("hid_lo", 6 * L, 4, L)
        H_hi = rounded("H_hi", 10 * L, KD, L)
        H_lo = nc.alloc_sbuf_tensor_at("H_lo", [P, KD, L], F32R, offset=h_at)
        SPLIT_AT = [18 * L + 2 * SLOT * i for i in (2, 1, 0)]
        w_hi = [rounded(f"w_hi{i}", a, SLOT) for i, a in enumerate(SPLIT_AT)]
        w_lo = [rounded(f"w_lo{i}", a + SLOT, SLOT) for i, a in enumerate(SPLIT_AT)]
        Z = part(0, KI, L)
        XBC = part(KI * L, 2 * KI, L)
        XT = part(3 * KI * L, 2, INNER)
        at = 4 * KI * L
        Wd = H.rearrange("p k t -> p (k t)")[:, 0:4 * TRI].rearrange("p (b t) -> p b t", b=4)
        Yt = H.rearrange("p k t -> p (k t)")[:, 4 * TRI:4 * TRI + 2 * L].rearrange("p (b t) -> p b t", b=2)
        dtx = part(at, 2, L)
        tri_r = rounded("tri_r", at, TRI)
        dta_hi = rounded("dta_hi", at + TRI, 2, SH)
        dta_lo = rounded("dta_lo", at + TRI + 2 * SH, 2, SH)
        dtT = part(at + 2 * TRI, 4, SH)
        acT = part(at + 2 * TRI + 4 * SH, 2, SH)
        dts = part(at + 2 * TRI + 6 * SH, 2, L)
        negA = modv[0:SH, 0:1]
        Q = part(0, KD, L)
        K = part(2048, KD, L)
        QR = part(2048, KD, L)
        V = part(4096, 2, D)
        O = part(6144, KD, L)
        LAG = 4
        PBUF = LAG + 1
        PT = part(8192, 2, TRI)
        nmax = part(8960, PBUF, 2)
        psum_ = part(8980, PBUF, 2)
        Pb = part(17888, PBUF, TRI)
        H_hi_moba = rounded("H_hi_moba", 6144, KD, L)
        w_hi_moba = [rounded(f"w_hi_moba{i}", 9000 + 2 * SLOT * i, SLOT) for i in range(3)]
        w_lo_moba = [rounded(f"w_lo_moba{i}", 9000 + 2 * SLOT * i + SLOT, SLOT) for i in range(3)]
        KS = part(10130, 2, L)
        KW = part(10642, 2, L)
        KC = part(11154, 2, L)
        VC = part(11666, 2, L)
        gates = part(12178, 2, 48)
        zk = part(12274, 16, 60)
        hidc = part(13234, 2, 60)
        hidr = part(13354, 2, 512)
        kcmp = part(14378, 30)
        vcmp = part(14408, 4, HD)
        pc = part(14664, 2, 512)
        PC = part(15688, 4, L)
        st32 = part(16712, 2, 32)
        sqb = part(16776, 512)
        sq12 = part(17888 + PBUF * TRI, 12, L)
        inv_rep = sq12.rearrange("p a t -> p (a t)")
        inv12 = part(17888 + PBUF * TRI + 12 * L, 48)
        rope_g = part(17888 + PBUF * TRI + 12 * L + 48, 3, P)
        kdiag = part(17888 + PBUF * TRI + 12 * L + 48 + 3 * P, P)
        zk2 = part(17888, 16, 60)
        UP = part(0, KD, 30 + L)
        CV = part(2304, KD, L)
        sgb = part(4352, 2, L)
        TAPS = 9
        taps = part(4864, TAPS, L)

        acc = ctx.enter_context(nc.psum_tensor("acc", [P, 4, 512], F32))
        up = ctx.enter_context(nc.psum_tensor("up", [P, 2, 512], F32))
        stat = ctx.enter_context(nc.psum_tensor("stat", [P, 512], F32))
        misc = ctx.enter_context(nc.psum_tensor("misc", [P, 512], F32))

        def acc_t(m):
            return acc[:, m // 2, (m % 2) * L:(m % 2 + 1) * L]

        def v1(name, col=0, n=1):
            return vec[:, VEC[name] + col:VEC[name] + col + n]

        def cs(name, a, b):
            return con[:, CON[name] + a:CON[name] + b]

        ident = cs("ident", 0, P)

        vec_landed, con_landed, small_landed, x_landed = (sem(s) for s in (
            "vec_landed", "con_landed", "small_landed", "x_landed"))
        slot_landed = [sem(f"slot_landed{i}") for i in range(RING)]
        mod_landed = [sem(f"mod_landed{i}") for i in range(MRING)]
        slot_done = sem("slot_done")
        mod_used = sem("mod_used")
        mod_reduced = sem("mod_reduced")
        modvec_ready = sem("modvec_ready")
        setup_done = sem("setup_done")
        c_landed = sem("c_landed")
        cact_ready = sem("cact_ready")
        x_ready = sem("x_ready")
        down_ready = sem("down_ready")
        sq_ready = sem("sq_ready")
        stat_ready = sem("stat_ready")
        rcp_ready = sem("rcp_ready")
        spread_ready = sem("spread_ready")
        root_ready = sem("root_ready")
        xn_ready = sem("xn_ready")
        h_ready = sem("h_ready")
        pair_free = sem("pair_free")
        silu_ready = sem("silu_ready")
        dwc_ready = sem("dwc_ready")
        hi_ready = sem("hi_ready")
        split_ready = sem("split_ready")
        hid_hi_ready = sem("hid_hi_ready")
        hid_ready = sem("hid_ready")
        presum_ready = sem("presum_ready")
        tap_ready = sem("tap_ready")
        tap_added = sem("tap_added")
        raw_ready = sem("raw_ready")
        misc_ready = sem("misc_ready")
        xt_ready = sem("xt_ready")
        misc_used = sem("misc_used")
        aux_v = sem("aux_v")
        aux_s = sem("aux_s")
        dta_ready = sem("dta_ready")
        bc_ready = sem("bc_ready")
        cb_ready = sem("cb_ready")
        seg_ready = sem("seg_ready")
        exp_ready = sem("exp_ready")
        w_ready = sem("w_ready")
        y_done = sem("y_done")
        y_free = sem("y_free")
        score_ready = sem("score_ready")
        mask_done = sem("mask_done")
        max_ready = sem("max_ready")
        pexp_ready = sem("pexp_ready")
        norm_ready = sem("norm_ready")
        p_ready = sem("p_ready")
        t_done = sem("t_done")
        pt_ready = sem("pt_ready")
        o_done = sem("o_done")
        v_done = sem("v_done")
        s_done = sem("s_done")
        g_done = sem("g_done")
        rope_ready = sem("rope_ready")
        head_inv = sem("head_inv")
        head_spread = sem("head_spread")
        head_used = sem("head_used")
        pick_ready = sem("pick_ready")
        zk_ready = sem("zk_ready")
        out_stored = sem("out_stored")

        block = ctx.enter_context(nc.Block())

        CONV_DVE, CONV_POOL, CONV_ORDER = (0, 1, 3, 5, 6, 7), (2, 4), (0, 1, 2, 3, 5, 4, 6, 7)
        GLU_TAPS = 18

        PRE = 4

        def hidden_tile(s):
            return s if s < 2 else None if (s - 2) % 3 == 2 else 2 + 2 * ((s - 2) // 3) + (s - 2) % 3

        ROUNDS = (PAIRS - 1) // 2

        NSA_HEADS = [(j // 4 * 2 + half) * 4 + j % 4 for j in range(KD) for half in (0, 1)]

        def units_moba():
            for h in range(AH):
                base = (h % 2) * HD
                yield dict(q=Q, k=K, kt=h // 2, qt=h // 2, base=base, vcol=h * HD, slope=2.0 ** (-8.0 * (h + 1) / AH),
                           gate=None, first=True, last=True, tile=h // 2, cmp=None)

        def units_nsa():
            for n, h in enumerate(NSA_HEADS):
                g = h // 4
                for b, (k, vc) in enumerate(((KS, 0), (KW, 256))):
                    yield dict(q=QR, k=k, kt=g // 2, qt=n // 2, base=(n % 2) * HD, vcol=vc + g * HD, slope=None,
                               gate=h * NB + 1 + b, first=b == 0, last=b == 1, tile=n // 2, cmp=h)

        @block.sync
        def _(sp):
            sp.dma_start(cact[:, :], c_in).then_inc(c_landed, 16)
            sp.dma_start(vec[:, :], vec_in).then_inc(vec_landed, 16)

            def load_mod(n, m, wait):
                if wait is not None:
                    sp.wait_ge(mod_used, wait)
                sp.dma_start(mring[:, n % MRING, :, :], mod_in[m]).then_inc(mod_landed[n % MRING], 16)

            for n in range(MRING):
                load_mod(n, n, None)
            sp.dma_start(X[:, :, :], x_in).then_inc(x_landed, 16)
            sp.dma_start(con[:, :], con_in).then_inc(con_landed, 16)
            for n in range(MRING, GATE_SLOT):
                load_mod(n, n, n - MRING + 1)
            for j in range(RING):
                sp.dma_start(ring[:, j, :], w_in[j]).then_inc(slot_landed[j], 16)
            for n in range(GATE_SLOT, MSLOTS):
                load_mod(n, n, n - MRING + 1)
            sp.dma_start(small[:, :], small_in).then_inc(small_landed, 16)
            MIX = (NMOD - 1) * MSLOTS // MRING
            with sp.Fori(1, MIX + 1) as it:
                for j in range(RING):
                    sp.wait_ge(slot_done, (it - 1) * RING + j + 1)
                    sp.dma_start(ring[:, j, :], w_in[it * RING + j]).then_inc(slot_landed[j], 16)
                for j in range(MRING):
                    load_mod(j, it * MRING + (MSLOTS - MRING) + j, it * MRING + (MSLOTS - 2 * MRING) + j + 1)
            with sp.Fori(MIX + 1, SLOTS // RING) as it:
                for j in range(RING):
                    sp.wait_ge(slot_done, (it - 1) * RING + j + 1)
                    sp.dma_start(ring[:, j, :], w_in[it * RING + j]).then_inc(slot_landed[j], 16)
            sp.wait_ge(x_ready, XR["end"])
            sp.dma_start(out, X[:, :, :]).then_inc(out_stored, 16)
            sp.wait_ge(out_stored, 16)

        @block.gpsimd
        def _(pool):
            order = Chain(pool, g_done)
            pool.wait_ge(mod_used, GATE_SLOT)
            pool.wait_ge(cact_ready, 1)

            def fold(m, it, slots=range(MSLOTS)):
                n0 = m * MSLOTS
                for i in slots:
                    w = mring[:, i % MRING, :, :]
                    pool.wait_ge(mod_landed[i % MRING], 16 * ((n0 + i) // MRING + 1) + it * (16 * 2 * MSLOTS // MRING))
                    order.link(pool.tensor_tensor(w, w, cact[:, :].unsqueeze(1).to_broadcast([P, 2, D]), ALU.mult))
                    half = D // 2
                    while half > MPART:
                        order.link(pool.tensor_tensor(w[:, :, 0:half], w[:, :, 0:half], w[:, :, half:2 * half], ALU.add))
                        half //= 2
                    pool.tensor_tensor(modsum[:, m % 2, 2 * i:2 * i + 2, :], w[:, :, 0:half], w[:, :, half:2 * half],
                                       ALU.add).then_inc(mod_used, 1)
                    pool.wait_ge(mod_used, n0 + i + 1 + it * 2 * MSLOTS)

            fold(0, 0, range(GATE_SLOT, MSLOTS))
            before = order.n
            fold(1, 0)
            links = order.n - before
            with pool.Fori(0, 2) as it:
                for m in (2, 3):
                    pool.wait_ge(mod_reduced, it * 2 + m - 1)
                    order.off = it * (2 * links)
                    fold(m, it)
            def attention(units, base):
                for u, a in enumerate(units):
                    b = u % PBUF
                    pool.wait_ge(norm_ready, base["u"] + u + 1)
                    for tt, (c0, c1) in enumerate(((0, P), (P, TRI))):
                        ins = pool.tensor_tensor(Pb[:, b, c0:c1], Pb[:, b, c0:c1],
                                                 psum_[:, b, tt:tt + 1].to_broadcast([P, c1 - c0]), ALU.mult)
                    ins.then_inc(p_ready, 1)

            attention(units_moba(), UNITS["moba"])
            for i, m in enumerate(CONV_POOL):
                pool.wait_ge(tap_ready, 31 * i + 1)
                for tap in range(1, 31):
                    n = 30 * i + tap - 1
                    pool.wait_ge(tap_ready, 31 * i + tap + 1)
                    pool.tensor_tensor(CV[:, m, :], CV[:, m, :], taps[:, n % (TAPS - 1), :], ALU.add).then_inc(tap_added, 1)
                    pool.wait_ge(tap_added, n + 1)
            attention(units_nsa(), UNITS["nsa"])

        @block.tensor
        def _(pe):
            state = dict(h=0, free=0, sq=0, misc=0, split=0, hid=0, rcp=0, presum=0, conv=0)
            mm = pe.matmul

            def landed(n, it=0):
                pe.wait_ge(slot_landed[n % RING], 16 * (n // RING + 1) + it * 16)
                return ring[:, n % RING, :]

            def sum_tiles(src, n, presum=True, done=0):
                if presum:
                    state["presum"] += 1
                    pe.wait_ge(presum_ready, state["presum"])
                for m in range(done, n):
                    state["sq"] += 1
                    if presum and 1 <= m < PRE:
                        continue
                    if not presum or m:
                        pe.wait_ge(sq_ready, state["sq"])
                    for tt in range(2):
                        ins = mm(stat[:, tt:tt + 1], src[:, m, tt * P:(tt + 1) * P], ones[:, 0:1],
                                 start=(m == 0 and tt == 0), stop=(m == n - 1), skip_group_check=True)
                ins.then_inc(stat_ready, 1)
                state["rcp"] += 1
                pe.wait_ge(rcp_ready, state["rcp"])
                for tt in range(2):
                    ins = mm(stat[:, L + tt * P:L + (tt + 1) * P], rtok[:, tt:tt + 1].to_broadcast([P, P]), ident,
                             start=(tt == 0), stop=True, skip_group_check=True)
                ins.then_inc(spread_ready, 1)

            def norm(presum=True):
                sum_tiles(H, KD, presum)

            def pair(n, bank, src, it=0, first=False, inc=True):
                w = landed(n, it)
                for k in range(KD):
                    if first:
                        state["h"] += 1
                        pe.wait_ge(h_ready, state["h"])
                    for e in range(2):
                        ins = mm(bank[:, e * L:(e + 1) * L], w[:, k * L + e * P:k * L + (e + 1) * P], src[:, k, :],
                                 start=(k == 0 and e == 0), stop=(k == KD - 1), skip_group_check=True)
                ins.then_inc(slot_done, 1)

            def three(dst, w, cols, x_hi, x_lo, start, stop):
                hi, lo = w_hi[w][:, cols], w_lo[w][:, cols]
                mm(dst, hi, x_hi, start=start, stop=False, skip_group_check=True)
                mm(dst, hi, x_lo, start=False, stop=False, skip_group_check=True)
                return mm(dst, lo, x_hi, start=False, stop=stop, skip_group_check=True)

            def ffn():
                f0, s0 = state["free"], state["split"]
                for b in range(4):
                    mm(acc[:, b, :], zeros[:, 0:P], zeros[:, :], start=True, stop=True, skip_group_check=True)

                def gate_up(s, it=0):
                    f = hidden_tile(s)
                    pe.wait_ge(split_ready, s0 + s + 1 + it * 6)
                    if f >= 2:
                        pe.wait_ge(pair_free, f0 + f - 1 + it * 4)
                    for k in range(KD):
                        if s == 0:
                            state["h"] += 1
                            pe.wait_ge(h_ready, state["h"])
                        for e in range(2):
                            ins = three(up[:, f % 2, e * L:(e + 1) * L], s % 3,
                                        slice(k * L + e * P, k * L + (e + 1) * P), H_hi[:, k, :], H_lo[:, k, :],
                                        start=(k == 0 and e == 0), stop=(k == KD - 1))
                    ins.then_inc(slot_done, 1)

                def down(s, p, it=0, last=False):
                    pe.wait_ge(split_ready, s0 + s + 1 + it * 6)
                    pe.wait_ge(hid_ready, f0h + 2 * p + 2 + it * 4)
                    for m in range(KD):
                        for e in range(2):
                            h = (2 * p + e) % 4
                            ins = three(acc_t(m), s % 3, slice((e * KD + m) * P, (e * KD + m + 1) * P),
                                        hid_hi[:, h, :], hid_lo[:, h, :], start=False, stop=False)
                        if last and m % 2 and m < KD - 1:
                            ins.then_inc(down_ready, 1)
                    ins.then_inc(slot_done, 1)

                f0h = state["hid"]
                gate_up(0)
                gate_up(1)
                with pe.Fori(0, ROUNDS) as it:
                    for s in (2, 5):
                        gate_up(s, it)
                        gate_up(s + 1, it)
                        down(s + 2, (s - 2) // 3, it)
                down(FSLOTS - 1, PAIRS - 1, last=True)
                state["free"] += NF
                state["hid"] += NF
                state["split"] += FSLOTS

            def project_out(n0, src):
                for j in range(4):
                    w = landed(n0 + j)
                    for k in range(KD):
                        if j == 0:
                            state["h"] += 1
                            pe.wait_ge(h_ready, state["h"])
                        for e in range(2):
                            ins = mm(acc[:, j, e * L:(e + 1) * L], w[:, k * L + e * P:k * L + (e + 1) * P],
                                     src[:, k, :], start=(k == 0 and e == 0), stop=(k == KD - 1),
                                     skip_group_check=True)
                    ins.then_inc(slot_done, 1)

            def misc_step(ins):
                ins.then_inc(misc_ready, 1)
                state["misc"] += 1

            def misc_wait():
                pe.wait_ge(misc_used, state["misc"])

            def ssm(n0):
                pe.wait_ge(small_landed, 16)
                wdt = small[:, 0:KD * SH].rearrange("p (k n) -> p k n", k=KD)
                for k in range(KD):
                    state["h"] += 1
                    pe.wait_ge(h_ready, state["h"])
                    ins = mm(misc[0:SH, 0:L], wdt[:, k, :], H[:, k, :], start=(k == 0), stop=(k == KD - 1),
                             skip_group_check=True)
                misc_step(ins)
                f0 = state["free"]
                pair(n0, up[:, 0, :], H)
                pair(n0 + 1, up[:, 1, :], H)
                for n in range(2, RING):
                    pe.wait_ge(pair_free, f0 + n - 1)
                    pair(n0 + n, up[:, n % 2, :], H)
                with pe.Fori(0, 3) as it:
                    for n in range(RING, 2 * RING):
                        pe.wait_ge(pair_free, f0 + n - 1 + it * RING)
                        pair(n0 + n, up[:, n % 2, :], H, it)
                state["free"] += 24
                misc_wait()
                for q in range(2):
                    for tt in range(2):
                        j = 2 * q + tt
                        ins = pe.transpose(misc[:, j * SH:(j + 1) * SH], dts[0:SH, q, tt * P:(tt + 1) * P],
                                           ident[0:SH, 0:SH])
                misc_step(ins)
                misc_wait()
                tri0, tri1 = cs("tri", 0, L), cs("tri", L, TRI)
                mm(misc[:, 0:SH], tri0[:, 0:P], dtT[:, 2, :], start=True, stop=True, skip_group_check=True)
                mm(misc[:, SH:2 * SH], tri0[:, P:L], dtT[:, 2, :], start=True, stop=False, skip_group_check=True)
                misc_step(mm(misc[:, SH:2 * SH], tri1, dtT[:, 3, :], start=False, stop=True,
                             skip_group_check=True))
                pe.wait_ge(pair_free, state["free"])
                for j in range(8):
                    if j >= 2:
                        pe.wait_ge(pair_free, state["free"] - 1)
                    for tt in range(2):
                        for e in range(2):
                            ins = pe.transpose(up[:, j % 2, (2 * tt + e) * P:(2 * tt + e + 1) * P],
                                               XBC[:, 2 * j + e, tt * P:(tt + 1) * P], ident)
                    ins.then_inc(xt_ready, 1)
                    state["free"] += 1
                pe.wait_ge(pair_free, state["free"])

                pe.wait_ge(dta_ready, 1)

                def y(h):
                    pe.wait_ge(w_ready, h + 1)
                    if h % 2 == 0 and h >= 4:
                        pe.wait_ge(y_free, h // 2 - 1)
                    dst = up[(h % 2) * HD:(h % 2 + 1) * HD, (h // 2) % 2, 0:L]
                    mm(dst, XT[:, 0, h * HD:(h + 1) * HD], Wd[:, h % 4, 0:L], start=True, stop=False,
                       skip_group_check=True)
                    mm(dst[:, P:L], XT[:, 1, h * HD:(h + 1) * HD], Wd[:, h % 4, L:TRI], start=False, stop=True,
                       skip_group_check=True).then_inc(y_done, 1)

                for h in range(SH):
                    g = h // HPG
                    if h % HPG == 0:
                        if g >= 2:
                            pe.wait_ge(w_ready, HPG * (g - 1))
                        Bg, Cg = XBC[:, KI + g, :], XBC[:, KI + GRP + g, :]
                        mm(acc[:, 2 + g % 2, 0:L], Bg[:, 0:P], Cg, start=True, stop=True, skip_group_check=True)
                        mm(acc[:, 2 + g % 2, L:TRI], Bg[:, P:L], Cg[:, P:L], start=False, stop=True,
                           skip_group_check=True).then_inc(cb_ready, 1)
                    if h >= 2:
                        pe.wait_ge(seg_ready, h - 1)
                    bc = acc[:, h % 2, :]
                    mm(bc[:, 0:L], dta_hi[:, 0, h:h + 1].to_broadcast([P, P]), tri_r[:, 0:L], start=True, stop=False,
                       skip_group_check=True)
                    mm(bc[:, 0:L], dta_lo[:, 0, h:h + 1].to_broadcast([P, P]), tri_r[:, 0:L], start=False, stop=False,
                       skip_group_check=True)
                    mm(bc[:, P:L], dta_hi[:, 1, h:h + 1].to_broadcast([P, P]), tri_r[:, L:TRI], start=False,
                       stop=False, skip_group_check=True)
                    mm(bc[:, P:L], dta_lo[:, 1, h:h + 1].to_broadcast([P, P]), tri_r[:, L:TRI], start=False,
                       stop=True, skip_group_check=True).then_inc(bc_ready, 1)
                    if h >= 2:
                        y(h - 2)
                    if h >= 11 and h % 2:
                        m = (h - 11) // 2
                        state["sq"] += 1
                        pe.wait_ge(sq_ready, state["sq"])
                        for tt in range(2):
                            mm(stat[:, tt:tt + 1], XBC[:, m, tt * P:(tt + 1) * P], ones[:, 0:1],
                               start=(m == 0 and tt == 0), stop=False, skip_group_check=True)
                y(SH - 2)
                y(SH - 1)
                sum_tiles(XBC, KI, presum=False, done=(SH - 11 + 1) // 2)
                for m in range(KD):
                    w = landed(n0 + 24 + m)
                    for k in range(KI):
                        if m == 0:
                            state["h"] += 1
                            pe.wait_ge(h_ready, state["h"])
                        ins = mm(acc_t(m), w[:, k * P:(k + 1) * P], Z[:, k, :], start=(k == 0 and m % 2 == 0),
                                 stop=(k == KI - 1), skip_group_check=True)
                    ins.then_inc(slot_done, 1)

            def value_pairs(n0, count):
                for j in range(count):
                    pe.wait_ge(pair_free, state["free"] - 1)
                    w = landed(n0 + j)
                    for k in range(KD):
                        for tt in range(2):
                            ins = mm(up[:, state["free"] % 2, tt * L:(tt + 1) * L], H[:, k, tt * P:(tt + 1) * P],
                                     w[:, k * L:(k + 1) * L], start=(k == 0 and tt == 0), stop=(k == KD - 1),
                                     skip_group_check=True)
                    ins.then_inc(slot_done, 1)
                    state["free"] += 1

            def pairs(n0, count):
                for j in range(count):
                    if j >= 2:
                        pe.wait_ge(pair_free, state["free"] - 1)
                    pair(n0 + j, up[:, state["free"] % 2, :], H, first=(j == 0))
                    state["free"] += 1

            def attention(units, base):
                units = list(units)
                n = len(units)
                for u in range(n + LAG + 2):
                    if u < n:
                        a = units[u]
                        if u >= 2:
                            pe.wait_ge(mask_done, base["u"] + u - 1)
                        q = a["q"][a["base"]:a["base"] + HD, a["qt"], :]
                        k = a["k"][a["base"]:a["base"] + HD, a["kt"], :]
                        mm(acc[:, u % 2, 0:P], q[:, 0:P], k[:, 0:P], start=True, stop=True, skip_group_check=True)
                        mm(acc[:, u % 2, P:TRI], q[:, P:L], k, start=False, stop=True,
                           skip_group_check=True).then_inc(score_ready, 1)
                    if LAG <= u < n + LAG:
                        t = u - LAG
                        pe.wait_ge(p_ready, base["u"] + t + 1)
                        if t >= 2:
                            pe.wait_ge(pt_ready, base["u"] + t - 1)
                        pb = Pb[:, t % PBUF, :]
                        pe.transpose(acc[:, 2 + t % 2, 0:P], pb[:, 0:P], ident)
                        pe.transpose(acc[:, 2 + t % 2, P:L], pb[:, P:L], ident)
                        pe.transpose(acc[:, 2 + t % 2, L:TRI], pb[:, L:TRI], ident).then_inc(t_done, 1)
                    if u >= LAG + 2:
                        t = u - LAG - 2
                        a = units[t]
                        pe.wait_ge(pt_ready, base["u"] + t + 1)
                        if a["first"] and a["base"] == 0 and a["tile"] >= 2:
                            pe.wait_ge(h_ready, state["h"] + a["tile"] - 1)
                        dst = up[a["base"]:a["base"] + HD, a["tile"] % 2, 0:L]
                        v = a["vcol"]
                        if a["cmp"] is not None and a["first"]:
                            r, g = a["cmp"] % 4, a["cmp"] // 4
                            mm(dst, vcmp[32 * r:32 * r + 32, g, :], PC[32 * r:32 * r + 32, g, :], start=True,
                               stop=False, skip_group_check=True)
                        mm(dst, V[:, 0, v:v + HD], PT[:, t % 2, 0:L], start=(a["first"] and a["cmp"] is None),
                           stop=False, skip_group_check=True)
                        mm(dst[:, P:L], V[:, 1, v:v + HD], PT[:, t % 2, L:TRI], start=False, stop=a["last"],
                           skip_group_check=True).then_inc(o_done, 1)

            def moba(n0):
                s0, f0 = state["split"], state["free"]
                for s in range(12):
                    pe.wait_ge(split_ready, s0 + s + 1)
                    if s >= 2:
                        pe.wait_ge(pair_free, f0 + s - 1)
                    bank, hi, lo = up[:, (f0 + s) % 2, :], w_hi_moba[s % 3], w_lo_moba[s % 3]
                    for k in range(KD):
                        if s == 0:
                            state["h"] += 1
                            pe.wait_ge(h_ready, state["h"])
                        for e in range(2):
                            for i, (w, x) in enumerate(((hi, H_hi_moba), (hi, H_lo), (lo, H_hi_moba))):
                                if s < 8:
                                    a, b = w[:, k * L + e * P:k * L + (e + 1) * P], x[:, k, :]
                                else:
                                    a, b = x[:, k, e * P:(e + 1) * P], w[:, k * L:(k + 1) * L]
                                ins = mm(bank[:, e * L:(e + 1) * L], a, b, start=(k == 0 and e == 0 and i == 0),
                                         stop=(k == KD - 1 and i == 2), skip_group_check=True)
                    ins.then_inc(slot_done, 1)
                state["free"] += 12
                state["split"] += 12
                pe.wait_ge(pair_free, state["free"])
                attention(units_moba(), UNITS["moba"])
                project_out(n0 + 12, O)

            def conformer(n0):
                pairs(n0, 8)
                sum_tiles_plain(CV)
                sum_tiles(H, KD)
                project_out(n0 + 8, CV)

            def sum_tiles_plain(src):
                for i, m in enumerate(CONV_ORDER):
                    if m in CONV_DVE:
                        state["h"] += 1
                        pe.wait_ge(h_ready, state["h"])
                    else:
                        pe.wait_ge(tap_added, 30 * (CONV_POOL.index(m) + 1))
                    ins = mm(stat[:, 0:L], ones[:, :], src[:, m, :], start=(i == 0), stop=(i == KD - 1),
                             skip_group_check=True)
                ins.then_inc(stat_ready, 1)

            def head_stat(rhs, n):
                misc_wait()
                state["sq"] += 1
                pe.wait_ge(sq_ready, state["sq"])
                misc_step(mm(misc[:, 0:n], cs("block", 0, P), rhs, start=True, stop=True, skip_group_check=True))

            def nsa(n0):
                qk = [(0, Q), (2, Q), (4, Q), (6, Q), (0, KS), (0, KW)]
                f0 = state["free"]

                def rotate(j):
                    pe.wait_ge(pair_free, f0 + j + 1)
                    misc_wait()
                    t0, buf = qk[j]
                    for e in range(2):
                        ins = mm(misc[:, e * L:(e + 1) * L], rope_g[:, max(0, j - 3), :], buf[:, t0 + e, :],
                                 start=(e == 0), stop=True, skip_group_check=True)
                    misc_step(ins)
                    state["sq"] += 1
                    pe.wait_ge(sq_ready, state["sq"])
                    for i in (2 * j, 2 * j + 1):
                        for tt in range(2):
                            c = 4 * i + 2 * tt
                            ins = mm(stat[:, c:c + 2], sq12[:, i, tt * P:(tt + 1) * P], cs("block", 0, P)[:, 0:P:HD],
                                     start=(c == 0), stop=True, skip_group_check=True)
                    if j == 5:
                        ins.then_inc(stat_ready, 1)

                def spread(j):
                    pe.wait_ge(head_inv, j + 1)
                    if j >= 4:
                        pe.wait_ge(head_used, j - 3)
                    for e in range(2):
                        for tt in range(2):
                            c = 8 * j + 4 * e + 2 * tt
                            ins = mm(acc[:, j % 4, e * L + tt * P:e * L + (tt + 1) * P],
                                     inv_rep[:, c * HD:(c + 2) * HD], ident,
                                     start=(e == 0 and tt == 0), stop=True, skip_group_check=True)
                    ins.then_inc(head_spread, 1)

                def pick(c, src):
                    pe.wait_ge(pair_free, f0 + 7 + c)
                    pe.wait_ge(head_used, 4 + 2 * c)
                    for g in range(4):
                        ins = mm(acc[:, 2 - 2 * c + g // 2, (g % 2) * L:(g % 2 + 1) * L], cs(f"pick{g % 2}", 0, P),
                                 src[:, g // 2, :], start=(g % 2 == 0), stop=True, skip_group_check=True)
                    ins.then_inc(pick_ready, 1)

                def hidden(c, m, dst):
                    w = landed(n0 + 10 + 2 * c + m)
                    z = (zk, zk2)[c]
                    for k in range(16):
                        ins = mm(dst[:, 60 * m:60 * m + 60], w[:, k * P:(k + 1) * P], z[:, k, :],
                                 start=(k == 0 and m == 0), stop=(k == 15), skip_group_check=True)
                    ins.then_inc(slot_done, 1)

                pe.wait_ge(con_landed, 16)
                wgl = small[:, SMALL["w_gl"]:SMALL["w_gl"] + KD * 48].rearrange("p (k n) -> p k n", k=KD)
                misc_wait()
                for k in range(KD):
                    state["h"] += 1
                    pe.wait_ge(h_ready, state["h"])
                    for tt in range(2):
                        ins = mm(misc[:, tt * 48:(tt + 1) * 48], H[:, k, tt * P:(tt + 1) * P], wgl[:, k, :],
                                 start=(k == 0 and tt == 0), stop=(k == KD - 1), skip_group_check=True)
                misc_step(ins)
                pe.wait_ge(rope_ready, 1)
                for j in range(8):
                    if j >= 2:
                        pe.wait_ge(pair_free, state["free"] - 1)
                    pair(n0 + j, up[:, state["free"] % 2, :], H)
                    state["free"] += 1
                    if 1 <= j <= 6:
                        rotate(j - 1)
                for j in range(4):
                    spread(j)
                value_pairs(n0 + 8, 1)
                spread(4)
                spread(5)
                pick(0, KC)
                value_pairs(n0 + 9, 1)
                pick(1, VC)
                w2 = [small[:, SMALL[second]:SMALL[second] + 2 * HD].rearrange("p (k n) -> p k n", k=2)
                      for second in ("ck2", "cv2")]
                hid_v = up[:, state["free"] % 2, :]
                pe.wait_ge(zk_ready, 1)
                hidden(0, 0, stat)
                hidden(0, 1, stat)
                pe.wait_ge(zk_ready, 2)
                pe.wait_ge(pair_free, state["free"] - 1)
                hidden(1, 0, hid_v)
                state["h"] += 1
                pe.wait_ge(h_ready, state["h"])
                hk = hidc.rearrange("p m (a b n) -> p m a b n", a=2, b=2)
                for par in range(2):
                    for m in range(2):
                        ins = mm(misc[par * HD:(par + 1) * HD, 0:30], w2[0][:, m, :], hk[:, m, :, par, :],
                                 start=(m == 0), stop=(m == 1), skip_group_check=True)
                misc_step(ins)
                hidden(1, 1, hid_v)
                head_stat(sqb[:, 0:30], 30)
                state["h"] += 1
                pe.wait_ge(h_ready, state["h"])
                misc_wait()
                for g in range(4):
                    for m in range(2):
                        ins = mm(misc[:, g * HD:(g + 1) * HD], hidr[:, m, g * P:(g + 1) * P], w2[1][:, m, :],
                                 start=(g == 0 and m == 0), stop=(m == 1), skip_group_check=True)
                misc_step(ins)
                pe.wait_ge(head_used, 6)
                for tt in range(2):
                    for j in range(KD):
                        ins = mm(acc[:, tt, j * HD:(j + 1) * HD], Q[:, j, tt * P:(tt + 1) * P],
                                 kdiag[:, (j // 4) * HD:(j // 4 + 1) * HD], start=(j == 0), stop=True,
                                 skip_group_check=True)
                misc_wait()
                misc_step(ins)
                misc_wait()
                for g in range(4):
                    for tt in range(2):
                        ins = pe.transpose(up[:, g // 2, ((g % 2) * 2 + tt) * P:((g % 2) * 2 + tt + 1) * P],
                                           pc[:, tt, g * P:(g + 1) * P], ident)
                misc_step(ins)
                misc_wait()
                attention(units_nsa(), UNITS["nsa"])
                project_out(n0 + 14, O)

            pe.wait_ge(setup_done, 3)
            pe.wait_ge(con_landed, 16)
            norm(presum=False)
            ffn()
            norm()
            ssm(AT_SLOT["ssm"])
            norm()
            ffn()
            norm()
            ffn()
            norm()
            moba(AT_SLOT["moba"])
            norm()
            ffn()
            norm()
            state["h"] += KD
            norm()
            conformer(AT_SLOT["conf"])
            norm()
            ffn()
            norm()
            nsa(AT_SLOT["nsa"])
            norm()
            ffn()

        @block.scalar
        def _(act):
            state = dict(x=0, h=0, xn=0, stat=0, free=0, hid=0, silu=0, dwc=0, misc=0, aux_v=0, mod=0)
            order = Chain(act, s_done)

            def root(width):
                state["stat"] += 1
                act.wait_ge(stat_ready, state["stat"])
                act.activation(rtok[:, :], stat[:, 0:2], ACT.Sqrt, scale=1.0 / width,
                               bias=eps[:, 0:1]).then_inc(root_ready, 1)

            def norm(scale, shift=None, mod=False, dest=H, own=False, first=False, parts=False, hi=H_hi):
                for m in range(KD):
                    if own:
                        act.wait_ge(h_ready, state["h"] - KD + m + 1)
                    elif first:
                        act.wait_ge(x_landed, 16)
                    else:
                        state["x"] += 1
                        act.wait_ge(x_ready, state["x"])
                    act.activation(H[:, m, :], X[:, m, :], ACT.Square).then_inc(sq_ready, 1)
                if hi is H_hi_moba:
                    high_moba(AT_SLOT["moba"], 0)
                root(D)
                if mod:
                    state["mod"] += 1
                    act.wait_ge(modvec_ready, state["mod"])
                for m in range(KD):
                    state["xn"] += 1
                    act.wait_ge(xn_ready, state["xn"])
                    if parts and shift is None:
                        ins = act.activation(hi[:, m, :], H[:, m, :], ACT.Copy)
                    elif parts:
                        ins = act.activation(hi[:, m, :], H[:, m, :], ACT.Identity, bias=shift(m))
                    elif shift is None:
                        ins = act.activation(dest[:, m, :], H[:, m, :], ACT.Copy, scale=scale(m))
                    else:
                        ins = act.activation(dest[:, m, :], H[:, m, :], ACT.Identity, scale=scale(m), bias=shift(m))
                    ins.then_inc(raw_ready if parts else h_ready, 1)
                    state["h"] += 1

            def mod_norm(first=False, parts=False, hi=H_hi):
                norm(lambda m: modsc[:, m:m + 1], lambda m: modv[:, m:m + 1], mod=True, first=first, parts=parts, hi=hi)

            def high(n0, s, it=0):
                if n0 + s >= 3:
                    act.wait_ge(slot_done, n0 + s - 2 + it * 6)
                n = n0 + s
                act.wait_ge(slot_landed[n % RING], 16 * (n // RING + 1) + it * 16)
                act.activation(w_hi[s % 3][:, :], ring[:, n % RING, :], ACT.Copy).then_inc(hi_ready, 1)

            def ffn(n0, conv=False):
                high(n0, 2)

                def after(s, it):
                    f = hidden_tile(s)
                    if f is not None:
                        a = act_buf[:, f % 2, :]
                        if conv:
                            act.wait_ge(dwc_ready, state["dwc"] + f + 1 + it * 4)
                            act.activation(a, a, ACT.Silu).then_inc(silu_ready, 1)
                        else:
                            act.wait_ge(slot_done, n0 + s + 1 + it * 6)
                            if f >= 2:
                                act.wait_ge(hid_ready, state["hid"] + f - 1 + it * 4)
                            act.activation(a, up[:, f % 2, 0:L], ACT.Silu).then_inc(silu_ready, 1)
                    if s + 3 + 6 * (it if isinstance(it, int) else 0) < FSLOTS:
                        high(n0, s + 3, it)
                    if f is not None:
                        act.wait_ge(pair_free, state["free"] + f + 1 + it * 4)
                        if f >= 2:
                            act.wait_ge(slot_done, n0 + 3 * (f // 2) - 1 + it * 6)
                        act.activation(hid_hi[:, f % 4, :], a, ACT.Copy).then_inc(hid_hi_ready, 1)

                for s in range(2):
                    after(s, 0)
                with act.Fori(0, ROUNDS - 1) as it:
                    for s in range(2, 8):
                        after(s, it)
                for s in range(2, 8):
                    after(s, ROUNDS - 1)
                state["free"] += NF
                state["hid"] += NF
                if conv:
                    state["dwc"] += NF

            def aux_wait():
                state["aux_v"] += 1
                act.wait_ge(aux_v, state["aux_v"])

            def ssm(n0):
                aux_wait()
                act.activation(dts[0:SH, 1, :], dts[0:SH, 1, :], ACT.Exp).then_inc(aux_s, 1)
                act.activation(negA, v1("a_log")[0:SH, :], ACT.Exp).then_inc(aux_s, 1)
                act.wait_ge(aux_s, 2)
                act.activation(dtx[0:SH, 0, :], dts[0:SH, 1, :], ACT.Ln, bias=ones[0:SH, 0:1]).then_inc(aux_s, 1)
                f0 = state["free"]
                with act.Fori(0, 8) as it:
                    for j in range(2):
                        act.wait_ge(pair_free, f0 + 1 + j + it * 2)
                        v = XBC[:, bass.ds(it * 4 + 2 * j, 2), :]
                        act.activation(v, v, ACT.Silu).then_inc(silu_ready, 1)
                with act.Fori(0, 4) as it:
                    for j in range(2):
                        act.wait_ge(slot_done, n0 + 17 + j + it * 2)
                        act.activation(Z[:, bass.ds(it * 4 + 2 * j, 2), :], up[:, j, :].rearrange("p (a t) -> p a t", a=2),
                                       ACT.Silu).then_inc(pair_free, 1)
                state["free"] += 24 + 8
                state["silu"] += 16
                act.wait_ge(misc_used, 1)
                act.activation(tri_r[:, :], cs("tri", 0, TRI), ACT.Copy).then_inc(aux_s, 1)

                def square(m):
                    act.wait_ge(y_free, 0 + m + 1)
                    act.activation(XBC[:, m, :], Z[:, m, :], ACT.Square).then_inc(sq_ready, 1)

                for h in range(SH):
                    act.wait_ge(seg_ready, h + 1)
                    act.activation(Wd[:, h % 4, :], Wd[:, h % 4, :], ACT.Exp).then_inc(exp_ready, 1)
                    if h >= 6 and h % 2 == 0:
                        square((h - 6) // 2)
                for m in range(SH // 2 - 3, SH // 2):
                    square(m)
                root(INNER)

            def attention(units, base):
                units = list(units)
                n = len(units)
                for u in range(n + LAG + 1):
                    if u > LAG:
                        t = u - LAG - 1
                        act.wait_ge(t_done, base["u"] + t + 1)
                        if t >= 2:
                            act.wait_ge(o_done, base["u"] + t - 1)
                        act.activation(PT[:, t % 2, :], acc[:, 2 + t % 2, 0:TRI], ACT.Copy).then_inc(pt_ready, 1)
                    if u < n:
                        act.wait_ge(max_ready, base["u"] + u + 1)
                        b = u % PBUF
                        for tt, (c0, c1) in enumerate(((0, P), (P, TRI))):
                            ins = act.activation(Pb[:, b, c0:c1], Pb[:, b, c0:c1], ACT.Exp, bias=nmax[:, b, tt:tt + 1],
                                                 accum_out=psum_[:, b, tt:tt + 1])
                        ins.then_inc(pexp_ready, 1)

            def evacuate(n, dst, scale=1.0):
                act.wait_ge(slot_done, n + 1)
                act.activation(dst, up[:, state["free"] % 2, :].rearrange("p (a t) -> p a t", a=2), ACT.Copy,
                               scale=scale).then_inc(pair_free, 1)
                state["free"] += 1

            def high_moba(n0, s):
                act.wait_ge(slot_done, n0 + max(0, s - 2))
                n = n0 + s
                act.wait_ge(slot_landed[n % RING], 16 * (n // RING + 1))
                act.activation(w_hi_moba[s % 3][:, :], ring[:, n % RING, :], ACT.Copy).then_inc(hi_ready, 1)

            def moba(n0):
                dst = [(Q[:, 2 * j:2 * j + 2, :], HD ** -0.5) for j in range(4)]
                dst += [(K[:, 2 * j:2 * j + 2, :], 1.0) for j in range(4)]
                dst += [(V[:, :, j * L:(j + 1) * L], 1.0) for j in range(4)]
                high_moba(n0, 1)
                high_moba(n0, 2)
                for j in range(12):
                    if j + 3 < 12:
                        high_moba(n0, j + 3)
                    evacuate(n0 + j, *dst[j])
                attention(units_moba(), UNITS["moba"])
                state["h"] += KD

            def conformer(n0):
                free0 = state["free"]
                todo = [(i, tap) for i in range(len(CONV_POOL)) for tap in range(31)]

                def products(count):
                    for i, tap in todo[:count]:
                        m, n = CONV_POOL[i], 30 * i + tap - 1
                        if tap == 0:
                            act.wait_ge(pair_free, free0 + m + 1)
                            act.activation(CV[:, m, :], UP[:, m, 0:L], ACT.Identity, scale=v1("w_dw", m),
                                           bias=v1("b_dw", m)).then_inc(tap_ready, 1)
                            continue
                        if n >= TAPS - 1:
                            act.wait_ge(tap_added, n - TAPS + 2)
                        act.activation(taps[:, n % (TAPS - 1), :], UP[:, m, tap:tap + L], ACT.Copy,
                                       scale=v1("w_dw", tap * KD + m)).then_inc(tap_ready, 1)
                    del todo[:count]

                for m in range(KD):
                    act.wait_ge(slot_done, n0 + m + 1)
                    if m >= 2:
                        act.wait_ge(pair_free, state["free"] - 1)
                    act.activation(sgb[:, m % 2, :], up[:, state["free"] % 2, L:2 * L], ACT.Sigmoid,
                                   bias=v1("b_pw1", KD + m)).then_inc(silu_ready, 1)
                    state["free"] += 1
                    if m >= CONV_POOL[0]:
                        products(12)
                products(len(todo))
                state["h"] += len(CONV_DVE)
                state["stat"] += 1
                for m in range(KD):
                    aux_wait()
                    act.activation(H[:, m, :], CV[:, m, :], ACT.Square).then_inc(sq_ready, 1)
                root(D)
                for m in range(KD):
                    state["xn"] += 1
                    act.wait_ge(xn_ready, state["xn"])
                    act.activation(CV[:, m, :], CV[:, m, :], ACT.Silu, scale=v1("ln_g", m),
                                   bias=v1("ln_b", m)).then_inc(h_ready, 1)
                    state["h"] += 1

            def head_root(n):
                state["misc"] += 1
                act.wait_ge(misc_ready, state["misc"])
                act.activation(rstd[:, 0:n], misc[:, 0:n], ACT.Sqrt, scale=1.0 / HD,
                               bias=eps[:, 0:1]).then_inc(root_ready, 1)

            def nsa(n0):
                base = UNITS["misc_at_nsa"]
                state["misc"] = base + 1
                act.wait_ge(misc_ready, state["misc"])
                act.activation(gates.rearrange("p a b -> p (a b)"), misc[:, 0:96], ACT.Sigmoid).then_inc(misc_used, 1)
                dst = [Q[:, 2 * j:2 * j + 2, :] for j in range(4)] + [KS, KW, KC, VC]
                for j in range(8):
                    evacuate(n0 + j, dst[j])
                    if j < 6:
                        act.wait_ge(pair_free, state["free"])
                        act.activation(sq12[:, 2 * j:2 * j + 2, :], dst[j], ACT.Square).then_inc(sq_ready, 1)
                    if j == 6:
                        state["stat"] += 1
                        act.wait_ge(stat_ready, state["stat"])
                        act.activation(inv12, stat[:, 0:48], ACT.Sqrt, scale=1.0 / HD,
                                       bias=eps[:, 0:1]).then_inc(root_ready, 1)
                for j in range(2):
                    evacuate(n0 + 8 + j, V[:, :, j * L:(j + 1) * L])
                hid_v = up[:, state["free"] % 2, 0:120]
                hc = hidc.rearrange("p m n -> p (m n)")
                state["misc"] += 7
                act.wait_ge(slot_done, n0 + 12)
                act.activation(hc, stat[:, 0:120], ACT.Silu).then_inc(h_ready, 1)
                act.wait_ge(misc_used, state["misc"])
                act.activation(sqb[:, 0:30], kcmp, ACT.Square).then_inc(sq_ready, 1)
                act.wait_ge(slot_done, n0 + 14)
                act.activation(hc, hid_v, ACT.Silu).then_inc(aux_s, 1)
                head_root(30)
                state["misc"] += 1
                state["h"] += 2
                aux_wait()
                act.activation(pc, pc, ACT.Exp).then_inc(aux_s, 1)
                attention(units_nsa(), UNITS["nsa"])
                state["h"] += KD

            act.wait_ge(vec_landed, 16)
            act.wait_ge(c_landed, 16)
            act.activation(cact[:, :], cact[:, :], ACT.Silu).then_inc(cact_ready, 1)
            act.wait_ge(setup_done, 3)

            def gated_ffn(name, first=False):
                if not first:
                    high(AT_SLOT[name], 0)
                    high(AT_SLOT[name], 1)
                mod_norm(first=first, parts=True)
                if first:
                    high(AT_SLOT[name], 0)
                    high(AT_SLOT[name], 1)
                ffn(AT_SLOT[name])

            def plain_ffn(name, i):
                high(AT_SLOT[name], 0)
                high(AT_SLOT[name], 1)
                norm(lambda m: v1("ffn_g", i * KD + m), parts=True)
                ffn(AT_SLOT[name], conv=True)

            gated_ffn("ffn0", first=True)
            mod_norm()
            ssm(AT_SLOT["ssm"])
            state["h"] += KI
            gated_ffn("ffn1")
            gated_ffn("ffn2")
            mod_norm(parts=True, hi=H_hi_moba)
            moba(AT_SLOT["moba"])
            gated_ffn("ffn3")
            norm(lambda m: v1("final_g", m), dest=X)
            norm(lambda m: v1("mix_g", m), own=True)
            conformer(AT_SLOT["conf"])
            plain_ffn("cffn0", 0)
            norm(lambda m: v1("mix_g", KD + m))
            nsa(AT_SLOT["nsa"])
            plain_ffn("cffn1", 1)

        @block.vector
        def _(dve):
            state = dict(root=0, free=0, silu=0, misc=0, mod=0, down=0, aux_s=3, split=0, hid=0, raw=0, rcp=0, sq=KD,
                         xn=0)
            order = Chain(dve, v_done)
            link = order.link

            def low(n0, s, it=0):
                n = n0 + s
                dve.wait_ge(hi_ready, state["split"] + s + 1 + it * 6)
                dve.tensor_tensor(w_lo[s % 3][:, :], ring[:, n % RING, :], w_hi[s % 3][:, :].bitcast(F32),
                                  ALU.subtract).then_inc(split_ready, 1)

            def low_moba(n0, s):
                dve.wait_ge(hi_ready, state["split"] + s + 1)
                dve.tensor_tensor(w_lo_moba[s % 3][:, :], ring[:, (n0 + s) % RING, :],
                                  w_hi_moba[s % 3][:, :].bitcast(F32), ALU.subtract).then_inc(split_ready, 1)

            def add_square(m):
                if not 1 <= m < PRE:
                    return
                dve.wait_ge(sq_ready, state["sq"] + m + 1)
                ins = dve.tensor_tensor(H[:, 0, :], H[:, 0, :], H[:, m, :], ALU.add)
                if m == PRE - 1:
                    ins.then_inc(presum_ready, 1)
                    state["sq"] += KD
                else:
                    link(ins)

            def inverse_root():
                state["root"] += 1
                dve.wait_ge(root_ready, state["root"])
                dve.reciprocal(rtok[:, :], rtok[:, :]).then_inc(rcp_ready, 1)
                state["rcp"] += 1
                dve.wait_ge(spread_ready, state["rcp"])

            def norm(mod=None, half=1.0, parts=False, gain=None, col=0, own=False, hi=H_hi):
                if own:
                    for m in range(PRE):
                        add_square(m)
                if mod is not None:
                    state["mod"] += 1
                    if mod == 0:
                        link(dve.tensor_tensor(modv[:, 0:16], modraw[:, 0:16], v1("mod_b", 0, 16), ALU.add))
                    else:
                        dve.wait_ge(mod_used, MSLOTS * (mod + 1))
                        link(dve.tensor_reduce(modraw[:, :], modsum[:, mod % 2, :, :], AX_X, ALU.add))
                        dve.tensor_tensor(modv[:, :], modraw[:, :], v1("mod_b", mod * 24, 24),
                                          ALU.add).then_inc(mod_reduced, 1)
                        dve.wait_ge(mod_reduced, mod + 1)
                        link(dve.tensor_scalar(gate[:, :], modv[:, 16:24], half, None, ALU.mult))
                    dve.scalar_tensor_tensor(out=modsc[:, :], in0=modv[:, 8:16], scalar=1.0,
                                             in1=v1("norm_g", mod * KD, KD), op0=ALU.add,
                                             op1=ALU.mult).then_inc(modvec_ready, 1)
                if hi is H_hi_moba:
                    low_moba(AT_SLOT["moba"], 0)
                inverse_root()
                if mod is not None:
                    dve.wait_ge(modvec_ready, state["mod"])
                if not parts:
                    for m in range(KD):
                        dve.tensor_tensor(H[:, m, :], X[:, m, :], stat[:, L:2 * L], ALU.mult).then_inc(xn_ready, 1)
                    return

                def scaled(m):
                    sc = v1(gain, col + m) if gain else modsc[:, m:m + 1]
                    dve.scalar_tensor_tensor(out=H[:, m, :], in0=X[:, m, :], scalar=sc, in1=stat[:, L:2 * L],
                                             op0=ALU.mult, op1=ALU.mult).then_inc(xn_ready, 1)

                scaled(0)
                scaled(1)
                for m in range(KD):
                    state["raw"] += 1
                    dve.wait_ge(raw_ready, state["raw"])
                    if gain:
                        ins = dve.tensor_tensor(H_lo[:, m, :], H[:, m, :], hi[:, m, :].bitcast(F32), ALU.subtract)
                    else:
                        ins = dve.scalar_tensor_tensor(out=H_lo[:, m, :], in0=H[:, m, :], scalar=modv[:, m:m + 1],
                                                       in1=hi[:, m, :].bitcast(F32), op0=ALU.add, op1=ALU.subtract)
                    ins.then_inc(h_ready, 1)
                    if m + 2 < KD:
                        scaled(m + 2)

            def update(m, how):
                if how == "gate":
                    ins = dve.scalar_tensor_tensor(out=X[:, m, :], in0=acc_t(m), scalar=gate[:, m:m + 1],
                                                   in1=X[:, m, :], op0=ALU.mult, op1=ALU.add)
                elif how == "bias":
                    ins = dve.scalar_tensor_tensor(out=X[:, m, :], in0=acc_t(m), scalar=v1("b_pw2", m),
                                                   in1=X[:, m, :], op0=ALU.add, op1=ALU.add)
                else:
                    ins = dve.tensor_tensor(X[:, m, :], acc_t(m), X[:, m, :], ALU.add)
                ins.then_inc(x_ready, 1)

            def update_ffn(n0, how, then=None, square=True):
                if n0 == 0:
                    dve.wait_ge(mod_used, MSLOTS)
                    link(dve.tensor_reduce(modraw[:, 16:24], modsum[:, 0, 16:24, :], AX_X, ALU.add))
                    dve.tensor_tensor(modv[:, 16:24], modraw[:, 16:24], v1("mod_b", 16, 8), ALU.add).then_inc(mod_reduced, 1)
                    dve.wait_ge(mod_reduced, 1)
                    link(dve.tensor_scalar(gate[:, :], modv[:, 16:24], 0.5, None, ALU.mult))
                if then is not None:
                    low(then, 0)
                    low(then, 1)
                for m in range(KD):
                    if m < KD - 2 and m % 2 == 0:
                        state["down"] += 1
                        dve.wait_ge(down_ready, state["down"])
                    elif m == KD - 2:
                        dve.wait_ge(slot_done, n0 + FSLOTS)
                    update(m, how)
                    if m >= 2 and square:
                        add_square(m - 2)

            def update_slots(n0, per, how):
                for m in range(KD):
                    if m % 2 == 0:
                        dve.wait_ge(slot_done, n0 + (m + 2) // per)
                    update(m, how)
                    if m >= 2:
                        add_square(m - 2)
                    if m in (3, 5):
                        low(n0 + KD // per, (m - 3) // 2)

            def ffn(n0, i=None, then=None):
                low(n0, 2)
                links = 0 if i is None else 8

                def after(s, it):
                    f = hidden_tile(s)
                    if f is not None:
                        o, a = act_buf[:, f % 2, :], up[:, f % 2, 0:L]
                        if i is not None:
                            def col(name, c):
                                if f < 2:
                                    return v1(name, c + f)
                                return vec[:, bass.ds(it * 4 + (VEC[name] + c + f), 1)]

                            if f >= 2:
                                dve.wait_ge(hid_ready, state["hid"] + f - 1 + it * 4)
                            dve.wait_ge(slot_done, n0 + s + 1 + it * 6)
                            w = [col("ffn_dw", (3 * i + j) * NF) for j in range(3)]
                            link(dve.tensor_scalar(o, a, w[2], col("ffn_db", i * NF), ALU.mult, ALU.add))
                            link(dve.scalar_tensor_tensor(out=o[:, 1:L], in0=a[:, 0:L - 1], scalar=w[1],
                                                          in1=o[:, 1:L], op0=ALU.mult, op1=ALU.add))
                            dve.scalar_tensor_tensor(out=o[:, 2:L], in0=a[:, 0:L - 2], scalar=w[0], in1=o[:, 2:L],
                                                     op0=ALU.mult, op1=ALU.add).then_inc(dwc_ready, 1)
                        dve.wait_ge(silu_ready, state["silu"] + f + 1 + it * 4)
                        dve.tensor_tensor(o, o, up[:, f % 2, L:2 * L], ALU.mult).then_inc(pair_free, 1)
                    if s + 3 + 6 * (it if isinstance(it, int) else 0) < FSLOTS:
                        low(n0, s + 3, it)
                    if f is not None:
                        dve.wait_ge(hid_hi_ready, state["hid"] + f + 1 + it * 4)
                        dve.tensor_tensor(hid_lo[:, f % 4, :], o, hid_hi[:, f % 4, :].bitcast(F32),
                                          ALU.subtract).then_inc(hid_ready, 1)

                for s in range(2):
                    after(s, 0)
                before = order.n
                with dve.Fori(0, ROUNDS - 1) as it:
                    if links:
                        order.off = it * links
                    for s in range(2, 8):
                        after(s, it)
                assert order.n - before == links
                order.n, order.off = before + links * (ROUNDS - 1), 0
                for s in range(2, 8):
                    after(s, ROUNDS - 1)
                state["silu"] += NF
                state["free"] += NF
                state["hid"] += NF
                state["split"] += FSLOTS
                update_ffn(n0, "gate" if i is None else "plain", then, square=i != 1)

            def misc_wait():
                state["misc"] += 1
                dve.wait_ge(misc_ready, state["misc"])

            def ssm(n0):
                misc_wait()
                v, e, lnu = dts[0:SH, 0, :], dts[0:SH, 1, :], dtx[0:SH, 0, :]
                u, dt = dtx[0:SH, 1, :], dts[0:SH, 0, :]
                link(dve.tensor_scalar(v, misc[0:SH, 0:L], v1("dt_bias")[0:SH, :], None, ALU.add))
                dve.scalar_tensor_tensor(out=e, in0=v, scalar=-1.0, in1=v, op0=ALU.mult,
                                         op1=ALU.min).then_inc(aux_v, 1)
                dve.wait_ge(aux_s, 3)
                link(dve.tensor_scalar(u, e, 1.0, -1.0, ALU.add, ALU.add))
                link(dve.tensor_tensor(lnu, lnu, e, ALU.mult))
                link(dve.scalar_tensor_tensor(out=e, in0=u, scalar=0.0, in1=e, op0=ALU.is_equal, op1=ALU.mult))
                link(dve.tensor_scalar(u, u, 1e-30, None, ALU.max))
                link(dve.reciprocal(u, u))
                link(dve.tensor_tensor(lnu, lnu, u, ALU.mult))
                link(dve.tensor_tensor(lnu, lnu, e, ALU.add))
                link(dve.scalar_tensor_tensor(out=dt, in0=v, scalar=0.0, in1=lnu, op0=ALU.max, op1=ALU.add))
                link(dve.tensor_scalar(negA, negA, -1.0, None, ALU.mult))
                dve.tensor_scalar(e, dt, negA, None, ALU.mult).then_inc(misc_used, 1)
                per = 14
                before = order.n
                with dve.Fori(0, 8) as it:
                    for j in range(2):
                        dve.wait_ge(slot_done, n0 + 1 + j + it * 2)
                        order.off = it * per
                        for tap in range(4):
                            for t in range(2):
                                c = it * 4 + 2 * j + t
                                a = up[:, j, t * L:(t + 1) * L]
                                o = XBC[:, bass.ds(c, 1), :].rearrange("p a t -> p (a t)")
                                w = vec[:, bass.ds(c + (VEC["conv_w"] + (3 - tap) * 32), 1)]
                                if tap == 0:
                                    ins = dve.tensor_scalar(o, a, w, vec[:, bass.ds(c + VEC["conv_b"], 1)],
                                                            ALU.mult, ALU.add)
                                else:
                                    ins = dve.scalar_tensor_tensor(out=o[:, tap:L], in0=a[:, 0:L - tap], scalar=w,
                                                                   in1=o[:, tap:L], op0=ALU.mult, op1=ALU.add)
                                if tap == 3 and t == 1:
                                    ins.then_inc(pair_free, 1)
                                else:
                                    link(ins)
                assert order.n - before == per
                order.n, order.off = before + per * 8, 0
                state["free"] += 24
                state["silu"] += 16
                misc_wait()
                dve.tensor_copy(dtT.rearrange("p a h -> p (a h)"), misc[:, 0:4 * SH]).then_inc(misc_used, 1)
                dve.wait_ge(misc_used, 2)
                misc_wait()
                dve.tensor_copy(acT.rearrange("p a h -> p (a h)"), misc[:, 0:2 * SH]).then_inc(misc_used, 1)
                dve.wait_ge(misc_used, 3)
                state["aux_s"] += 1
                dve.wait_ge(aux_s, state["aux_s"])
                link(dve.tensor_copy(dta_hi[:, :, :], dtT[:, 2:4, :]))
                dve.tensor_tensor(dta_lo[:, :, :], dtT[:, 2:4, :], dta_hi[:, :, :].bitcast(F32),
                                  ALU.subtract).then_inc(dta_ready, 1)
                for j in range(8):
                    dve.wait_ge(xt_ready, j + 1)
                    dve.tensor_tensor(
                        XT[:, :, j * L:(j + 1) * L].rearrange("p a (h c) -> p a h c", c=HD),
                        up[:, j % 2, :].rearrange("p (a h c) -> p a h c", a=2, c=HD),
                        dtT[:, 0:2, 4 * j:4 * j + 4].unsqueeze(3).to_broadcast([P, 2, 4, HD]),
                        ALU.mult).then_inc(pair_free, 1)
                state["free"] += 8

                def weight(h):
                    dve.wait_ge(exp_ready, h + 1)
                    if h % HPG == 0:
                        dve.wait_ge(cb_ready, h // HPG + 1)
                    dve.tensor_tensor(Wd[:, h % 4, :], Wd[:, h % 4, :], acc[:, 2 + (h // HPG) % 2, 0:TRI],
                                      ALU.mult).then_inc(w_ready, 1)

                def gated(m):
                    dve.wait_ge(y_done, 2 * m + 2)
                    link(dve.scalar_tensor_tensor(out=Yt[:, m % 2, :], in0=XBC[:, m, :], scalar=v1("ssm_d", m),
                                                  in1=up[:, m % 2, 0:L], op0=ALU.mult, op1=ALU.add))
                    dve.tensor_tensor(Z[:, m, :], Z[:, m, :], Yt[:, m % 2, :], ALU.mult).then_inc(y_free, 1)

                for h in range(SH):
                    dve.wait_ge(bc_ready, h + 1)
                    if h >= 4:
                        dve.wait_ge(y_done, h - 3)
                    dve.scalar_tensor_tensor(out=Wd[:, h % 4, 0:L], in0=acc[:, h % 2, 0:L], scalar=acT[:, 0, h:h + 1],
                                             in1=cs("mask_sq", 0, L), op0=ALU.subtract, op1=ALU.add)
                    dve.scalar_tensor_tensor(out=Wd[:, h % 4, L:TRI], in0=acc[:, h % 2, P:L],
                                             scalar=acT[:, 1, h:h + 1], in1=cs("mask_sq", L, TRI), op0=ALU.subtract,
                                             op1=ALU.add).then_inc(seg_ready, 1)
                    if h >= 1:
                        weight(h - 1)
                    if h >= 5 and h % 2:
                        gated((h - 5) // 2)
                weight(SH - 1)
                for m in (KI - 2, KI - 1):
                    gated(m)
                state["sq"] += KI
                inverse_root()
                for m in range(KI):
                    dve.scalar_tensor_tensor(out=Z[:, m, :], in0=Z[:, m, :], scalar=v1("ssm_norm", m),
                                             in1=stat[:, L:2 * L], op0=ALU.mult, op1=ALU.mult).then_inc(h_ready, 1)
                update_slots(n0 + 24, 1, "gate")

            def attention(units, base):
                units = list(units)
                n = len(units)

                def normalise(t):
                    a, b = units[t], t % PBUF
                    dve.wait_ge(pexp_ready, base["u"] + t + 1)
                    ins = dve.reciprocal(psum_[:, b, :], psum_[:, b, :])
                    if a["gate"] is not None:
                        link(ins)
                        ins = dve.tensor_tensor(psum_[:, b, :], psum_[:, b, :], gates[:, :, a["gate"]], ALU.mult)
                    ins.then_inc(norm_ready, 1)

                def take(t):
                    a = units[t]
                    if a["last"] and a["base"] == HD:
                        dve.wait_ge(o_done, base["u"] + t + 1)
                        dve.tensor_copy(O[:, a["tile"], :], up[:, a["tile"] % 2, 0:L]).then_inc(h_ready, 1)

                for u in range(n + LAG + 3):
                    if u < n:
                        a, b = units[u], u % PBUF
                        dve.wait_ge(score_ready, base["u"] + u + 1)
                        if u >= PBUF:
                            dve.wait_ge(t_done, base["u"] + u - PBUF + 1)
                        if a["slope"] is not None:
                            dve.scalar_tensor_tensor(out=Pb[:, b, :], in0=cs("dist", 0, TRI), scalar=a["slope"],
                                                     in1=acc[:, u % 2, 0:TRI], op0=ALU.mult,
                                                     op1=ALU.add).then_inc(mask_done, 1)
                        else:
                            dve.tensor_tensor(Pb[:, b, :], acc[:, u % 2, 0:TRI], cs("mask_qk", 0, TRI),
                                              ALU.add).then_inc(mask_done, 1)
                        dve.wait_ge(mask_done, base["u"] + u + 1)
                        dve.tensor_reduce(nmax[:, b, 0:1], Pb[:, b, 0:P], AX_X, ALU.max, negate=True)
                        dve.tensor_reduce(nmax[:, b, 1:2], Pb[:, b, P:TRI], AX_X, ALU.max,
                                          negate=True).then_inc(max_ready, 1)
                    if 1 <= u <= n:
                        normalise(u - 1)
                    if u >= LAG + 3:
                        take(u - LAG - 3)

            def moba(n0):
                for s in range(1, 12):
                    low_moba(n0, s)
                state["split"] += 12
                state["free"] += 12
                attention(units_moba(), UNITS["moba"])
                update_slots(n0 + 12, 2, "gate")

            def conformer(n0):
                link(dve.memset(UP[:, :, 0:30], 0.0))
                free0 = state["free"]

                def glu():
                    m = state["free"] - free0
                    state["silu"] += 1
                    dve.wait_ge(silu_ready, state["silu"])
                    dve.scalar_tensor_tensor(out=UP[:, m, 30:30 + L], in0=up[:, state["free"] % 2, 0:L],
                                             scalar=v1("b_pw1", m), in1=sgb[:, m % 2, :], op0=ALU.add,
                                             op1=ALU.mult).then_inc(pair_free, 1)
                    state["free"] += 1

                done = 0
                odd = taps[:, TAPS - 1, :]
                for m in CONV_DVE:
                    for tap in range(31):
                        while state["free"] - free0 < KD and (state["free"] - free0 <= m
                                                              or done >= GLU_TAPS * (state["free"] - free0)):
                            glu()
                        done += 1
                        part_sum = odd if tap % 2 else CV[:, m, :]
                        if tap == 0:
                            dve.wait_ge(pair_free, free0 + m + 1)
                            ins = dve.tensor_scalar(part_sum, UP[:, m, 0:L], v1("w_dw", m), v1("b_dw", m), ALU.mult,
                                                    ALU.add)
                        elif tap == 1:
                            if m != CONV_DVE[0]:
                                dve.wait_ge(h_ready, UNITS["h_at_conf"] + CONV_DVE.index(m))
                            ins = dve.tensor_scalar(part_sum, UP[:, m, tap:tap + L], v1("w_dw", tap * KD + m), None,
                                                    ALU.mult)
                        else:
                            ins = dve.scalar_tensor_tensor(out=part_sum, in0=UP[:, m, tap:tap + L],
                                                           scalar=v1("w_dw", tap * KD + m), in1=part_sum,
                                                           op0=ALU.mult, op1=ALU.add)
                        if tap < 30:
                            order.link(ins, behind=1)
                        else:
                            link(ins)
                    dve.tensor_tensor(CV[:, m, :], CV[:, m, :], odd, ALU.add).then_inc(h_ready, 1)
                state["stat"] = UNITS["stat_at_conf"] + 1
                dve.wait_ge(stat_ready, state["stat"])
                link(dve.tensor_scalar(rstd[:, L:2 * L], stat[:, 0:L], 1.0 / D, None, ALU.mult))
                for m in range(KD):
                    dve.tensor_tensor(CV[:, m, :], CV[:, m, :], rstd[:, L:2 * L], ALU.subtract).then_inc(aux_v, 1)
                    if m >= 2:
                        add_square(m - 2)
                inverse_root()
                for m in range(KD):
                    dve.tensor_tensor(CV[:, m, :], CV[:, m, :], stat[:, L:2 * L], ALU.mult).then_inc(xn_ready, 1)
                update_slots(n0 + 8, 2, "bias")

            def nsa(n0):
                state["misc"] = UNITS["misc_at_nsa"] + 1
                state["sq"] += 7
                link(dve.memset(pc, 0.0))
                link(dve.memset(hidr, 0.0))
                link(dve.memset(kdiag, 0.0))
                gains = ["q_norm"] * 4 + ["ks_norm", "kw_norm"]
                cos = cs("cos", 0, L).unsqueeze(1).to_broadcast([P, 2, L])
                sin = cs("sin", 0, L).unsqueeze(1).to_broadcast([P, 2, L])
                for i in range(3):
                    ins = dve.tensor_scalar(rope_g[:, i, :], cs("rope", 0, P), v1(gains[3 + i]), None, ALU.mult)
                ins.then_inc(rope_ready, 1)
                for j in range(6):
                    v = Q[:, 2 * j:2 * j + 2, :] if j < 4 else (KS, KW)[j - 4]
                    dst = QR[:, 2 * j:2 * j + 2, :] if j < 4 else v
                    rot = rstd[:, :].rearrange("p (a t) -> p a t", a=2)
                    state["misc"] += 1
                    dve.wait_ge(misc_ready, state["misc"])
                    link(dve.tensor_tensor(rot, misc[:, :].rearrange("p (a t) -> p a t", a=2), sin, ALU.mult))
                    if j >= 4:
                        dve.wait_ge(sq_ready, state["sq"] - 7 + j + 1)
                    link(dve.scalar_tensor_tensor(out=dst, in0=v, scalar=v1(gains[j]), in1=cos, op0=ALU.mult,
                                                  op1=ALU.mult))
                    dve.tensor_tensor(dst, dst, rot, ALU.add).then_inc(misc_used, 1)
                state["root"] += 1
                dve.wait_ge(root_ready, state["root"])
                link(dve.reciprocal(inv12, inv12))
                for j in range(6):
                    dve.tensor_scalar(inv_rep[:, 8 * j * HD:8 * (j + 1) * HD].rearrange("p (c d) -> p c d", c=8),
                                      inv12[:, 8 * j:8 * j + 8].unsqueeze(2).to_broadcast([P, 8, HD]),
                                      HD ** -0.5 if j < 4 else 1.0, None, ALU.mult).then_inc(head_inv, 1)

                def head_norm_pair(j):
                    dve.wait_ge(head_spread, j + 1)
                    inv = acc[:, j % 4, :].rearrange("p (a t) -> p a t", a=2)
                    v = QR[:, 2 * j:2 * j + 2, :] if j < 4 else (KS, KW)[j - 4]
                    ins = dve.tensor_tensor(v, v, inv, ALU.mult)
                    if j < 4:
                        v = Q[:, 2 * j:2 * j + 2, :]
                        ins = dve.scalar_tensor_tensor(out=v, in0=v, scalar=v1(gains[j]), in1=inv, op0=ALU.mult,
                                                       op1=ALU.mult)
                    ins.then_inc(head_used, 1)

                def blocks(c, pe_name, z):
                    dve.wait_ge(pick_ready, c + 1)
                    z4 = z.rearrange("p l (g n) -> p l g n", g=4)
                    for g in range(4):
                        for par in range(2):
                            rows = slice(par * HD, (par + 1) * HD)
                            tok = acc[rows, 2 - 2 * c + g // 2, (g % 2) * L:(g % 2 + 1) * L]
                            tok = bass.AP(tok.tensor, tok.offset + par, [list(tok.ap[0]), [2, 16], [16, NCMP]])
                            pe_b = v1(pe_name, 0, 16)[rows].unsqueeze(2).to_broadcast([HD, 16, NCMP])
                            ins = dve.tensor_tensor(z4[rows, :, g, :], tok, pe_b, ALU.add)
                    ins.then_inc(zk_ready, 1)

                dve.wait_ge(misc_used, state["misc"])
                for j in range(6):
                    head_norm_pair(j)
                blocks(0, "pe_k", zk)
                blocks(1, "pe_v", zk2)
                state["free"] += 10
                state["misc"] += 1
                dve.wait_ge(misc_ready, state["misc"])
                dve.tensor_copy(kcmp, misc[:, 0:30]).then_inc(misc_used, 1)
                dve.wait_ge(misc_used, state["misc"])
                state["aux_s"] += 1
                dve.wait_ge(aux_s, state["aux_s"])
                hr = hidr.rearrange("p m (g r n) -> p m g r n", g=4, r=4)
                hc = hidc.rearrange("p m (g n) -> p m g n", g=4)
                for m in range(2):
                    for g in range(4):
                        ins = dve.tensor_copy(hr[:, m, g, :, 0:NCMP],
                                              hc[:, m, g, :].unsqueeze(1).to_broadcast([P, 4, NCMP]))
                ins.then_inc(h_ready, 1)
                state["root"] += 1
                dve.wait_ge(root_ready, state["root"])
                link(dve.reciprocal(rstd[:, 0:30], rstd[:, 0:30]))
                k4 = kdiag.rearrange("p (a b n) -> p a b n", a=2, b=2)
                for half in range(2):
                    rows = slice(half * HD, (half + 1) * HD)
                    ins = dve.scalar_tensor_tensor(
                        out=k4[rows, :, half, 0:NCMP], in0=kcmp[rows].rearrange("p (a n) -> p a n", a=2),
                        scalar=v1("kc_norm")[rows], in1=rstd[rows, 0:30].rearrange("p (a n) -> p a n", a=2),
                        op0=ALU.mult, op1=ALU.mult)
                ins.then_inc(misc_used, 1)
                state["misc"] += 2
                dve.wait_ge(misc_ready, state["misc"])
                dve.tensor_copy(vcmp.rearrange("p g c -> p (g c)"), misc[:, 0:L]).then_inc(misc_used, 1)
                state["misc"] += 1
                dve.wait_ge(misc_ready, state["misc"])
                p3 = pc.rearrange("p a (h n) -> p a h n", n=32)
                for tt in range(2):
                    add = cs("cmp_add", tt * 32, tt * 32 + NCMP).unsqueeze(1).unsqueeze(1).to_broadcast([P, 2, 4, NCMP])
                    for half in range(2):
                        link(dve.tensor_tensor(
                            p3[:, tt].rearrange("p (a b r) n -> p a b r n", a=2, b=2)[:, :, half, :, 0:NCMP],
                            acc[:, tt, :].rearrange("p (a r b n) -> p a r b n", a=2, r=4, b=2)[:, :, :, half, 0:NCMP],
                            add, ALU.add))
                    link(dve.tensor_reduce(st32[:, 0, tt * AH:(tt + 1) * AH], p3[:, tt, :, 0:NCMP], AX_X, ALU.max))
                    ins = dve.tensor_tensor(
                        p3[:, tt, :, 0:NCMP], p3[:, tt, :, 0:NCMP],
                        st32[:, 0, tt * AH:(tt + 1) * AH].unsqueeze(2).to_broadcast([P, AH, NCMP]), ALU.subtract)
                    if tt == 0:
                        link(ins)
                ins.then_inc(aux_v, 1)
                state["aux_s"] += 1
                dve.wait_ge(aux_s, state["aux_s"])
                for tt in range(2):
                    one = cs("cmp_one", tt * 32, tt * 32 + 32).unsqueeze(1).to_broadcast([P, AH, 32])
                    link(dve.tensor_tensor(p3[:, tt], p3[:, tt], one, ALU.mult))
                    link(dve.tensor_reduce(st32[:, 0, tt * AH:(tt + 1) * AH], p3[:, tt], AX_X, ALU.add))
                link(dve.tensor_scalar(st32[:, 0, :], st32[:, 0, :], 1e-30, None, ALU.max))
                link(dve.reciprocal(st32[:, 0, :], st32[:, 0, :]))
                g3 = gates.rearrange("p a (h b) -> p a h b", b=NB)[:, :, :, 0]
                link(dve.tensor_tensor(st32[:, 0, :].rearrange("p (a h) -> p a h", a=2),
                                       st32[:, 0, :].rearrange("p (a h) -> p a h", a=2), g3, ALU.mult))
                for tt in range(2):
                    ins = dve.tensor_tensor(
                        p3[:, tt], p3[:, tt],
                        st32[:, 0, tt * AH:(tt + 1) * AH].unsqueeze(2).to_broadcast([P, AH, 32]), ALU.mult)
                ins.then_inc(misc_used, 1)
                state["misc"] += 1
                dve.wait_ge(misc_ready, state["misc"])
                dve.tensor_copy(PC.rearrange("p g t -> p (g t)"),
                                up[:, :, :].rearrange("p a t -> p (a t)")).then_inc(misc_used, 1)
                attention(units_nsa(), UNITS["nsa"])
                update_slots(n0 + 14, 2, "plain")

            dve.memset(ones[:, :], 1.0).then_inc(setup_done, 1)
            dve.memset(eps[:, :], EPS).then_inc(setup_done, 1)
            dve.memset(zeros[:, :], 0.0).then_inc(setup_done, 1)
            dve.wait_ge(cact_ready, 1)
            for i in range(GATE_SLOT):
                dve.wait_ge(mod_landed[i % MRING], 16 * (i // MRING + 1))
                for e in range(2):
                    w = mring[:, i % MRING, e, :]
                    ins = dve.scalar_tensor_tensor(out=w, in0=w, scalar=1.0, in1=cact[:, :], op0=ALU.mult, op1=ALU.mult,
                                                   accum_out=modraw[:, 2 * i + e:2 * i + e + 1])
                ins.then_inc(mod_used, 1)
            dve.wait_ge(mod_used, GATE_SLOT)
            dve.wait_ge(vec_landed, 16)
            dve.wait_ge(con_landed, 16)
            norm(0, 0.5, parts=True)
            low(0, 0)
            low(0, 1)
            ffn(AT_SLOT["ffn0"])
            norm(1)
            ssm(AT_SLOT["ssm"])
            norm(2, 0.5, parts=True)
            ffn(AT_SLOT["ffn1"], then=AT_SLOT["ffn2"])
            norm(3, 0.5, parts=True)
            ffn(AT_SLOT["ffn2"])
            norm(4, parts=True, hi=H_hi_moba)
            moba(AT_SLOT["moba"])
            norm(5, 0.5, parts=True)
            ffn(AT_SLOT["ffn3"])
            norm()
            norm(own=True)
            conformer(AT_SLOT["conf"])
            norm(parts=True, gain="ffn_g")
            ffn(AT_SLOT["cffn0"], i=0)
            norm()
            nsa(AT_SLOT["nsa"])
            norm(parts=True, gain="ffn_g", col=KD)
            ffn(AT_SLOT["cffn1"], i=1)


XR = {"end": 10 * KD}
UNITS = {
    "moba": dict(u=0),
    "nsa": dict(u=AH),
    "misc_at_nsa": 3,
    "stat_at_conf": 9,
    "h_at_conf": 9 * KD + KI,
}


def kernel(x, c, norm_g, mod_w, mod_b, ffn_w_gate, ffn_w_up, ffn_w_down, ssm_w_in, ssm_conv_w, ssm_conv_b,
           ssm_dt_bias, ssm_a_log, ssm_d, ssm_norm_w, ssm_w_out, attn_w_qkv, attn_w_out, final_norm_g,
           mix_norm_g_2, ffn_norm_g_2, conv_w_pw1_2, conv_b_pw1_2, conv_w_dw_2, conv_b_dw_2, conv_ln_g_2,
           conv_ln_b_2, conv_w_pw2_2, conv_b_pw2_2, nsa_w_in_2, nsa_q_norm_2, nsa_kc_norm_2, nsa_ks_norm_2,
           nsa_kw_norm_2, nsa_pe_k_2, nsa_pe_v_2, nsa_ck_w1_2, nsa_ck_w2_2, nsa_cv_w1_2, nsa_cv_w2_2,
           nsa_w_out_2, ffn_w_up_2, ffn_w_dw_2, ffn_b_dw_2, ffn_w_down_2):
    import concourse.bacc as bacc
    from concourse.bass_utils import run_bass_kernel_spmd

    A = np.asarray

    def cols(a):
        a = A(a).reshape(-1, A(a).shape[-1])
        return a.reshape(a.shape[0], -1, P).transpose(2, 0, 1).reshape(P, -1)

    def pad(a):
        out = np.zeros((P, 1), np.float32)
        out[:A(a).size, 0] = A(a).reshape(-1)
        return out

    def twice(a):
        return np.tile(A(a).reshape(-1), 2).reshape(P, 1)

    def pe_pairs(a):
        return A(a).reshape(16, 2, HD).transpose(1, 2, 0).reshape(P, 16)

    vecs = dict(norm_g=cols(norm_g), mod_b=cols(mod_b), conv_w=cols(A(ssm_conv_w)[0, :, 0]),
                conv_b=cols(ssm_conv_b), dt_bias=pad(ssm_dt_bias), a_log=pad(ssm_a_log),
                ssm_d=cols(np.repeat(A(ssm_d)[0], HD)[None]), ssm_norm=cols(ssm_norm_w),
                final_g=cols(A(final_norm_g)[None]), mix_g=cols(mix_norm_g_2), ffn_g=cols(ffn_norm_g_2),
                b_pw1=cols(conv_b_pw1_2), w_dw=cols(A(conv_w_dw_2)[0]), b_dw=cols(conv_b_dw_2),
                ln_g=cols(conv_ln_g_2), ln_b=cols(conv_ln_b_2), b_pw2=cols(conv_b_pw2_2),
                q_norm=twice(nsa_q_norm_2), kc_norm=twice(nsa_kc_norm_2), ks_norm=twice(nsa_ks_norm_2),
                kw_norm=twice(nsa_kw_norm_2), pe_k=pe_pairs(A(nsa_pe_k_2)[0]), pe_v=pe_pairs(A(nsa_pe_v_2)[0]),
                ffn_dw=cols(ffn_w_dw_2), ffn_db=cols(ffn_b_dw_2))
    vec = np.concatenate([vecs[k] for k in VEC], 1)

    def ktiles(w):
        w = A(w)
        return w.reshape(w.shape[0] // P, P, w.shape[1]).transpose(1, 0, 2)

    w_in = ktiles(ssm_w_in[0])
    nsa_in = ktiles(nsa_w_in_2[0])
    at = np.cumsum([0, 1024] + [256] * 6 + [48])
    small = np.concatenate([w_in[:, :, INNER + 4096:].reshape(P, -1), nsa_in[:, :, at[7]:].reshape(P, -1),
                            ktiles(nsa_ck_w2_2[0]).reshape(P, -1), ktiles(nsa_cv_w2_2[0]).reshape(P, -1)], 1)

    def wide(w, width=L):
        return [w[:, :, j:j + width].reshape(P, -1) for j in range(0, w.shape[2], width)]

    def both(a, b):
        return [np.concatenate([a[:, :, j:j + P], b[:, :, j:j + P]], 2).reshape(P, -1)
                for j in range(0, a.shape[2], P)]

    def feed_forward(a, b, down):
        ups = both(a, b)
        d = ktiles(down)
        downs = [d[:, 2 * p:2 * p + 2, :].reshape(P, -1) for p in range(PAIRS)]
        out = ups[0:2]
        for p in range(1, PAIRS):
            out += [ups[2 * p], ups[2 * p + 1], downs[p - 1]]
        return out + [downs[-1]]

    def swiglu(i, j):
        return feed_forward(ktiles(ffn_w_gate[i, j]), ktiles(ffn_w_up[i, j]), ffn_w_down[i, j])

    def conv_ffn(i):
        w = ktiles(ffn_w_up_2[i])
        return feed_forward(w[:, :, :FF], w[:, :, FF:], ffn_w_down_2[i])

    heads = [(j // 4 * 2 + half) * 4 + j % 4 for j in range(KD) for half in (0, 1)]
    q_cols = np.concatenate([np.arange(h * HD, (h + 1) * HD) for h in heads])
    pw1 = ktiles(conv_w_pw1_2[0])
    stream = {
        "ffn0": swiglu(0, 0),
        "ssm": wide(w_in[:, :, INNER:INNER + 4096]) + wide(w_in[:, :, :INNER]) + wide(ktiles(ssm_w_out[0]), P),
        "ffn1": swiglu(0, 1),
        "ffn2": swiglu(1, 0),
        "moba": wide(ktiles(attn_w_qkv[0])) + wide(ktiles(attn_w_out[0])),
        "ffn3": swiglu(1, 1),
        "conf": both(pw1[:, :, :D], pw1[:, :, D:]) + wide(ktiles(conv_w_pw2_2[0])),
        "cffn0": conv_ffn(0),
        "nsa": wide(nsa_in[:, :, q_cols]) + [nsa_in[:, :, at[i]:at[i + 1]].reshape(P, -1) for i in (3, 5, 1, 2, 4, 6)]
        + wide(ktiles(nsa_ck_w1_2[0]), P) + wide(ktiles(nsa_cv_w1_2[0]), P) + wide(ktiles(A(nsa_w_out_2[0])[q_cols])),
        "cffn1": conv_ffn(1),
    }
    weights = np.stack([s for name, _ in LAYERS for s in stream[name]])
    mods = A(mod_w).reshape(NMOD, D, MSLOTS, 2, P).transpose(0, 2, 4, 3, 1).reshape(NMOD * MSLOTS, P, 2, D)
    arrays = {"in_x": cols(A(x)[0]).reshape(P, L, KD).transpose(0, 2, 1),
              "in_c": np.broadcast_to(A(c).reshape(1, D), (P, D)), "in_vectors": vec, "in_small": small, "in_constants": constants(),
              "in_mods": mods, "in_weights": weights}
    arrays = {k: np.ascontiguousarray(v) for k, v in arrays.items()}

    nc = bacc.Bacc("TRN2", target_bir_lowering=False, num_devices=1)
    args = [nc.dram_tensor(n, a.shape, F32, kind="ExternalInput").ap() for n, a in arrays.items()]
    out = nc.dram_tensor("out", (P, KD, L), F32, kind="ExternalOutput").ap()
    build(nc, *args, out)
    r = run_bass_kernel_spmd(nc, [arrays], core_ids=[0])
    y = r.results[0]["out"]
    return y.transpose(2, 1, 0).reshape(1, L, D)
```
